# Optimizing a Trainium2 kernel written in Bass

```python
import math
import jax, jax.numpy as jnp
from jax import lax
import numpy as np

D_MODEL = 1024
BATCH = 1
SEQ = 512
DEPTH = 1

GRID_W = 64
CTX_LEN = 256
EPS = 1e-6
N_MOD = 6
SSD_EXPAND = 2
D_SSD = SSD_EXPAND * D_MODEL
SSD_HEADDIM = 64
SSD_HEADS = D_SSD // SSD_HEADDIM
SSD_GROUPS = 4
SSD_HPG = SSD_HEADS // SSD_GROUPS
SSD_STATE = 128
SSD_CONV = 3
SSD_CHUNK = 128
D_BC = SSD_GROUPS * SSD_STATE
D_XBC = D_SSD + 2 * D_BC
DT_MIN = 1e-3
DT_MAX = 1e-1
ATT_HEADS = 16
ATT_KV_HEADS = 4
ATT_GROUP = ATT_HEADS // ATT_KV_HEADS
ATT_HEADDIM = 64
WINDOW = 128
ATT_BLOCK = 128
D_Q = ATT_HEADS * ATT_HEADDIM
D_KV = ATT_KV_HEADS * ATT_HEADDIM
ROPE_BASE = 10000.0
D_FF = 2816
FFN_CONV = 3
N_BRANCH = 2
Z0 = 0
XBC0 = Z0 + D_SSD
DT0 = XBC0 + D_XBC
Q0 = DT0 + 2 * SSD_HEADS
K0 = Q0 + D_Q
V0 = K0 + D_KV
G0 = V0 + D_KV
D_IN = G0 + N_BRANCH * D_MODEL


def rmsnorm(x, g):
    x32 = x.astype(jnp.float32)
    y = x32 * lax.rsqrt(jnp.mean(x32 * x32, axis=-1, keepdims=True) + EPS)
    return (y * g.astype(jnp.float32)).astype(x.dtype)

def modulate(x, g, shift, scale):
    return rmsnorm(x, g) * (1 + scale) + shift

def dwconv_centred(x, w, b):
    K, C = w.shape
    y = lax.conv_general_dilated(x, w[:, None, :].astype(x.dtype), window_strides=(1,),
                                 padding=[(K // 2, K // 2)],
                                 dimension_numbers=('NWC', 'WIO', 'NWC'),
                                 feature_group_count=C)
    return y + b.astype(x.dtype)

def segsum(a):
    T = a.shape[-1]
    cs = jnp.cumsum(a, axis=-1)
    diff = cs[..., :, None] - cs[..., None, :]
    return jnp.where(jnp.tril(jnp.ones((T, T), dtype=bool)), diff, -jnp.inf)

def ssd_scan(xs, la, bm, cm, h0, with_output):
    f32 = jnp.float32
    Bsz, L, G, R, P = xs.shape
    N = bm.shape[-1]
    T = SSD_CHUNK
    nc = L // T
    xc = xs.astype(f32).reshape(Bsz, nc, T, G, R, P)
    bc = bm.astype(f32).reshape(Bsz, nc, T, G, N)
    cc = cm.astype(f32).reshape(Bsz, nc, T, G, N)
    ac = la.astype(f32).reshape(Bsz, nc, T, G, R).transpose(0, 3, 4, 1, 2)
    cs = jnp.cumsum(ac, axis=-1)
    decay_to_end = jnp.exp(cs[..., -1:] - cs)
    states = jnp.einsum('bcsgn,bgrcs,bcsgrp->bcgrpn', bc, decay_to_end, xc)
    if h0 is None:
        h0 = jnp.zeros((Bsz, G, R, P, N), f32)
    states = jnp.concatenate([h0[:, None].astype(f32), states], axis=1)
    chunk_decay = jnp.exp(segsum(jnp.pad(cs[..., -1], ((0, 0), (0, 0), (0, 0), (1, 0)))))
    states = jnp.einsum('bgrzc,bcgrpn->bzgrpn', chunk_decay, states)
    final = states[:, -1]
    if not with_output:
        return None, final
    cb = jnp.einsum('bclgn,bcsgn->bgcls', cc, bc)
    scores = cb[:, :, None] * jnp.exp(segsum(ac))
    y_diag = jnp.einsum('bgrcls,bcsgrp->bclgrp', scores, xc)
    y_off = jnp.einsum('bclgn,bcgrpn,bgrcl->bclgrp', cc, states[:, :-1], jnp.exp(cs))
    return (y_diag + y_off).reshape(Bsz, L, G, R, P).astype(xs.dtype), final

def ssd_prepare(xbc_raw, dt_raw, conv_w, conv_b, dt_bias, a_log):
    xbc = jax.nn.silu(dwconv_centred(xbc_raw, conv_w, conv_b))
    Bsz, L, _ = xbc.shape
    xs = xbc[..., :D_SSD].reshape(Bsz, L, SSD_GROUPS, SSD_HPG, SSD_HEADDIM)
    bm = xbc[..., D_SSD:D_SSD + D_BC].reshape(Bsz, L, SSD_GROUPS, SSD_STATE)
    cm = xbc[..., D_SSD + D_BC:].reshape(Bsz, L, SSD_GROUPS, SSD_STATE)
    dt = jax.nn.softplus(dt_raw.astype(jnp.float32).reshape(Bsz, L, 2, SSD_HEADS)
                         + dt_bias.astype(jnp.float32))
    la = dt * (-jnp.exp(a_log.astype(jnp.float32)))
    dt = dt.reshape(Bsz, L, 2, SSD_GROUPS, SSD_HPG)
    la = la.reshape(Bsz, L, 2, SSD_GROUPS, SSD_HPG)
    return xs, bm, cm, dt, la

def ssd_bidir(xs, bm, cm, dt, la, h0f, h0b, with_output):
    xf = xs * dt[:, :, 0, :, :, None].astype(xs.dtype)
    xb = xs * dt[:, :, 1, :, :, None].astype(xs.dtype)
    yf, hf = ssd_scan(xf, la[:, :, 0], bm, cm, h0f, with_output)
    yb, hb = ssd_scan(jnp.flip(xb, axis=1), jnp.flip(la[:, :, 1], axis=1), jnp.flip(bm, axis=1),
                      jnp.flip(cm, axis=1), h0b, with_output)
    y = yf + jnp.flip(yb, axis=1) if with_output else None
    return y, hf, hb

def ssd_output(y, xs, z, d_skip, g):
    Bsz, L = y.shape[:2]
    y = y + d_skip.reshape(SSD_GROUPS, SSD_HPG, 1).astype(y.dtype) * xs
    return rmsnorm(y.reshape(Bsz, L, D_SSD) * jax.nn.silu(z), g)

def axial_rope(t, row, col):
    half = ATT_HEADDIM // 2
    inv = ROPE_BASE ** (-jnp.arange(0, half, 2, dtype=jnp.float32) / half)

    def rot(u, pos):
        ang = pos.astype(jnp.float32)[:, None] * inv[None]
        cos = jnp.cos(ang)[None, :, None, :].astype(u.dtype)
        sin = jnp.sin(ang)[None, :, None, :].astype(u.dtype)
        u1, u2 = u[..., :half // 2], u[..., half // 2:]
        return jnp.concatenate([u1 * cos - u2 * sin, u2 * cos + u1 * sin], axis=-1)

    return jnp.concatenate([rot(t[..., :half], row), rot(t[..., half:], col)], axis=-1)

def window_ctx_attention(q, k, v, kc, vc, sink):
    Bsz, L, H, Dh = q.shape
    nb = L // ATT_BLOCK
    scale = Dh ** -0.5
    qb = q.reshape(Bsz, nb, ATT_BLOCK, ATT_KV_HEADS, ATT_GROUP, Dh)

    def band(t):
        tb = t.reshape(Bsz, nb, ATT_BLOCK, ATT_KV_HEADS, Dh)
        tp = jnp.pad(tb, ((0, 0), (1, 1), (0, 0), (0, 0), (0, 0)))
        return jnp.concatenate([tp[:, :-2], tp[:, 1:-1], tp[:, 2:]], axis=2)

    kb, vb = band(k), band(v)
    s_win = jnp.einsum('bnqkgd,bnjkd->bnkgqj', qb, kb) * scale
    s_ctx = jnp.einsum('bnqkgd,bckd->bnkgqc', qb, kc) * scale
    qpos = jnp.arange(nb)[:, None] * ATT_BLOCK + jnp.arange(ATT_BLOCK)[None]
    kpos = (jnp.arange(nb)[:, None] - 1) * ATT_BLOCK + jnp.arange(3 * ATT_BLOCK)[None]
    valid = ((jnp.abs(qpos[:, :, None] - kpos[:, None, :]) <= WINDOW)
             & (kpos >= 0)[:, None, :] & (kpos < L)[:, None, :])
    s_win = jnp.where(valid[None, :, None, None], s_win, -jnp.inf)
    s_sink = jnp.broadcast_to(sink.reshape(1, 1, ATT_KV_HEADS, ATT_GROUP, 1, 1).astype(s_win.dtype),
                              s_win.shape[:-1] + (1,))
    logits = jnp.concatenate([s_win, s_ctx, s_sink], axis=-1).astype(jnp.float32)
    p = jax.nn.softmax(logits, axis=-1).astype(v.dtype)
    nw = 3 * ATT_BLOCK
    Lc = kc.shape[1]
    o = (jnp.einsum('bnkgqj,bnjkd->bnqkgd', p[..., :nw], vb)
         + jnp.einsum('bnkgqc,bckd->bnqkgd', p[..., nw:nw + Lc], vc))
    return o.reshape(Bsz, L, H * Dh)

def ctx_self_attention(q, k, v, sink):
    Bsz, Lc, H, Dh = q.shape
    qg = q.reshape(Bsz, Lc, ATT_KV_HEADS, ATT_GROUP, Dh)
    s = jnp.einsum('bqkgd,bckd->bkgqc', qg, k) * (Dh ** -0.5)
    s_sink = jnp.broadcast_to(sink.reshape(1, ATT_KV_HEADS, ATT_GROUP, 1, 1).astype(s.dtype),
                              s.shape[:-1] + (1,))
    p = jax.nn.softmax(jnp.concatenate([s, s_sink], axis=-1).astype(jnp.float32), axis=-1)
    o = jnp.einsum('bkgqc,bckd->bqkgd', p[..., :Lc].astype(v.dtype), v)
    return o.reshape(Bsz, Lc, H * Dh)

def merge_branches(p, y_ssd, y_att, w_o_ssd, w_o_att, w_out):
    gates = jax.nn.sigmoid(p[..., G0:D_IN])
    g_ssd, g_att = gates[..., :D_MODEL], gates[..., D_MODEL:]
    return (g_ssd * (y_ssd @ w_o_ssd) + g_att * (y_att @ w_o_att)) @ w_out

def token_mixer(h_lat, h_ctx, row, col, w_in, conv_w, conv_b, dt_bias, a_log, d_skip, ssd_g,
                w_o_ssd, w_o_att, sink, w_out, with_ctx_out):
    Bsz, L, _ = h_lat.shape
    Lc = h_ctx.shape[1]
    p_lat = h_lat @ w_in
    p_ctx = h_ctx @ w_in
    xs_c, bm_c, cm_c, dt_c, la_c = ssd_prepare(p_ctx[..., XBC0:DT0], p_ctx[..., DT0:Q0],
                                               conv_w, conv_b, dt_bias, a_log)
    y_c, hf_c, hb_c = ssd_bidir(xs_c, bm_c, cm_c, dt_c, la_c, None, None, with_ctx_out)
    xs_l, bm_l, cm_l, dt_l, la_l = ssd_prepare(p_lat[..., XBC0:DT0], p_lat[..., DT0:Q0],
                                               conv_w, conv_b, dt_bias, a_log)
    y_l, _, _ = ssd_bidir(xs_l, bm_l, cm_l, dt_l, la_l, hf_c, hb_c, True)
    ssd_lat = ssd_output(y_l, xs_l, p_lat[..., Z0:XBC0], d_skip, ssd_g)
    q_l = axial_rope(p_lat[..., Q0:K0].reshape(Bsz, L, ATT_HEADS, ATT_HEADDIM), row, col)
    k_l = axial_rope(p_lat[..., K0:V0].reshape(Bsz, L, ATT_KV_HEADS, ATT_HEADDIM), row, col)
    v_l = p_lat[..., V0:G0].reshape(Bsz, L, ATT_KV_HEADS, ATT_HEADDIM)
    k_c = p_ctx[..., K0:V0].reshape(Bsz, Lc, ATT_KV_HEADS, ATT_HEADDIM)
    v_c = p_ctx[..., V0:G0].reshape(Bsz, Lc, ATT_KV_HEADS, ATT_HEADDIM)
    att_lat = window_ctx_attention(q_l, k_l, v_l, k_c, v_c, sink)
    out_lat = merge_branches(p_lat, ssd_lat, att_lat, w_o_ssd, w_o_att, w_out)
    if not with_ctx_out:
        return out_lat, None
    ssd_ctx = ssd_output(y_c, xs_c, p_ctx[..., Z0:XBC0], d_skip, ssd_g)
    q_c = p_ctx[..., Q0:K0].reshape(Bsz, Lc, ATT_HEADS, ATT_HEADDIM)
    att_ctx = ctx_self_attention(q_c, k_c, v_c, sink)
    out_ctx = merge_branches(p_ctx, ssd_ctx, att_ctx, w_o_ssd, w_o_att, w_out)
    return out_lat, out_ctx

def conv_ffn(h, w_up, conv_w, conv_b, w_down):
    u = dwconv_centred(h @ w_up, conv_w, conv_b)
    a, b = u[..., :D_FF], u[..., D_FF:]
    return (jax.nn.silu(a) * b) @ w_down

def first_inputs(seed: int = 0) -> dict:
    key = jax.random.key(seed)
    ks = jax.random.split(key, 24)
    f32 = jnp.float32

    def nrm(k, shape, scale):
        return jax.random.normal(k, shape, f32) * scale

    dt0 = jnp.exp(jax.random.uniform(ks[10], (DEPTH, 2, SSD_HEADS), f32,
                                     math.log(DT_MIN), math.log(DT_MAX)))
    return {
        'x': nrm(ks[0], (BATCH, SEQ, D_MODEL), 1.0),
        'c': nrm(ks[1], (BATCH, D_MODEL), 1.0),
        'ctx': nrm(ks[2], (BATCH, CTX_LEN, D_MODEL), 1.0),
        'c_ctx': nrm(ks[3], (D_MODEL,), 1.0),
        'w_mod': nrm(ks[4], (DEPTH, D_MODEL, N_MOD * D_MODEL), 0.5 * D_MODEL ** -0.5),
        'b_mod': nrm(ks[5], (DEPTH, N_MOD * D_MODEL), 0.01),
        'norm1_g': 1.0 + nrm(ks[6], (DEPTH, D_MODEL), 0.05),
        'norm2_g': 1.0 + nrm(ks[7], (DEPTH, D_MODEL), 0.05),
        'w_in': nrm(ks[8], (DEPTH, D_MODEL, D_IN), D_MODEL ** -0.5),
        'ssd_conv_w': nrm(ks[9], (DEPTH, SSD_CONV, D_XBC), SSD_CONV ** -0.5),
        'ssd_conv_b': nrm(ks[11], (DEPTH, D_XBC), 0.01),
        'ssd_dt_bias': dt0 + jnp.log(-jnp.expm1(-dt0)),
        'ssd_a_log': jnp.log(jax.random.uniform(ks[12], (DEPTH, 2, SSD_HEADS), f32, 1.0, 16.0)),
        'ssd_d': 1.0 + nrm(ks[13], (DEPTH, SSD_HEADS), 0.1),
        'ssd_norm_g': 1.0 + nrm(ks[14], (DEPTH, D_SSD), 0.05),
        'w_o_ssd': nrm(ks[15], (DEPTH, D_SSD, D_MODEL), D_SSD ** -0.5),
        'w_o_att': nrm(ks[16], (DEPTH, D_Q, D_MODEL), D_Q ** -0.5),
        'att_sink': nrm(ks[17], (DEPTH, ATT_HEADS), 0.5),
        'w_out': nrm(ks[18], (DEPTH, D_MODEL, D_MODEL), D_MODEL ** -0.5),
        'w_up': nrm(ks[19], (DEPTH, D_MODEL, 2 * D_FF), D_MODEL ** -0.5),
        'ffn_conv_w': nrm(ks[20], (DEPTH, FFN_CONV, 2 * D_FF), FFN_CONV ** -0.5),
        'ffn_conv_b': nrm(ks[21], (DEPTH, 2 * D_FF), 0.01),
        'w_down': nrm(ks[22], (DEPTH, D_FF, D_MODEL), D_FF ** -0.5),
        'final_g': 1.0 + nrm(ks[23], (D_MODEL,), 0.05),
    }

def first_block(x, c, ctx, c_ctx, w_mod, b_mod, norm1_g, norm2_g, w_in, ssd_conv_w, ssd_conv_b,
              ssd_dt_bias, ssd_a_log, ssd_d, ssd_norm_g, w_o_ssd, w_o_att, att_sink, w_out,
              w_up, ffn_conv_w, ffn_conv_b, w_down, final_g):
    L = x.shape[1]
    ROWS = L // GRID_W
    row = jnp.broadcast_to(jnp.arange(ROWS)[:, None], (ROWS, GRID_W)).reshape(-1)
    col = jnp.broadcast_to(jnp.arange(GRID_W)[None, :], (ROWS, GRID_W)).reshape(-1)
    for l in range(DEPTH):
        last = l == DEPTH - 1
        mod = jax.nn.silu(c) @ w_mod[l] + b_mod[l]
        sh1, sc1, gt1, sh2, sc2, gt2 = jnp.split(mod[:, None, :], N_MOD, axis=-1)
        mod_c = jax.nn.silu(c_ctx) @ w_mod[l] + b_mod[l]
        csh1, csc1, cgt1, csh2, csc2, cgt2 = jnp.split(mod_c, N_MOD, axis=-1)
        h_lat = modulate(x, norm1_g[l], sh1, sc1)
        h_ctx = modulate(ctx, norm1_g[l], csh1, csc1)
        o_lat, o_ctx = token_mixer(h_lat, h_ctx, row, col, w_in[l], ssd_conv_w[l], ssd_conv_b[l],
                                   ssd_dt_bias[l], ssd_a_log[l], ssd_d[l], ssd_norm_g[l],
                                   w_o_ssd[l], w_o_att[l], att_sink[l], w_out[l], not last)
        x = x + gt1 * o_lat
        x = x + gt2 * conv_ffn(modulate(x, norm2_g[l], sh2, sc2), w_up[l], ffn_conv_w[l],
                               ffn_conv_b[l], w_down[l])
        if not last:
            ctx = ctx + cgt1 * o_ctx
            ctx = ctx + cgt2 * conv_ffn(modulate(ctx, norm2_g[l], csh2, csc2), w_up[l],
                                        ffn_conv_w[l], ffn_conv_b[l], w_down[l])
    return rmsnorm(x, final_g)


CHUNK = 64
MEM_LEN = 256
NEG = -1e30

FOX_HEAD_DIM = 64
D_FOX = 3 * D_MODEL // 4
FOX_HEADS = D_FOX // FOX_HEAD_DIM
Q_BLOCK = 128

D_S5 = 3 * D_MODEL // 4
S5_GROUP = 16
S5_GROUPS = D_S5 // S5_GROUP
S5_STATE = 64

D_MEM = D_MODEL // 2
MEM_HEADS = 4
MEM_HEAD_DIM = D_MEM // MEM_HEADS

N_BRANCH_2 = 3
IN_SIZES = (D_FOX, D_FOX, D_FOX, FOX_HEADS, D_FOX,
            D_S5, D_S5,
            D_MEM, D_MEM,
            N_BRANCH_2 * D_MODEL)
N_IN = sum(IN_SIZES)


def rms_norm(x, g):
    xf = x.astype(jnp.float32)
    y = xf * lax.rsqrt(jnp.mean(xf * xf, axis=-1, keepdims=True) + EPS)
    return (y * g.astype(jnp.float32)).astype(x.dtype)

def split_cols(z):
    offs = np.cumsum(np.array(IN_SIZES))[:-1].tolist()
    return jnp.split(z, offs, axis=-1)

def forgetting_attention(q, k, v, log_f):
    Bn, L, H, Dh = q.shape
    nb = L // Q_BLOCK
    F = jnp.cumsum(log_f, axis=1).transpose(0, 2, 1)
    kh = k.astype(jnp.float32).transpose(0, 2, 1, 3)
    vh = v.astype(jnp.float32).transpose(0, 2, 1, 3)
    qb = (q.astype(jnp.float32) * (Dh ** -0.5)).reshape(Bn, nb, Q_BLOCK, H, Dh).transpose(1, 0, 3, 2, 4)
    Fq = F.reshape(Bn, H, nb, Q_BLOCK).transpose(2, 0, 1, 3)
    starts = jnp.arange(nb, dtype=jnp.int32) * Q_BLOCK
    key_pos = jnp.arange(L, dtype=jnp.int32)

    def block(args):
        qi, Fi, s0 = args
        s = jnp.einsum('bhqd,bhkd->bhqk', qi, kh)
        s = s + Fi[..., None] - F[:, :, None, :]
        qpos = s0 + jnp.arange(Q_BLOCK, dtype=jnp.int32)
        s = jnp.where(key_pos[None, :] <= qpos[:, None], s, NEG)
        p = jax.nn.softmax(s, axis=-1)
        return jnp.einsum('bhqk,bhkd->bhqd', p, vh)

    out = lax.map(block, (qb, Fq, starts))
    return out.transpose(1, 0, 3, 2, 4).reshape(Bn, L, H * Dh).astype(q.dtype)

def s5_ssm(u, lam_re, lam_im, log_step, b_re, b_im, c_re, c_im, d_skip):
    Bn, L, _ = u.shape
    f32 = jnp.float32
    uf = u.astype(f32).reshape(Bn, L, S5_GROUPS, S5_GROUP)
    step = jnp.exp(log_step.astype(f32))[:, None]
    lr, li = lam_re.astype(f32), lam_im.astype(f32)
    mag = jnp.exp(lr * step)
    ab_re, ab_im = mag * jnp.cos(li * step), mag * jnp.sin(li * step)
    den = lr * lr + li * li
    nr, ni = ab_re - 1.0, ab_im
    f_re = (nr * lr + ni * li) / den
    f_im = (ni * lr - nr * li) / den
    br, bi = b_re.astype(f32), b_im.astype(f32)
    bb_re = f_re[..., None] * br - f_im[..., None] * bi
    bb_im = f_re[..., None] * bi + f_im[..., None] * br
    x_re = jnp.einsum('gph,blgh->blgp', bb_re, uf)
    x_im = jnp.einsum('gph,blgh->blgp', bb_im, uf)
    a_re = jnp.broadcast_to(ab_re[None, None], (1, L, S5_GROUPS, S5_STATE))
    a_im = jnp.broadcast_to(ab_im[None, None], (1, L, S5_GROUPS, S5_STATE))

    def combine(e1, e2):
        a1r, a1i, b1r, b1i = e1
        a2r, a2i, b2r, b2i = e2
        return (a2r * a1r - a2i * a1i,
                a2r * a1i + a2i * a1r,
                a2r * b1r - a2i * b1i + b2r,
                a2r * b1i + a2i * b1r + b2i)

    _, _, h_re, h_im = lax.associative_scan(combine, (a_re, a_im, x_re, x_im), axis=1)
    y = (jnp.einsum('ghp,blgp->blgh', c_re.astype(f32), h_re)
         - jnp.einsum('ghp,blgp->blgh', c_im.astype(f32), h_im))
    y = y + d_skip.astype(f32).reshape(S5_GROUPS, S5_GROUP) * uf
    return y.reshape(Bn, L, D_S5).astype(u.dtype)

def memory_attention(q, mk, mv):
    Bn, L = q.shape[:2]
    s = jnp.einsum('blhd,bmhd->bhlm', q.astype(jnp.float32), mk.astype(jnp.float32)) * (MEM_HEAD_DIM ** -0.5)
    p = jax.nn.softmax(s, axis=-1)
    o = jnp.einsum('bhlm,bmhd->blhd', p, mv.astype(jnp.float32))
    return o.reshape(Bn, L, D_MEM).astype(q.dtype)

def second_inputs(seed: int = 0) -> dict:
    key = jax.random.key(seed)
    ks = jax.random.split(key, 24)
    f32 = jnp.float32
    nrm = lambda k, shape, scale: jax.random.normal(k, shape, f32) * scale
    x = nrm(ks[0], (BATCH, SEQ, D_MODEL), 1.0)
    mem = nrm(ks[1], (BATCH, MEM_LEN, D_MODEL), 1.0)
    g_norm = 1.0 + nrm(ks[2], (DEPTH, D_MODEL), 0.02)
    g_mem_norm = 1.0 + nrm(ks[3], (DEPTH, D_MODEL), 0.02)
    g_final = 1.0 + nrm(ks[4], (D_MODEL,), 0.02)
    w_in = nrm(ks[5], (DEPTH, D_MODEL, N_IN), D_MODEL ** -0.5)
    b_forget = jax.random.uniform(ks[6], (DEPTH, FOX_HEADS), f32, 1.0, 4.0)
    b_merge = nrm(ks[7], (DEPTH, N_BRANCH_2 * D_MODEL), 0.01)
    w_mem_kv = nrm(ks[8], (DEPTH, D_MODEL, 2 * D_MEM), D_MODEL ** -0.5)
    lam_re = -0.5 + nrm(ks[9], (DEPTH, S5_GROUPS, S5_STATE), 0.01)
    lam_im = (math.pi * jnp.arange(S5_STATE, dtype=f32))[None, None, :] + nrm(ks[10], (DEPTH, S5_GROUPS, S5_STATE), 0.01)
    log_step = jax.random.uniform(ks[11], (DEPTH, S5_GROUPS), f32, math.log(1e-3), math.log(1e-1))
    s5_b_re = nrm(ks[12], (DEPTH, S5_GROUPS, S5_STATE, S5_GROUP), (2 * S5_GROUP) ** -0.5)
    s5_b_im = nrm(ks[13], (DEPTH, S5_GROUPS, S5_STATE, S5_GROUP), (2 * S5_GROUP) ** -0.5)
    s5_c_re = nrm(ks[14], (DEPTH, S5_GROUPS, S5_GROUP, S5_STATE), (2 * S5_STATE) ** -0.5)
    s5_c_im = nrm(ks[15], (DEPTH, S5_GROUPS, S5_GROUP, S5_STATE), (2 * S5_STATE) ** -0.5)
    s5_d = nrm(ks[16], (DEPTH, D_S5), 1.0)
    w_glu = nrm(ks[17], (DEPTH, D_S5, D_S5), D_S5 ** -0.5)
    b_glu = nrm(ks[18], (DEPTH, D_S5), 0.01)
    w_proj_fox = nrm(ks[19], (DEPTH, D_FOX, D_MODEL), D_FOX ** -0.5)
    w_proj_s5 = nrm(ks[20], (DEPTH, D_S5, D_MODEL), D_S5 ** -0.5)
    w_proj_mem = nrm(ks[21], (DEPTH, D_MEM, D_MODEL), D_MEM ** -0.5)
    w_out = nrm(ks[22], (DEPTH, D_MODEL, D_MODEL), D_MODEL ** -0.5)
    return {"x": x, "mem": mem, "g_norm": g_norm, "g_mem_norm": g_mem_norm, "g_final": g_final,
            "w_in": w_in, "b_forget": b_forget, "b_merge": b_merge, "w_mem_kv": w_mem_kv,
            "lam_re": lam_re, "lam_im": lam_im, "log_step": log_step,
            "s5_b_re": s5_b_re, "s5_b_im": s5_b_im, "s5_c_re": s5_c_re, "s5_c_im": s5_c_im,
            "s5_d": s5_d, "w_glu": w_glu, "b_glu": b_glu,
            "w_proj_fox": w_proj_fox, "w_proj_s5": w_proj_s5, "w_proj_mem": w_proj_mem, "w_out": w_out}

def second_block(x, mem, g_norm, g_mem_norm, g_final, w_in, b_forget, b_merge, w_mem_kv,
              lam_re, lam_im, log_step, s5_b_re, s5_b_im, s5_c_re, s5_c_im, s5_d,
              w_glu, b_glu, w_proj_fox, w_proj_s5, w_proj_mem, w_out):
    Bn, L, _ = x.shape
    M = mem.shape[1]
    for l in range(DEPTH):
        h = rms_norm(x, g_norm[l])
        z = h @ w_in[l]
        q, k, v, fl, gf, u, gs, qm, gm, gl = split_cols(z)

        log_f = jax.nn.log_sigmoid(fl.astype(jnp.float32) + b_forget[l].astype(jnp.float32))
        y_fox = forgetting_attention(q.reshape(Bn, L, FOX_HEADS, FOX_HEAD_DIM),
                                     k.reshape(Bn, L, FOX_HEADS, FOX_HEAD_DIM),
                                     v.reshape(Bn, L, FOX_HEADS, FOX_HEAD_DIM), log_f)
        y_fox = y_fox * jax.nn.silu(gf)

        y_s5 = s5_ssm(u, lam_re[l], lam_im[l], log_step[l], s5_b_re[l], s5_b_im[l],
                      s5_c_re[l], s5_c_im[l], s5_d[l])
        y_s5 = jax.nn.gelu(y_s5)
        y_s5 = y_s5 * jax.nn.sigmoid(y_s5 @ w_glu[l] + b_glu[l])
        y_s5 = y_s5 * jax.nn.silu(gs)

        kv = rms_norm(mem, g_mem_norm[l]) @ w_mem_kv[l]
        mk, mv = jnp.split(kv, 2, axis=-1)
        y_mem = memory_attention(qm.reshape(Bn, L, MEM_HEADS, MEM_HEAD_DIM),
                                 mk.reshape(Bn, M, MEM_HEADS, MEM_HEAD_DIM),
                                 mv.reshape(Bn, M, MEM_HEADS, MEM_HEAD_DIM))
        y_mem = y_mem * jax.nn.silu(gm)

        gates = jax.nn.sigmoid(gl + b_merge[l]).reshape(Bn, L, N_BRANCH_2, D_MODEL)
        merged = (gates[:, :, 0] * (y_fox @ w_proj_fox[l])
                  + gates[:, :, 1] * (y_s5 @ w_proj_s5[l])
                  + gates[:, :, 2] * (y_mem @ w_proj_mem[l]))
        x = x + merged @ w_out[l]
    return rms_norm(x, g_final)


def setup_inputs(seed=0):
    out = dict(first_inputs(seed))
    for name, value in second_inputs(seed + 1).items():
        if name != "x":
            out[name + "_2"] = value
    return out


def reference(
    x, c, ctx, c_ctx, w_mod, b_mod, norm1_g, norm2_g, w_in, ssd_conv_w, ssd_conv_b, ssd_dt_bias,
    ssd_a_log, ssd_d, ssd_norm_g, w_o_ssd, w_o_att, att_sink, w_out, w_up, ffn_conv_w,
    ffn_conv_b, w_down, final_g, mem_2, g_norm_2, g_mem_norm_2, g_final_2, w_in_2, b_forget_2,
    b_merge_2, w_mem_kv_2, lam_re_2, lam_im_2, log_step_2, s5_b_re_2, s5_b_im_2, s5_c_re_2,
    s5_c_im_2, s5_d_2, w_glu_2, b_glu_2, w_proj_fox_2, w_proj_s5_2, w_proj_mem_2, w_out_2,
):
    x = first_block(
        x, c, ctx, c_ctx, w_mod, b_mod, norm1_g, norm2_g, w_in, ssd_conv_w, ssd_conv_b,
        ssd_dt_bias, ssd_a_log, ssd_d, ssd_norm_g, w_o_ssd, w_o_att, att_sink, w_out, w_up,
        ffn_conv_w, ffn_conv_b, w_down, final_g,
    )
    return second_block(
        x, mem_2, g_norm_2, g_mem_norm_2, g_final_2, w_in_2, b_forget_2, b_merge_2, w_mem_kv_2,
        lam_re_2, lam_im_2, log_step_2, s5_b_re_2, s5_b_im_2, s5_c_re_2, s5_c_im_2, s5_d_2,
        w_glu_2, b_glu_2, w_proj_fox_2, w_proj_s5_2, w_proj_mem_2, w_out_2,
    )


_drawn_inputs = setup_inputs


def setup_inputs(seed=0):
    import zlib

    import numpy as np

    out = dict(_drawn_inputs(seed))
    spreads = {}
    factors = {'ctx': 3.76,
     'b_mod': 5.101,
     'norm1_g': 4.253,
     'norm2_g': 3.496,
     'ssd_conv_b': 8.0,
     'ssd_d': 51.156,
     'ssd_norm_g': 6.457,
     'att_sink': 8.0,
     'ffn_conv_b': 8.0,
     'g_norm_2': 8.0,
     'g_mem_norm_2': 8.0,
     'g_final_2': 8.349,
     'b_merge_2': 41.701,
     'lam_re_2': 64.0,
     'lam_im_2': 64.0,
     'log_step_2': 62.712,
     's5_b_re_2': 64.0,
     's5_b_im_2': 64.0,
     's5_c_re_2': 64.0,
     's5_c_im_2': 64.0,
     'b_glu_2': 64.0}
    for name, (base, spread) in spreads.items():
        noise = np.random.default_rng([zlib.crc32(name.encode()), seed]).standard_normal(out[name].shape)
        drawn = base * np.exp(spread * noise) if base else spread * noise
        out[name] = __import__('jax').numpy.asarray(drawn.astype(out[name].dtype))
    for name, factor in factors.items():
        out[name] = (out[name] * factor).astype(out[name].dtype)
    return out
```

```python
from contextlib import ExitStack

import numpy as np

import concourse.bass as bass
from concourse import mybir

ALU = mybir.AluOpType
ACT = mybir.ActivationFunctionType
F32 = mybir.dt.float32
BF16 = mybir.dt.bfloat16
AXX = mybir.AxisListType.X

P = 128
EPS = 1e-6
L = 512
LC = 256
LT = L + LC
NSLOT = 8

VECS = [("bmod", 48), ("g1", 8), ("g2", 8), ("cw0", 24), ("cw1", 24), ("cw2", 24), ("cb", 24),
        ("sg", 16), ("fw0", 44), ("fw1", 44), ("fw2", 44), ("fb", 44), ("fg", 8), ("gn", 8),
        ("gm", 8), ("gf", 8), ("bmerge", 24), ("bglu", 6), ("s5d", 6), ("lre", 24), ("lim", 24),
        ("lstep", 24), ("dsk", 16), ("c", 16)]
VOFF = {}
_o = 0
for _n, _k in VECS:
    VOFF[_n] = (_o, _k)
    _o += _k
NVEC = _o
ROWS = [("dtb", 64), ("alog", 64), ("sink", 16), ("bfor", 12)]
CONSTS = [("ident", 128), ("trif", 128), ("trib", 128), ("perm", 128), ("ml", 128), ("mr", 128),
          ("ones", 128), ("cos", 512), ("sin", 512)]


class Engine:

    def __init__(self, eng, sem):
        self.eng, self.sem, self.n, self.seen = eng, sem, 0, {}

    def wait(self, *toks):
        for t in toks:
            if t is None:
                continue
            if isinstance(t, (list, tuple)) and not (len(t) == 2 and isinstance(t[1], int)):
                self.wait(*t)
                continue
            s, v = t
            if self.seen.get(id(s), 0) < v:
                self.seen[id(s)] = v
                self.eng.wait_ge(s, v)

    def __call__(self, fn, *toks):
        self.wait(*toks)
        self.n += 1
        fn(self.eng).then_inc(self.sem, 1)
        return (self.sem, self.n)

    def quiet(self, fn, *toks):
        self.wait(*toks)
        fn(self.eng)

    def last(self):
        return (self.sem, self.n)


class Ring:

    def __init__(self, slots):
        self.slots, self.free, self.i = slots, [[] for _ in slots], 0

    def take(self):
        k = self.i % len(self.slots)
        self.i += 1
        return k, self.slots[k], self.free[k]

    def give(self, k, *toks):
        self.free[k] = list(toks)


def fused_blocks(nc, A, out):
    ctx = ExitStack()
    with ctx:
        def sb(name, shape, dt=F32, c=ctx):
            return c.enter_context(nc.sbuf_tensor(name, shape, dt))

        def sem(name):
            return ctx.enter_context(nc.semaphore(name))

        ps = ctx.enter_context(nc.psum_tensor("ps", [P, 8, 512], F32))

        def bank(b):
            return ps[:, b, :]

        pe = Engine(nc.tensor, sem("s_pe"))
        dve = Engine(nc.vector, sem("s_dve"))
        act = Engine(nc.scalar, sem("s_act"))
        pool = Engine(nc.gpsimd, sem("s_pool"))
        sp = Engine(nc.sync, sem("s_sp"))

        class Dma:

            def __init__(self, name):
                self.sem, self.n = sem(name), 0

            def start(self, eng, dst, src, *toks):
                eng.wait(*toks)
                self.n += 16
                eng.eng.dma_start(dst, src).then_inc(self.sem, 16)
                return (self.sem, self.n)

        def fence():
            marks = [e.last() for e in (pe, dve, act, pool)]
            for e in (pe, dve, act, pool):
                e.wait(marks)
            return marks

        wslots = sb("wslots", [P, NSLOT, 1024])
        wdma = [Dma(f"s_w{i}") for i in range(NSLOT)]
        wring = Ring([wslots[:, i, :] for i in range(NSLOT)])

        def wload(src, n):
            k, ap, free = wring.take()
            t = wdma[k].start(sp, ap[:, 0:n], src, free)
            return k, ap[:, 0:n], t

        G = Ring([0, 1])

        def gemm(wd, m, KT, rhs, ranges, acc_waits=()):
            slots = []
            for k0 in range(0, KT, 8):
                kk = min(8, KT - k0)
                slots.append(wload(wd[m, :, k0 * 128:(k0 + kk) * 128], kk * 128))
            res = []
            for (t0, t1) in ranges:
                gk, b, free = G.take()
                pe.wait(free, acc_waits)
                for k in range(KT):
                    wk, wap, wt = slots[k // 8]
                    pe.wait(wt)
                    f = lambda e, b=b, w=wap[:, (k % 8) * 128:(k % 8 + 1) * 128], r=rhs(k)[:, t0:t1], k=k: \
                        e.matmul(ps[:, b, 0:r.shape[1]], w, r, start=(k == 0), stop=(k == KT - 1))
                    if k == KT - 1:
                        tok = pe(f)
                    else:
                        pe.quiet(f)
                res.append((gk, ps[:, b, 0:t1 - t0], tok))
            for wk, _, _ in slots:
                wring.give(wk, tok)
            return res

        vc = sb("vc", [P, NVEC])
        rows = sb("rows", [P, 156])
        cst = sb("cst", [P, 896])
        maskb = sb("maskb", [P, 3, 128], BF16)
        dc = Dma("s_c")
        dx = Dma("s_x")
        t_vc = dc.start(sp, vc[:, :], A["vecs"])

        def V(name, i=0, n=None):
            o, k = VOFF[name]
            return vc[:, o + i:o + i + (n or 1)]

        def C(name):
            return cst[:, ["ident", "trif", "trib", "perm", "ml", "mr", "ones"].index(name) * 128:][:, 0:128]

        ident, ones = C("ident"), C("ones")

        cs_ = sb("cs_", [P, 16])
        tmp16 = sb("tmp16", [P, 16])
        modS = sb("modS", [P, 48, 2])
        A1 = sb("A1", [P, 8, 2])
        A2 = sb("A2", [P, 8])
        acc = sb("acc", [P, LT])
        rstd = sb("rstd", [P, LT])
        sq = sb("sq", [P, 2, LT])
        sqr = Ring([sq[:, 0, :], sq[:, 1, :]])

        def norm_T(X, KT, ranges, affine, in_toks=(), inv=None, split=True):
            T = max(r[1] for r in ranges)
            tacc = None
            for k in range(KT):
                i, s, free = sqr.take()
                ta = act(lambda e, s=s, k=k: e.activation(s[:, 0:T], X(k)[:, 0:T], ACT.Square), free, in_toks)
                if k == 0:
                    tacc = dve(lambda e, s=s: e.tensor_copy(acc[:, 0:T], s[:, 0:T]), ta)
                else:
                    tacc = dve(lambda e, s=s: e.tensor_tensor(acc[:, 0:T], acc[:, 0:T], s[:, 0:T], ALU.add), ta, tacc)
                sqr.give(i, tacc)
            return norm_rstd(ranges, tacc, inv or 1.0 / (KT * 128))

        def norm_rstd(ranges, tacc, inv):
            nrm = sq
            tr = []
            for (t0, t1) in ranges:
                gk, b, free = G.take()
                tm = pe(lambda e, b=b, t0=t0, t1=t1: e.matmul(ps[:, b, 0:t1 - t0], ones, acc[:, t0:t1], start=True, stop=True),
                        free, tacc)
                t = dve(lambda e, b=b, t0=t0, t1=t1: e.tensor_scalar(rstd[:, t0:t1], ps[:, b, 0:t1 - t0], inv, EPS, ALU.mult, ALU.add), tm)
                G.give(gk, t)
                v, r, w = rstd[:, t0:t1], nrm[:, 0, t0:t1], nrm[:, 1, t0:t1]
                ta = act(lambda e, v=v, r=r: e.activation(r, v, ACT.Sqrt), t)
                t = dve(lambda e, r=r: e.reciprocal(r, r), ta)
                t = dve(lambda e, r=r, w=w: e.tensor_tensor(w, r, r, ALU.mult), t)
                t = dve(lambda e, v=v, w=w: e.tensor_tensor(w, w, v, ALU.mult), t)
                t = dve(lambda e, w=w: e.tensor_scalar(w, w, -0.5, 1.5, ALU.mult, ALU.add), t)
                t = dve(lambda e, v=v, r=r, w=w: e.tensor_tensor(v, r, w, ALU.mult), t)
                tr.append(t)
                sqr.give(0, t)
                sqr.give(1, t)
            return tr

        blk1 = ExitStack()
        hT = sb("hT", [P, 8, LT], c=blk1)
        yssd = sb("yssd", [P, 16, L], c=blk1)

        t_hx = [dx.start(sp, hT[:, :, 0:L], A["xT"]), dx.start(sp, hT[:, :, L:LT], A["ctxT"])]
        t_hx = t_hx[-1]
        t_rows = dc.start(sp, rows[:, :], A["rows"])
        t_cst = dc.start(sp, cst[:, :], A["consts"][:, 0:896])
        for e in (pe, dve, act, pool):
            e.wait(t_cst)
        t_mb = dve(lambda e: e.tensor_copy(maskb[:, 0, :], ident))
        t_mb = dve(lambda e: e.tensor_copy(maskb[:, 1:3, :].rearrange("p a b -> p (a b)"), cst[:, 512:768]))
        pe.wait(t_mb)
        ta = act(lambda e: e.activation(tmp16[:, :], V("c", 0, 16), ACT.Tanh, scale=0.5))
        t = dve(lambda e: e.scalar_tensor_tensor(out=cs_[:, :], in0=tmp16[:, :], scalar=1.0, in1=V("c", 0, 16), op0=ALU.add, op1=ALU.mult), ta)
        t_c = dve(lambda e: e.tensor_scalar(cs_[:, :], cs_[:, :], 0.5, None, ALU.mult), t)
        for nm in ("cw0", "cw1", "cw2", "cb"):
            dve(lambda e, nm=nm: e.tensor_scalar(V(nm, 0, 24), V(nm, 0, 24), 0.5, None, ALU.mult))
        for nm in ("fw0", "fw1", "fw2", "fb"):
            dve(lambda e, nm=nm: e.tensor_scalar(V(nm, 0, 22), V(nm, 0, 22), 0.5, None, ALU.mult))

        def mod_blocks(m0, m1):
            gk, b, free = G.take()
            pe.wait(free, t_c)
            for m in range(m0, m1):
                wk, wap, wt = wload(A["w_mod"][m], 1024)
                pe.wait(wt)
                for k in range(8):
                    f = lambda e, m=m, k=k, wap=wap, b=b: e.matmul(ps[:, b, 2 * (m - m0):2 * (m - m0) + 2], wap[:, k * 128:(k + 1) * 128],
                                                                   cs_[:, 2 * k:2 * k + 2], start=(k == 0), stop=(k == 7))
                    if k == 7:
                        t = pe(f)
                    else:
                        pe.quiet(f)
                wring.give(wk, t)
            o = VOFF["bmod"][0]
            n = m1 - m0
            t = dve(lambda e: e.tensor_tensor(modS[:, m0:m1, :], ps[:, b, 0:2 * n].rearrange("p (m s) -> p m s", s=2),
                                              vc[:, o + m0:o + m1].unsqueeze(2).to_broadcast([P, n, 2]), ALU.add), t)
            G.give(gk, t)
            return t

        t_r = norm_T(lambda k: hT[:, k, :], 8, [(0, L), (L, LT)], None, t_hx)
        t = mod_blocks(0, 16)
        t = dve(lambda e: e.tensor_scalar(A1[:, :, :], modS[:, 8:16, :], 1.0, None, ALU.add), t)
        t_A1 = dve(lambda e: e.tensor_tensor(A1[:, :, :], A1[:, :, :], V("g1", 0, 8).unsqueeze(2).to_broadcast([P, 8, 2]), ALU.mult), t)
        t_h = []
        for k in range(8):
            t = dve(lambda e, k=k: e.tensor_tensor(hT[:, k, :], hT[:, k, :], rstd[:, :], ALU.mult), t_r, t_A1)
            act(lambda e, k=k: e.activation(hT[:, k, 0:L], hT[:, k, 0:L], ACT.Identity, bias=modS[:, k, 0:1], scale=A1[:, k, 0:1]), t)
            t_h.append(act(lambda e, k=k: e.activation(hT[:, k, L:LT], hT[:, k, L:LT], ACT.Identity, bias=modS[:, k, 1:2], scale=A1[:, k, 1:2])))
        pe.wait(t_h)
        t_mod2 = mod_blocks(16, 48)
        t = dve(lambda e: e.tensor_scalar(A2[:, :], modS[:, 32:40, 0], 1.0, None, ALU.add), t_mod2)
        t_A2 = dve(lambda e: e.tensor_tensor(A2[:, :], A2[:, :], V("g2", 0, 8), ALU.mult), t)

        def softplus(x, u, w, n):
            t = dve(lambda e: e.scalar_tensor_tensor(out=u, in0=x, scalar=-1.0, in1=x, op0=ALU.mult, op1=ALU.max), dve.last())
            t = act(lambda e: e.activation(u, u, ACT.Exp, scale=-1.0), t)
            t1 = dve(lambda e: e.tensor_scalar(w, u, 1.0, None, ALU.add), t)
            ta = act(lambda e: e.activation(n, w, ACT.Ln), t1)
            t = dve(lambda e: e.scalar_tensor_tensor(out=u, in0=w, scalar=-1.0, in1=u, op0=ALU.add, op1=ALU.subtract), t1)
            t = dve(lambda e: e.reciprocal(w, w), t, ta)
            t = dve(lambda e: e.scalar_tensor_tensor(out=u, in0=u, scalar=-1.0, in1=w, op0=ALU.mult, op1=ALU.mult), t)
            t = dve(lambda e: e.tensor_tensor(u, u, n, ALU.add), t, ta)
            return dve(lambda e: e.scalar_tensor_tensor(out=x, in0=x, scalar=0.0, in1=u, op0=ALU.max, op1=ALU.add), t)

        ssd = ExitStack()
        dt_ = sb("dt_", [P, 6, 64], c=ssd)
        la = sb("la", [P, 6, 64], c=ssd)
        csm = sb("csm", [P, 6, 64], c=ssd)
        wdec = sb("wdec", [P, 6, 64], c=ssd)
        etot = sb("etot", [P, 6, 64], c=ssd)
        csT = sb("csT", [64, L], c=ssd)
        csd = A["csd"]
        xsT = sb("xsT", [P, 4, LT], c=ssd)
        BT = sb("BT", [P, LT], c=ssd)
        CT = sb("CT", [P, L], c=ssd)
        xtok = sb("xtok", [P, 6, 512], c=ssd)
        Btok = sb("Btok", [P, 6, 128], c=ssd)
        st = sb("st", [P, 2, 4, 512], c=ssd)
        stt_ = sb("stt_", [P, 512], c=ssd)
        st0 = sb("st0", [P, 512], c=ssd)
        csbc = sb("csbc", [P, 2, 16, 128], c=ssd)
        cbm = sb("cbm", [P, 2, 128], c=ssd)
        Ew = sb("Ew", [P, 2, 8, 128], c=ssd)
        Cs = sb("Cs", [P, 2, 8, 128], c=ssd)
        xw = sb("xw", [P, 2, 512], c=ssd)

        wk, wdt, wt = wload(A["w_dt"], 512)
        gk, b, free = G.take()
        pe.wait(free, wt)
        for c in range(6):
            for k in range(8):
                f = lambda e, c=c, k=k, b=b: e.matmul(ps[:, b, c * 64:c * 64 + 64], hT[:, k, c * 128:c * 128 + 128], wdt[:, k * 64:k * 64 + 64],
                                                      start=(k == 0), stop=(k == 7))
                if c == 5 and k == 7:
                    t = pe(f)
                else:
                    pe.quiet(f)
        wring.give(wk, t)
        flat = lambda x: x[:, :, :].rearrange("p a b -> p (a b)")
        t = dve(lambda e, b=b: e.tensor_tensor(dt_[:, :, :], ps[:, b, 0:384].rearrange("p (c h) -> p c h", h=64),
                                               rows[:, 0:64].unsqueeze(1).to_broadcast([P, 6, 64]), ALU.add), t)
        G.give(gk, t)
        ta = act(lambda e: e.activation(rows[:, 64:128], rows[:, 64:128], ACT.Exp))
        t_dt = softplus(flat(dt_), flat(csm), flat(wdec), flat(etot))
        t = dve(lambda e: e.scalar_tensor_tensor(out=la[:, :, :], in0=dt_[:, :, :], scalar=-1.0,
                                                 in1=rows[:, 64:128].unsqueeze(1).to_broadcast([P, 6, 64]), op0=ALU.mult, op1=ALU.mult), t_dt, ta)
        pv = lambda b: ps[:, b, 0:384].rearrange("p (c h) -> p c h", h=64)
        pe.quiet(lambda e: e.matmul(pv(2)[:, :, 0:32], C("trif"), la[:, :, 0:32], start=True, stop=True), t)
        t1 = pe(lambda e: e.matmul(pv(3)[:, :, 32:64], C("trib"), la[:, :, 32:64], start=True, stop=True))
        t2 = pe(lambda e: e.matmul(pv(4), ones, la[:, :, :], start=True, stop=True))
        dve(lambda e: e.tensor_copy(csm[:, :, 0:32], pv(2)[:, :, 0:32]), t1)
        t = dve(lambda e: e.tensor_copy(csm[:, :, 32:64], pv(3)[:, :, 32:64]))
        t = dve(lambda e: e.tensor_tensor(wdec[:, :, :], pv(4), csm[:, :, :], ALU.subtract), t2, t)
        te = act(lambda e: e.activation(etot[:, :, :], pv(4), ACT.Exp), t2, t)
        t = dve(lambda e: e.tensor_scalar(flat(wdec), flat(wdec), 0.0, None, ALU.min), t)
        ta = act(lambda e: e.activation(wdec[:, :, :], wdec[:, :, :], ACT.Exp), t)
        t_wd = dve(lambda e: e.tensor_tensor(wdec[:, :, :], wdec[:, :, :], dt_[:, :, :], ALU.mult), ta)
        for c in range(4):
            t = pe(lambda e, c=c: e.transpose(ps[0:64, 5, c * 128:c * 128 + 128], csm[:, c, :], ident), t_wd)
        t = dve(lambda e: e.tensor_copy(csT[:, :], ps[0:64, 5, :]), t)
        dcs = Dma("s_csd")
        t_csd = dcs.start(pool, csd.rearrange("d h t -> (d h) t"), csT[:, :], t)
        pool.wait(t_csd, te)
        pe.wait(t_wd)
        dve.wait(te)
        dbc = [Dma("s_bc0"), Dma("s_bc1")]
        t_pre = t_wd

        def conv(psum, T, m, names, dst, *toks):
            w0, w1, w2, bb = (V(n, m) for n in names)
            t = act(lambda e: e.activation(dst, psum, ACT.Identity, bias=bb, scale=w1), toks)
            t = dve(lambda e: e.scalar_tensor_tensor(out=dst[:, 1:T], in0=psum[:, 0:T - 1], scalar=w0, in1=dst[:, 1:T],
                                                     op0=ALU.mult, op1=ALU.add), t)
            return dve(lambda e: e.scalar_tensor_tensor(out=dst[:, 0:T - 1], in0=psum[:, 1:T], scalar=w2, in1=dst[:, 0:T - 1],
                                                        op0=ALU.mult, op1=ALU.add), t)

        tring = Ring([sq[:, 0, 0:L], sq[:, 1, 0:L]])
        bcr = Ring([0, 1])
        CW = ("cw0", "cw1", "cw2", "cb")
        Tb = Ring([2, 3])
        Yb = Ring([4, 5])
        Sb = Ring([6])
        Qb = Ring([7])
        busy = {"x": [], "B": [], "C": [], "xtok": [], "Btok": [], "st": [], "acc": None}
        tacc_ssd = None
        for g in range(4):
            tx = {}
            for i in range(6):
                m = [g * 4 + 0, g * 4 + 1, g * 4 + 2, g * 4 + 3, 16 + g, 20 + g][i]
                rng = [(0, L), (L, LT)] if i < 5 else [(0, L)]
                D = xsT[:, i, :] if i < 4 else (BT[:, :] if i == 4 else CT[:, :])
                wait = busy["x"] if i < 4 else busy["B"] if i == 4 else busy["C"]
                outs = gemm(A["w_xbc"], m, 8, lambda k: hT[:, k, :], rng)
                tt = []
                for (t0, t1), (gk, pp, tok) in zip(rng, outs):
                    dst = D[:, t0:t1]
                    t = conv(pp, t1 - t0, m, CW, dst, tok, wait)
                    G.give(gk, t)
                    i_, s, free = tring.take()
                    ta = act(lambda e, s=s, dst=dst: e.activation(s[:, 0:dst.shape[1]], dst, ACT.Tanh), t, free)
                    t = dve(lambda e, s=s, dst=dst: e.scalar_tensor_tensor(out=dst, in0=s[:, 0:dst.shape[1]], scalar=1.0, in1=dst,
                                                                           op0=ALU.add, op1=ALU.mult), ta)
                    tring.give(i_, t)
                    tt.append(t)
                tx[i] = tt
            t_xt = {}
            for c in range(6):
                ik, b, free = Tb.take()
                for j in range(4):
                    t = pe(lambda e, b=b, j=j, c=c: e.transpose(ps[:, b, j * 128:(j + 1) * 128], xsT[:, j, c * 128:(c + 1) * 128], ident), free, tx[j])
                if c % 2:
                    t = dve(lambda e, b=b, c=c: e.tensor_copy(xtok[:, c, :], bank(b)), t, busy["xtok"])
                else:
                    t = act(lambda e, b=b, c=c: e.copy(xtok[:, c, :], bank(b)), t, busy["xtok"])
                Tb.give(ik, t)
                t_xt[c] = t
            for c0, c1 in ((0, 4), (4, 6)):
                ik, b, free = Tb.take()
                for c in range(c0, c1):
                    t = pe(lambda e, b=b, c=c, c0=c0: e.transpose(ps[:, b, (c - c0) * 128:(c - c0 + 1) * 128], BT[:, c * 128:(c + 1) * 128], ident), free, tx[4])
                t = act(lambda e, b=b, c0=c0, c1=c1: e.copy(Btok[:, c0:c1, :].rearrange("p a b -> p (a b)"), ps[:, b, 0:(c1 - c0) * 128]), t, busy["Btok"])
                Tb.give(ik, t)
            t_bt = t
            t_st = {}
            xwr = Ring([xw[:, 0, :], xw[:, 1, :]]) if g == 0 else xwr
            last_st = []
            for d in (0, 1):
                prev, tp = None, None
                seq = [4, 5, 0, 1, 2] if d == 0 else [5, 4, 3, 2, 1]
                for n, c in enumerate(seq):
                    h0 = d * 32 + g * 8
                    ik, x_, free = xwr.take()
                    t = pool(lambda e, x_=x_, c=c, h0=h0: e.tensor_tensor(x_.rearrange("p (r q) -> p r q", q=64), xtok[:, c, :].rearrange("p (r q) -> p r q", q=64),
                                                                           wdec[:, c, h0:h0 + 8].unsqueeze(2).to_broadcast([P, 8, 64]), ALU.mult),
                             free, t_xt[c], t_wd)
                    sk, b, sfree = Sb.take()
                    t = pe(lambda e, b=b, c=c, x_=x_: e.matmul(bank(b), Btok[:, c, :], x_, start=True, stop=True), t, t_bt, sfree)
                    xwr.give(ik, t)
                    if n == 0:
                        dst = st0[:, :]
                        tp = dve(lambda e, b=b, dst=dst: e.tensor_copy(dst, bank(b)), t, tp)
                    else:
                        use = n - 1 if d == 0 else 4 - n
                        dst = st[:, d, use, :]
                        t2 = dve(lambda e, prev=prev, c=c, h0=h0: e.tensor_tensor(stt_[:, :].rearrange("p (r q) -> p r q", q=64), prev.rearrange("p (r q) -> p r q", q=64),
                                                                                  etot[:, c, h0:h0 + 8].unsqueeze(2).to_broadcast([P, 8, 64]), ALU.mult), tp)
                        tp = dve(lambda e, b=b, dst=dst: e.tensor_tensor(dst, stt_[:, :], bank(b), ALU.add), t, t2, busy["st"])
                        t_st[(d, use)] = tp
                    prev = dst
                    Sb.give(sk, tp)
            busy_y = []
            for c in range(4):
                bk, bb, bfree = bcr.take()
                for d in (0, 1):
                    t_b = dbc[bk].start(pool, csbc[:, bb, d * 8:d * 8 + 8, :],
                                        csd[d, g * 8:g * 8 + 8, c * 128:(c + 1) * 128].unsqueeze(0).to_broadcast([P, 8, 128]), bfree)
                qk, b, free = Qb.take()
                t = pe(lambda e, b=b, c=c: e.matmul(ps[:, b, 0:128], BT[:, c * 128:(c + 1) * 128], CT[:, c * 128:(c + 1) * 128], start=True, stop=True), free, tx[4], tx[5])
                dve(lambda e, b=b: e.tensor_tensor(cbm[:, 0, :], ps[:, b, 0:128], C("trif"), ALU.mult), t)
                t_cb = dve(lambda e, b=b: e.tensor_tensor(cbm[:, 1, :], ps[:, b, 0:128], C("trib"), ALU.mult))
                Qb.give(qk, t_cb)
                tw = []
                tcs = []
                for d in (0, 1):
                    for r in range(8):
                        h = d * 32 + g * 8 + r
                        t = dve(lambda e, d=d, r=r, h=h, bb=bb, c=c: e.tensor_scalar(Ew[:, d, r, :], csbc[:, bb, d * 8 + r, :], csm[:, c, h:h + 1], 0.0,
                                                                                     ALU.subtract, ALU.min), t_b, busy_y)
                    ta = act(lambda e, d=d: e.activation(Ew[:, d, :, :], Ew[:, d, :, :], ACT.Exp), t)
                    te_ = act(lambda e, d=d, bb=bb: e.activation(Cs[:, d, :, :], csbc[:, bb, d * 8:d * 8 + 8, :], ACT.Exp), t_b, busy_y)
                    tcs.append(pool(lambda e, d=d, c=c: e.tensor_tensor(Cs[:, d, :, :], Cs[:, d, :, :],
                                                                       CT[:, c * 128:(c + 1) * 128].unsqueeze(1).to_broadcast([P, 8, 128]), ALU.mult), te_, tx[5]))
                    for r in range(8):
                        h = d * 32 + g * 8 + r
                        t = dve(lambda e, d=d, r=r, h=h, c=c: e.scalar_tensor_tensor(out=Ew[:, d, r, :], in0=Ew[:, d, r, :], scalar=dt_[:, c, h:h + 1],
                                                                                     in1=cbm[:, d, :], op0=ALU.mult, op1=ALU.mult), ta, t_cb)
                bcr.give(bk, te_, t)
                t_w = dve(lambda e: e.tensor_tensor(Ew[:, 0, :, :], Ew[:, 0, :, :], Ew[:, 1, :, :], ALU.add), t)
                yk, b, free = Yb.take()
                pe.wait(free, t_w, tcs, t_st[(0, c)], t_st[(1, c)])
                for r in range(8):
                    o = ps[(r % 2) * 64:(r % 2) * 64 + 64, b, (r // 2) * 128:(r // 2 + 1) * 128]
                    pe.quiet(lambda e, o=o, c=c, r=r: e.matmul(o, xtok[:, c, r * 64:r * 64 + 64], Ew[:, 0, r, :], start=True, stop=False))
                    pe.quiet(lambda e, o=o, c=c, r=r: e.matmul(o, st[:, 0, c, r * 64:r * 64 + 64], Cs[:, 0, r, :], start=False, stop=False))
                    t_y = pe(lambda e, o=o, c=c, r=r: e.matmul(o, st[:, 1, c, r * 64:r * 64 + 64], Cs[:, 1, r, :], start=False, stop=True))
                busy_y = [t_y]
                for j in range(4):
                    t = dve(lambda e, b=b, j=j, c=c, g=g: e.scalar_tensor_tensor(out=yssd[:, 4 * g + j, c * 128:(c + 1) * 128], in0=xsT[:, j, c * 128:(c + 1) * 128],
                                                                                 scalar=V("dsk", 4 * g + j), in1=ps[:, b, j * 128:(j + 1) * 128], op0=ALU.mult, op1=ALU.add), t_y)
                Yb.give(yk, t)
            busy = {"x": [t], "B": [t_y], "C": [t_y, tcs], "xtok": [t_y], "Btok": [t_y], "st": [t_y]}
            for j in range(4):
                m = 4 * g + j
                (gk, pp, tok), = gemm(A["w_z"], m, 8, lambda k: hT[:, k, :], [(0, L)])
                i_, s, free = tring.take()
                ta = act(lambda e, s=s, pp=pp: e.activation(s, pp, ACT.Tanh, scale=0.5), tok, free)
                t1 = dve(lambda e, s=s, pp=pp: e.scalar_tensor_tensor(out=s, in0=s, scalar=1.0, in1=pp, op0=ALU.add, op1=ALU.mult), ta)
                G.give(gk, t1)
                t1 = dve(lambda e, s=s, m=m: e.tensor_tensor(yssd[:, m, :], yssd[:, m, :], s, ALU.mult), t1, t)
                ta = act(lambda e, s=s, m=m: e.activation(s, yssd[:, m, :], ACT.Square), t1)
                if m == 0:
                    tacc_ssd = dve(lambda e, s=s: e.tensor_copy(acc[:, 0:L], s), ta)
                else:
                    tacc_ssd = dve(lambda e, s=s: e.tensor_tensor(acc[:, 0:L], acc[:, 0:L], s, ALU.add), ta, tacc_ssd)
                t_yg = act(lambda e, m=m: e.activation(yssd[:, m, :], yssd[:, m, :], ACT.Copy, scale=V("sg", m)), ta)
                tring.give(i_, tacc_ssd)
        t = norm_rstd([(0, L)], tacc_ssd, 0.25 / 2048)
        t_rs = dve(lambda e: e.tensor_scalar(rstd[:, 0:L], rstd[:, 0:L], 0.25, None, ALU.mult), t)
        fence()
        ssd.close()

        att = ExitStack()
        qT = sb("qT", [P, 8, L], c=att)
        wa = ExitStack()
        kT = sb("kT", [P, 2, LT], c=wa)
        vt = sb("vt", [P, 6, 256], c=wa)
        rope = sb("rope", [P, 2, L], c=wa)
        raw = sb("raw", [P, 2, L], c=wa)
        rt = sb("rt", [P, 2, L], c=wa)
        Pm = sb("Pm", [P, 4, 640], c=wa)
        PT = sb("PT", [P, 5, 4, 128], c=wa)
        small = sb("small", [P, 4, 4], c=wa)
        dr = Dma("s_rope")
        t_rope = dr.start(pool, rope[:, :, :].rearrange("p a b -> p (a b)"), A["consts"][:, 896:1920], fence())
        rawr = Ring([0, 1])
        Pb = Ring([2, 3])
        t_q = {}
        for m in range(10):
            isq = m < 8
            rng = [(0, L)] if isq else [(0, L), (L, LT)]
            outs = gemm(A["w_qk"], m, 8, lambda k: hT[:, k, :], rng)
            gk, pp, tok = outs[0]
            ik, i_, free = rawr.take()
            ta = act(lambda e, i_=i_, pp=pp, isq=isq: e.mul(raw[:, i_, :], pp, 0.125 if isq else 1.0), tok, free)
            G.give(gk, ta)
            bk, b, bfree = Pb.take()
            tp = pe(lambda e, b=b, i_=i_: e.matmul(bank(b), C("perm"), raw[:, i_, :], start=True, stop=True), ta, bfree)
            tg = pool(lambda e, i_=i_: e.tensor_tensor(rt[:, i_, :], raw[:, i_, :], rope[:, 0, :], ALU.mult), ta, t_rope, free)
            dst = qT[:, m, :] if isq else kT[:, m - 8, 0:L]
            t = dve(lambda e, b=b, dst=dst: e.tensor_tensor(dst, bank(b), rope[:, 1, :], ALU.mult), tp, t_rope)
            Pb.give(bk, t)
            t = dve(lambda e, i_=i_, dst=dst: e.tensor_tensor(dst, dst, rt[:, i_, :], ALU.add), t, tg)
            rawr.give(ik, tp, tg, t)
            t_q[m] = [t]
            if not isq:
                gk, pp, tok = outs[1]
                ta = act(lambda e, pp=pp, m=m: e.copy(kT[:, m - 8, L:LT], pp), tok)
                G.give(gk, ta)
                t_q[m].append(ta)

        def tokmajor(wd, nb, src, NT, dst):
            tl = []
            for q in range(nb):
                s0 = wload(wd[q, 0], 1024)
                s1 = wload(wd[q, 1], 1024)
                for c in range(NT):
                    gk, b, free = G.take()
                    pe.wait(free, s0[2], s1[2])
                    for k in range(8):
                        w = (s0, s1)[k // 4][1][:, (k % 4) * 256:(k % 4 + 1) * 256]
                        f = lambda e, b=b, k=k, c=c, w=w: e.matmul(ps[:, b, 0:256], src(k)[:, c * 128:(c + 1) * 128], w, start=(k == 0), stop=(k == 7))
                        if k == 7:
                            t = pe(f)
                        else:
                            pe.quiet(f)
                    ta = act(lambda e, b=b, c=c, q=q: e.copy(dst(c)[:, q * 256:(q + 1) * 256], ps[:, b, 0:256]), t)
                    G.give(gk, ta)
                    tl.append(ta)
                wring.give(s0[0], t)
                wring.give(s1[0], t)
            return tl

        t_v = tokmajor(A["w_v"], 1, lambda k: hT[:, k, :], 6, lambda c: vt[:, c, :])

        def softmax(S, W, dstP, sm, scale, sink, ready, free):
            t = dve(lambda e: e.tensor_reduce(sm[:, 0:1], S, AXX, ALU.max), ready, free)
            if sink is not None:
                t = dve(lambda e: e.tensor_scalar(sm[:, 1:2], sm[:, 0:1], sink, -1.0, ALU.max, ALU.mult), t)
            else:
                t = dve(lambda e: e.tensor_scalar(sm[:, 1:2], sm[:, 0:1], -scale, None, ALU.mult), t)
            ta = act(lambda e: e.activation(dstP, S, ACT.Exp, bias=sm[:, 1:2], scale=scale, accum_out=sm[:, 2:3]), t, free)
            if sink is not None:
                ta = act(lambda e: e.activation(sm[:, 3:4], sink, ACT.Exp, bias=sm[:, 1:2]), t)
            return ta

        def normalise(dstP, sm, sink, ta):
            t = ta
            if sink is not None:
                t = dve(lambda e: e.tensor_tensor(sm[:, 2:3], sm[:, 2:3], sm[:, 3:4], ALU.add), t)
            t = dve(lambda e: e.reciprocal(sm[:, 1:2], sm[:, 2:3]), t)
            return dve(lambda e: e.tensor_scalar(dstP, dstP, sm[:, 1:2], None, ALU.mult), t)

        t_kv = [t_q[8], t_q[9], t_v]
        pe.wait([t_q[m] for m in range(10)], t_v)
        Sr = Ring([2, 4])
        Tr = Ring([6])
        Or = Ring([7])
        pr = Ring([0, 1, 2, 3])
        pt_busy = []
        for n in range(4):
            lo = max(n - 1, 0)
            hi = min(n + 1, 3)
            nw = hi - lo + 1
            for kv in range(4):
                half = (kv % 2) * 64
                kt = kv // 2
                state = []

                def scores(j):
                    h = 4 * kv + j
                    qrow = (h % 2) * 64
                    sk, b, free = Sr.take()
                    w0 = 512 - nw * 128
                    q = qT[qrow:qrow + 64, h // 2, n * 128:(n + 1) * 128]
                    K = (kT if qrow == half else kTs)
                    kk = K[qrow:qrow + 64, kt, :]
                    pe.wait(free)
                    first = [0]
                    pe.quiet(lambda e: e.matmul(ps[:, b, w0:512], q, kk[:, lo * 128:(hi + 1) * 128], start=True, stop=False))
                    if n > 0:
                        pe.quiet(lambda e: e.matmul(ps[:, b, w0:w0 + 128], maskb[:, 0, :], maskb[:, 1, :], start=False, stop=(n == 3)))
                    if n < 3:
                        pe.quiet(lambda e: e.matmul(ps[:, b, 384:512], maskb[:, 0, :], maskb[:, 2, :], start=False, stop=True))
                    t = pe(lambda e: e.matmul(ps[:, b + 1, 0:256], q, kk[:, L:LT], start=True, stop=True))
                    W = nw * 128 + 256
                    S = ps[:, b:b + 2, :].rearrange("p a b -> p (a b)")[:, w0:w0 + W]
                    pk, pi, pfree = pr.take()
                    ta = softmax(S, W, Pm[:, pi, 0:W], small[:, pi, :], 1.0, rows[:, 128 + h:129 + h], t, pfree)
                    Sr.give(sk, ta)
                    return pk, pi, ta, W, h

                if n == 0 and kv == 0:
                    kTs = sb("kTs", [P, 2, LT], c=wa)
                    dks = Dma("s_ks")
                    pool.wait(t_q[8], t_q[9])
                    dks.start(pool, kTs[0:64, :, :], kT[64:128, :, :])
                    pe.wait(dks.start(pool, kTs[64:128, :, :], kT[0:64, :, :]))
                pend = []
                for j in range(4):
                    pend.append(scores(j))
                tn = []
                for j, (pk, pi, ta, W, h) in enumerate(pend):
                    tn.append(normalise(Pm[:, pi, 0:W], small[:, pi, :], 1, ta))
                nk = nw + 2
                t_pt = []
                for kb in range(nk):
                    tk, b, free = Tr.take()
                    for j, (pk, pi, ta, W, h) in enumerate(pend):
                        t = pe(lambda e, b=b, j=j, pi=pi, kb=kb: e.transpose(ps[:, b, j * 128:(j + 1) * 128], Pm[:, pi, kb * 128:(kb + 1) * 128], ident), free, tn[j])
                    if kb % 2:
                        t2 = dve(lambda e, b=b, kb=kb: e.tensor_copy(PT[:, kb, :, :].rearrange("p a b -> p (a b)"), bank(b)), t, pt_busy)
                    else:
                        t2 = act(lambda e, b=b, kb=kb: e.copy(PT[:, kb, :, :].rearrange("p a b -> p (a b)"), bank(b)), t, pt_busy)
                    Tr.give(tk, t2)
                    t_pt.append(t2)
                for j, (pk, pi, ta, W, h) in enumerate(pend):
                    pr.give(pk, t, tn)
                ok, b, free = Or.take()
                pe.wait(free, t_pt)
                for par in (0, 1):
                    for kb in range(nk):
                        c = lo + kb if kb < nw else 4 + kb - nw
                        t = pe(lambda e, b=b, par=par, kb=kb, c=c, kv=kv, nk=nk: e.matmul(
                            ps[par * 64:par * 64 + 64, b, 0:256].rearrange("p (a b) -> p a b", b=128), vt[:, c, kv * 64:(kv + 1) * 64],
                            PT[:, kb, par:4:2, :], start=(kb == 0), stop=(kb == nk - 1)))
                pt_busy = [t]
                t_o = dve(lambda e, b=b, kv=kv, n=n: e.tensor_copy(qT[:, 2 * kv:2 * kv + 2, n * 128:(n + 1) * 128],
                                                                   ps[:, b, 0:256].rearrange("p (a b) -> p a b", b=128)), t)
                Or.give(ok, t_o)
        fence()
        wa.close()

        mg = ExitStack()
        mrg = sb("mrg", [P, 8, L], c=mg)
        gt = sb("gt", [P, 4, L], c=mg)
        gr = Ring([0, 1, 2, 3])
        t_m = []
        for m in range(8):
            t_ = []
            for which, (wd, KT, src) in enumerate((("w_os", 16, yssd), ("w_oa", 8, qT))):
                (gk, pp, tok), = gemm(A["w_g"], which * 8 + m, 8, lambda k: hT[:, k, :], [(0, L)])
                ik, i_, free = gr.take()
                ta = act(lambda e, i_=i_, pp=pp: e.activation(gt[:, i_, :], pp, ACT.Tanh, scale=0.5), tok, free)
                G.give(gk, ta)
                (gk, pp, tok), = gemm(A[wd], m, KT, lambda k, src=src: src[:, k, :], [(0, L)])
                t = dve(lambda e, i_=i_, pp=pp: e.scalar_tensor_tensor(out=gt[:, i_, :], in0=gt[:, i_, :], scalar=1.0, in1=pp, op0=ALU.add, op1=ALU.mult), tok, ta)
                G.give(gk, t)
                t_.append((ik, i_, t))
            (ka, ia, ta), (kb_, ib, tb) = t_
            t = dve(lambda e, ia=ia: e.tensor_tensor(gt[:, ia, :], gt[:, ia, :], rstd[:, 0:L], ALU.mult), ta)
            t = dve(lambda e, ia=ia, ib=ib, m=m: e.scalar_tensor_tensor(out=mrg[:, m, :], in0=gt[:, ib, :], scalar=0.5, in1=gt[:, ia, :], op0=ALU.mult, op1=ALU.add), t, tb)
            gr.give(ka, t)
            gr.give(kb_, t)
            t_m.append(t)
        fence()
        mg_marks = fence()
        xT = sb("xT", [P, 8, L], c=mg)
        t_x = Dma("s_xr").start(pool, xT[:, :, :], A["xT"], mg_marks)
        t_xr = []
        for m in range(8):
            (gk, pp, tok), = gemm(A["w_out"], m, 8, lambda k: mrg[:, k, :], [(0, L)], t_m)
            t = dve(lambda e, m=m, pp=pp: e.scalar_tensor_tensor(out=xT[:, m, :], in0=pp, scalar=modS[:, 16 + m, 0:1], in1=xT[:, m, :], op0=ALU.mult, op1=ALU.add), tok, t_x)
            G.give(gk, t)
            t_xr.append(t)
        dsx = Dma("s_sx")
        t_sx = dsx.start(pool, A["xsc"], xT[:, :, :], t_xr)
        fence()
        pool.wait(t_sx)
        mg.close()
        att.close()
        blk1.close()

        X = sb("X", [P, 8, L])
        t_x = dsx.start(pool, X[:, :, :], A["xsc"])
        ff = ExitStack()
        h2 = sb("h2", [P, 8, L], c=ff)
        pr_ = sb("pr_", [P, 22, L], c=ff)
        ua = sb("ua", [P, 4, L], c=ff)
        ub = sb("ub", [P, 2, L], c=ff)
        t_r = norm_T(lambda k: X[:, k, :], 8, [(0, L)], None, t_x)
        t_h = []
        for k in range(8):
            t = dve(lambda e, k=k: e.tensor_tensor(h2[:, k, :], X[:, k, :], rstd[:, 0:L], ALU.mult), t_r)
            t_h.append(act(lambda e, k=k: e.activation(h2[:, k, :], h2[:, k, :], ACT.Identity, bias=modS[:, 24 + k, 0:1], scale=A2[:, k:k + 1]), t, t_A2))
        pe.wait(t_h)
        uar, ubr = Ring([0, 1, 2, 3]), Ring([0, 1])
        FW = ("fw0", "fw1", "fw2", "fb")
        t_p = []
        for m in range(22):
            tt = []
            for which in (0, 1):
                mm = m + 22 * which
                (gk, pp, tok), = gemm(A["w_up"], mm, 8, lambda k: h2[:, k, :], [(0, L)])
                ik, i_, free = uar.take()
                t = conv(pp, L, mm, FW, ua[:, i_, :], tok, free)
                G.give(gk, t)
                tt.append((ik, i_, t))
            (ka, ia, ta_), (kb_, ib, tb_) = tt
            k2, i2, free = ubr.take()
            ta = act(lambda e, i2=i2, ia=ia: e.activation(ub[:, i2, :], ua[:, ia, :], ACT.Tanh), ta_, free)
            t = dve(lambda e, i2=i2, ia=ia: e.scalar_tensor_tensor(out=ub[:, i2, :], in0=ub[:, i2, :], scalar=1.0, in1=ua[:, ia, :], op0=ALU.add, op1=ALU.mult), ta)
            t = pool(lambda e, i2=i2, ib=ib, m=m: e.tensor_tensor(pr_[:, m, :], ub[:, i2, :], ua[:, ib, :], ALU.mult), t, tb_)
            uar.give(ka, t)
            uar.give(kb_, t)
            ubr.give(k2, t)
            t_p.append(t)
        t_x2 = []
        for m in range(8):
            (gk, pp, tok), = gemm(A["w_down"], m, 22, lambda k: pr_[:, k, :], [(0, L)], t_p)
            t = dve(lambda e, m=m, pp=pp: e.scalar_tensor_tensor(out=X[:, m, :], in0=pp, scalar=modS[:, 40 + m, 0:1], in1=X[:, m, :], op0=ALU.mult, op1=ALU.add), tok)
            G.give(gk, t)
            t_x2.append(t)
        t_r = norm_T(lambda k: X[:, k, :], 8, [(0, L)], None, t_x2)
        tl = []
        for k in range(8):
            t = dve(lambda e, k=k: e.tensor_tensor(X[:, k, :], X[:, k, :], rstd[:, 0:L], ALU.mult), t_r)
            tl.append(act(lambda e, k=k: e.activation(X[:, k, :], X[:, k, :], ACT.Copy, scale=V("fg", k)), t))
        fence()
        ff.close()
        H = sb("H", [P, 8, L])
        t_r = norm_T(lambda k: X[:, k, :], 8, [(0, L)], None, tl)
        tl = []
        for k in range(8):
            tl.append(dve(lambda e, k=k: e.scalar_tensor_tensor(out=H[:, k, :], in0=X[:, k, :], scalar=V("gn", k), in1=rstd[:, 0:L], op0=ALU.mult, op1=ALU.mult), t_r))
        pe.wait(tl)

        yf = sb("yf", [P, 6, L])
        ysv = sb("ysv", [P, 6, L])
        ym = sb("ym", [P, 4, L])

        fx = ExitStack()
        kf = sb("kf", [P, 6, L], c=fx)
        vf = sb("vf", [P, 4, 768], c=fx)
        lf = sb("lf", [P, 4, 12], c=fx)
        l2 = sb("l2", [P, 3, 48], c=fx)
        FT = sb("FT", [12, L], c=fx)
        Pf = sb("Pf", [P, 4, L], c=fx)
        PTf = sb("PTf", [P, 2, 4, L], c=fx)
        smf = sb("smf", [P, 4, 4], c=fx)
        tq = []
        for m in range(12):
            (gk, pp, tok), = gemm(A["w_fqk"], m, 8, lambda k: H[:, k, :], [(0, L)])
            dst = yf[:, m, :] if m < 6 else kf[:, m - 6, :]
            ta = act(lambda e, dst=dst, pp=pp, m=m: e.mul(dst, pp, 0.125 if m < 6 else 1.0), tok)
            G.give(gk, ta)
            tq.append(ta)
        tq += tokmajor(A["w_fv"], 3, lambda k: H[:, k, :], 4, lambda c: vf[:, c, :])
        wk, wfl, wt = wload(A["w_fl"], 96)
        gk, b, free = G.take()
        pe.wait(free, wt)
        for c in range(4):
            for k in range(8):
                f = lambda e, c=c, k=k, b=b: e.matmul(ps[:, b, c * 12:c * 12 + 12], H[:, k, c * 128:c * 128 + 128], wfl[:, k * 12:k * 12 + 12],
                                                      start=(k == 0), stop=(k == 7))
                t = pe(f) if (c == 3 and k == 7) else pe.quiet(f)
        wring.give(wk, t)
        t = dve(lambda e, b=b: e.scalar_tensor_tensor(out=lf[:, :, :], in0=ps[:, b, 0:48].rearrange("p (c h) -> p c h", h=12), scalar=-1.0,
                                                      in1=rows[:, 144:156].unsqueeze(1).to_broadcast([P, 4, 12]), op0=ALU.mult, op1=ALU.subtract), t)
        G.give(gk, t)
        t_lf = softplus(flat(lf), l2[:, 0, :], l2[:, 1, :], l2[:, 2, :])
        pe.wait(t_lf)
        for c in range(4):
            for cc in range(c + 1):
                t = pe(lambda e, c=c, cc=cc: e.matmul(ps[0:12, 2, c * 128:(c + 1) * 128], lf[:, cc, :], C("trif") if cc == c else ones,
                                                      start=(cc == 0), stop=(cc == c)))
        t = dve(lambda e: e.tensor_copy(FT[:, :], ps[0:12, 2, :]), t)
        pe.wait(t, tq)
        Sr = Ring([2, 3])
        Tr = Ring([4, 5])
        Or = Ring([6, 7])
        pr = Ring([0, 1, 2, 3])
        ptr = Ring([0, 1])
        for h in range(12):
            hp = (h % 2) * 64
            qi, pt, ptf = ptr.take()
            pend = []
            for n in range(4):
                W = (n + 1) * 128
                sk, b, free = Sr.take()
                pe.wait(free)
                pe.quiet(lambda e, b=b, W=W, n=n, h=h, hp=hp: e.matmul(ps[:, b, 0:W], yf[hp:hp + 64, h // 2, n * 128:(n + 1) * 128], kf[hp:hp + 64, h // 2, 0:W],
                                                                       start=True, stop=False))
                pe.quiet(lambda e, b=b, W=W, h=h: e.matmul(ps[:, b, 0:W], ident[0:12, h:h + 1].to_broadcast([12, 128]), FT[:, 0:W], start=False, stop=False))
                t = pe(lambda e, b=b, n=n, W=W: e.matmul(ps[:, b, n * 128:W], maskb[:, 0, :], maskb[:, 2, :], start=False, stop=True))
                pk, pi, pfree = pr.take()
                ta = softmax(ps[:, b, 0:W], W, Pf[:, pi, 0:W], smf[:, pi, :], 1.0, None, t, pfree)
                Sr.give(sk, ta)
                pend.append((pk, pi, ta, W))
            tn = [normalise(Pf[:, pi, 0:W], smf[:, pi, :], None, ta) for pk, pi, ta, W in pend]
            t_pt = []
            for kb in range(4):
                tk, b, free = Tr.take()
                for n in range(kb, 4):
                    t = pe(lambda e, b=b, n=n, kb=kb, pi=pend[n][1]: e.transpose(ps[:, b, n * 128:(n + 1) * 128], Pf[:, pi, kb * 128:(kb + 1) * 128], ident), free, tn[n])
                cp = (lambda e, b=b, kb=kb, pt=pt: e.tensor_copy(PTf[:, pt, kb, kb * 128:L], ps[:, b, kb * 128:L])) if kb % 2 else \
                     (lambda e, b=b, kb=kb, pt=pt: e.copy(PTf[:, pt, kb, kb * 128:L], ps[:, b, kb * 128:L]))
                t2 = (dve if kb % 2 else act)(cp, t, ptf)
                Tr.give(tk, t2)
                t_pt.append(t2)
            for pk, pi, ta, W in pend:
                pr.give(pk, t)
            if h % 2 == 0:
                ok, ob, free = Or.take()
                pe.wait(free)
            pe.wait(t_pt)
            for kb in range(4):
                t = pe(lambda e, ob=ob, kb=kb, h=h, hp=hp, pt=pt: e.matmul(ps[hp:hp + 64, ob, kb * 128:L], vf[:, kb, h * 64:(h + 1) * 64], PTf[:, pt, kb, kb * 128:L],
                                                                          start=(kb == 0), stop=(kb == 3)))
            ptr.give(qi, t)
            if h % 2:
                (gk, pp, tok), = gemm(A["w_gf"], h // 2, 8, lambda k: H[:, k, :], [(0, L)])
                i_, s, sfree = sqr.take()
                s = s[:, 0:L]
                ta = act(lambda e, s=s, pp=pp: e.activation(s, pp, ACT.Tanh, scale=0.5), tok, sfree)
                t1 = dve(lambda e, s=s, pp=pp: e.scalar_tensor_tensor(out=s, in0=s, scalar=1.0, in1=pp, op0=ALU.add, op1=ALU.mult), ta)
                G.give(gk, t1)
                t1 = dve(lambda e, s=s, ob=ob, h=h: e.tensor_tensor(yf[:, h // 2, :], s, bank(ob), ALU.mult), t1, t)
                sqr.give(i_, t1)
                Or.give(ok, t1)
        fence()
        fx.close()

        me = ExitStack()
        hm = sb("hm", [P, 8, LC], c=me)
        mk = sb("mk", [P, 4, LC], c=me)
        mv = sb("mv", [P, 2, 512], c=me)
        Pq = sb("Pq", [P, 4, LC], c=me)
        PTm = sb("PTm", [P, 2, L], c=me)
        smm = sb("smm", [P, 4, 4], c=me)
        dm = Dma("s_mem")
        t_x = dm.start(pool, hm[:, :, :], A["memT"], fence())
        t_r = norm_T(lambda k: hm[:, k, :], 8, [(0, LC)], None, t_x)
        tl = []
        for k in range(8):
            tl.append(dve(lambda e, k=k: e.scalar_tensor_tensor(out=hm[:, k, :], in0=hm[:, k, :], scalar=V("gm", k), in1=rstd[:, 0:LC], op0=ALU.mult, op1=ALU.mult), t_r))
        pe.wait(tl)
        tq = []
        for m in range(4):
            (gk, pp, tok), = gemm(A["w_mk"], m, 8, lambda k: hm[:, k, :], [(0, LC)])
            ta = act(lambda e, pp=pp, m=m: e.copy(mk[:, m, :], pp), tok)
            G.give(gk, ta)
            (gk, pp, tok2), = gemm(A["w_qm"], m, 8, lambda k: H[:, k, :], [(0, L)])
            ta2 = act(lambda e, pp=pp, m=m: e.copy(ym[:, m, :], pp), tok2)
            G.give(gk, ta2)
            tq += [ta, ta2]
        tq += tokmajor(A["w_mv"], 2, lambda k: hm[:, k, :], 2, lambda c: mv[:, c, :])
        pe.wait(tq)
        MS = float(128) ** -0.5
        ptb = []
        for h in range(4):
            pend = []
            for n in range(4):
                sk, b, free = Sr.take()
                t = pe(lambda e, b=b, n=n, h=h: e.matmul(ps[:, b, 0:LC], ym[:, h, n * 128:(n + 1) * 128], mk[:, h, :], start=True, stop=True), free)
                pk, pi, pfree = pr.take()
                ta = softmax(ps[:, b, 0:LC], LC, Pq[:, pi, :], smm[:, pi, :], MS, None, t, pfree)
                Sr.give(sk, ta)
                pend.append((pk, pi, ta))
            tn = [normalise(Pq[:, pi, :], smm[:, pi, :], None, ta) for pk, pi, ta in pend]
            t_pt = []
            for kb in range(2):
                tk, b, free = Tr.take()
                for n in range(4):
                    t = pe(lambda e, b=b, n=n, kb=kb, pi=pend[n][1]: e.transpose(ps[:, b, n * 128:(n + 1) * 128], Pq[:, pi, kb * 128:(kb + 1) * 128], ident), free, tn[n])
                t2 = act(lambda e, b=b, kb=kb: e.copy(PTm[:, kb, :], bank(b)), t, ptb)
                Tr.give(tk, t2)
                t_pt.append(t2)
            for pk, pi, ta in pend:
                pr.give(pk, t)
            ok, ob, free = Or.take()
            pe.wait(free, t_pt)
            for kb in range(2):
                t = pe(lambda e, ob=ob, kb=kb, h=h: e.matmul(bank(ob), mv[:, kb, h * 128:(h + 1) * 128], PTm[:, kb, :], start=(kb == 0), stop=(kb == 1)))
            ptb = [t]
            (gk, pp, tok), = gemm(A["w_gm"], h, 8, lambda k: H[:, k, :], [(0, L)])
            i_, s, sfree = sqr.take()
            s = s[:, 0:L]
            ta = act(lambda e, s=s, pp=pp: e.activation(s, pp, ACT.Tanh, scale=0.5), tok, sfree)
            t1 = dve(lambda e, s=s, pp=pp: e.scalar_tensor_tensor(out=s, in0=s, scalar=1.0, in1=pp, op0=ALU.add, op1=ALU.mult), ta)
            G.give(gk, t1)
            t1 = dve(lambda e, s=s, ob=ob, h=h: e.tensor_tensor(ym[:, h, :], s, bank(ob), ALU.mult), t1, t)
            sqr.give(i_, t1)
            Or.give(ok, t1)
        fence()
        me.close()

        s5 = ExitStack()
        uT = sb("uT", [P, 6, L], c=s5)
        pk_ = sb("pk_", [P, 24, 24], c=s5)
        bre = sb("bre", [P, 24, 32], c=s5)
        bim = sb("bim", [P, 24, 32], c=s5)
        bb = sb("bb", [P, 3, 24, 32], c=s5)
        bl = sb("bl", [P, 2, 6, 128], c=s5)
        cl = sb("cl", [P, 2, 24, 32], c=s5)
        z32 = sb("z32", [P, 2, 24, 32], c=s5)
        q16 = sb("q16", [P, 2, 24, 16], c=s5)
        Tc = sb("Tc", [P, 2, 2, L], c=s5)
        Wk = sb("Wk", [P, 8, L], c=s5)
        wglu_toks = []
        d5 = Dma("s_s5")
        marks = fence()
        d5.start(pool, bre[:, :, :].rearrange("p a b -> p (a b)"), A["s5b"][0], marks)
        d5.start(pool, bim[:, :, :].rearrange("p a b -> p (a b)"), A["s5b"][1])
        d5.start(pool, cl[:, 0, :, :].rearrange("p a b -> p (a b)"), A["s5c"][0])
        t_d5 = d5.start(pool, cl[:, 1, :, :].rearrange("p a b -> p (a b)"), A["s5c"][1])
        K = lambda i: pk_[:, i, :]
        lr, li, ls = V("lre", 0, 24), V("lim", 0, 24), V("lstep", 0, 24)

        def chain(fns):
            for eng, f in fns:
                eng(f, dve.last(), act.last())

        PI2 = 2 * np.pi
        C1 = 6.28125
        C2 = float(np.float32(PI2 - C1).view(np.uint32) & np.uint32(0xFFFFF000)) if False else 0.0019350051879882812
        C3 = PI2 - C1 - C2
        MAGIC = 12582912.0
        TT = lambda o, a, b_, op: (dve, lambda e: e.tensor_tensor(o, a, b_, op))
        TS = lambda o, a, s1, s2, o1, o2=None: (dve, lambda e: e.tensor_scalar(o, a, s1, s2, o1, *([o2] if o2 is not None else [])))
        ST = lambda o, a, s, b_, o1, o2: (dve, lambda e: e.scalar_tensor_tensor(out=o, in0=a, scalar=s, in1=b_, op0=o1, op1=o2))
        AC = lambda o, a, f, sc=1.0: (act, lambda e: e.activation(o, a, f, scale=sc))
        chain([
            AC(K(0), ls, ACT.Exp),
            TT(K(1), lr, K(0), ALU.mult),
            AC(K(2), K(1), ACT.Exp),
            TT(K(3), li, K(0), ALU.mult),
            TS(K(4), K(3), 1.0 / PI2, MAGIC, ALU.mult, ALU.add),
            TS(K(4), K(4), MAGIC, None, ALU.subtract),
            ST(K(3), K(4), -C1, K(3), ALU.mult, ALU.add),
            ST(K(3), K(4), -C2, K(3), ALU.mult, ALU.add),
            ST(K(3), K(4), -C3, K(3), ALU.mult, ALU.add),
            TS(K(3), K(3), 3.1415925, -3.1415925, ALU.min, ALU.max),
            AC(K(5), K(3), ACT.Sin),
            AC(K(6), K(3), ACT.Sin, 0.5),
            TT(K(6), K(6), K(6), ALU.mult),
            TS(K(6), K(6), -2.0, 1.0, ALU.mult, ALU.add),
            TT(K(7), K(2), K(6), ALU.mult),
            TS(K(7), K(7), 1.0, None, ALU.subtract),
            TT(K(8), K(2), K(5), ALU.mult),
            TT(K(9), lr, lr, ALU.mult),
            TT(K(10), li, li, ALU.mult),
            TT(K(9), K(9), K(10), ALU.add),
            (dve, lambda e: e.reciprocal(K(9), K(9))),
            TT(K(10), K(7), lr, ALU.mult),
            TT(K(11), K(8), li, ALU.mult),
            TT(K(10), K(10), K(11), ALU.add),
            TT(K(10), K(10), K(9), ALU.mult),
            TT(K(11), K(8), lr, ALU.mult),
            TT(K(12), K(7), li, ALU.mult),
            TT(K(11), K(11), K(12), ALU.subtract),
            TT(K(11), K(11), K(9), ALU.mult),
        ])
        fre = K(10).unsqueeze(2).to_broadcast([P, 24, 32])
        fim = K(11).unsqueeze(2).to_broadcast([P, 24, 32])
        dve.wait(t_d5)
        act.wait(t_d5)
        chain([
            TT(bb[:, 0], bre[:, :, :], fre, ALU.mult), TT(bb[:, 2], bim[:, :, :], fim, ALU.mult),
            TT(bb[:, 0], bb[:, 0], bb[:, 2], ALU.subtract),
            TT(bb[:, 1], bim[:, :, :], fre, ALU.mult), TT(bb[:, 2], bre[:, :, :], fim, ALU.mult),
            TT(bb[:, 1], bb[:, 1], bb[:, 2], ALU.add),
            TS(cl[:, 1].rearrange("p a b -> p (a b)"), cl[:, 1].rearrange("p a b -> p (a b)"), -1.0, None, ALU.mult),
        ])
        for ri in (0, 1):
            for j in range(6):
                tk, b, free = Tr.take()
                t = pe(lambda e, b=b, ri=ri, j=j: e.transpose(ps[:, b, 0:128], bb[:, ri, 4 * j:4 * j + 4, :].rearrange("p a b -> p (a b)"), ident), free, dve.last())
                t = act(lambda e, b=b, ri=ri, j=j: e.copy(bl[:, ri, j, :], ps[:, b, 0:128]), t)
                Tr.give(tk, t)
        t_bl = t
        cre, cim = K(6), K(5)

        def cmul(o, a, z, n, tmp, sc):
            zr = z[0].unsqueeze(2).to_broadcast([P, 24, n])
            zi = z[1].unsqueeze(2).to_broadcast([P, 24, n])
            return [TT(tmp, a[1], zi, ALU.mult), TT(o[0], a[0], zr, ALU.mult), TT(o[0], o[0], tmp, ALU.subtract),
                    TT(tmp, a[0], zi, ALU.mult), TT(o[1], a[1], zr, ALU.mult), TT(o[1], o[1], tmp, ALU.add)]

        def csq(o, a):
            return [TT(K(14), a[1], a[1], ALU.mult), TT(K(15), a[0], a[0], ALU.mult), TT(K(15), K(15), K(14), ALU.subtract),
                    ST(K(16), a[0], 2.0, a[1], ALU.mult, ALU.mult),
                    (dve, lambda e: e.tensor_copy(o[0], K(15))), (dve, lambda e: e.tensor_copy(o[1], K(16)))]

        def powers(tab, z, n):
            seq = [(dve, lambda e: e.memset(tab[:, 0, :, 0], 1.0)), (dve, lambda e: e.memset(tab[:, 1, :, 0], 0.0)),
                   (dve, lambda e: e.tensor_copy(K(12), z[0])), (dve, lambda e: e.tensor_copy(K(13), z[1]))]
            k = 1
            while k < n:
                seq += cmul((tab[:, 0, :, k:2 * k], tab[:, 1, :, k:2 * k]), (tab[:, 0, :, 0:k], tab[:, 1, :, 0:k]), (K(12), K(13)), k, bb[:, 2, :, 0:k], None)
                seq += csq((K(12), K(13)), (K(12), K(13)))
                k *= 2
            return seq

        dve.wait(t_bl, pe.last())
        chain(powers(z32, (cre, cim), 32))
        chain(powers(q16, (K(12), K(13)), 16))
        t_pw = dve.last()
        pool.wait(t_pw)
        tu = []
        for m in range(6):
            (gk, pp, tok), = gemm(A["w_u"], m, 8, lambda k: H[:, k, :], [(0, L)])
            ta = act(lambda e, pp=pp, m=m: e.copy(uT[:, m, :], pp), tok)
            G.give(gk, ta)
            tu.append(ta)
        pe.wait(tu, t_bl)
        W_ = lambda i: Wk[:, i, :]
        Xr = Ring([2, 4])
        Yr = Ring([6, 7])
        tcr = Ring([0, 1])
        for s in range(24):
            j, i = s // 4, s % 4
            ck, cb_, cfree = tcr.take()
            tre, tim = Tc[:, cb_, 0, :], Tc[:, cb_, 1, :]
            v3 = lambda x: x.rearrange("p (a b) -> p a b", b=32)
            Pr, Pi = (z32[:, q, s, :].unsqueeze(1).to_broadcast([P, 16, 32]) for q in (0, 1))
            Qr, Qi = (q16[:, q, s, :].unsqueeze(2).to_broadcast([P, 16, 32]) for q in (0, 1))
            a1 = pool(lambda e, tre=tre, Pr=Pr, Qr=Qr: e.tensor_tensor(v3(tre), Pr, Qr, ALU.mult), cfree)
            a2 = pool(lambda e, Pi=Pi, Qi=Qi: e.tensor_tensor(v3(W_(6)), Pi, Qi, ALU.mult), pool.last())
            a3 = pool(lambda e, tre=tre: e.tensor_tensor(tre, tre, W_(6), ALU.subtract), a2)
            a1 = pool(lambda e, tim=tim, Pi=Pi, Qr=Qr: e.tensor_tensor(v3(tim), Pi, Qr, ALU.mult), a3)
            a2 = pool(lambda e, Pr=Pr, Qi=Qi: e.tensor_tensor(v3(W_(6)), Pr, Qi, ALU.mult), a1)
            t_tab = pool(lambda e, tim=tim: e.tensor_tensor(tim, tim, W_(6), ALU.add), a2)
            xk, b, free = Xr.take()
            for ri in (0, 1):
                t = pe(lambda e, b=b, ri=ri, i=i, j=j: e.matmul(bank(b + ri), bl[32 * i:32 * i + 32, ri, j, :], uT[32 * i:32 * i + 32, j, :],
                                                                start=True, stop=True), free)
            xr, xi = bank(b), bank(b + 1)
            d1 = dve(lambda e, xr=xr, tre=tre: e.tensor_tensor(W_(0), xr, tre, ALU.mult), t, t_tab, pe.last(), act.last())
            d2 = dve(lambda e, xi=xi, tim=tim: e.tensor_tensor(W_(1), xi, tim, ALU.mult))
            d3 = dve(lambda e, xi=xi, tre=tre: e.tensor_tensor(W_(2), xi, tre, ALU.mult))
            d4 = dve(lambda e, xr=xr, tim=tim: e.tensor_tensor(W_(3), xr, tim, ALU.mult))
            Xr.give(xk, d4)
            d2 = dve(lambda e: e.tensor_tensor(W_(0), W_(0), W_(1), ALU.add), d2)
            d4 = dve(lambda e: e.tensor_tensor(W_(2), W_(2), W_(3), ALU.subtract), d4)
            mag = K(2)[:, s:s + 1].to_broadcast([P, L])
            d1 = dve(lambda e, mag=mag: e.tensor_tensor_scan(W_(1), mag, W_(0), 0.0, ALU.mult, ALU.add), d4)
            d2 = dve(lambda e, mag=mag: e.tensor_tensor_scan(W_(3), mag, W_(2), 0.0, ALU.mult, ALU.add), d1)
            d5_ = dve(lambda e, tre=tre: e.tensor_tensor(W_(4), W_(1), tre, ALU.mult), d2, pe.last())
            d6 = dve(lambda e, tim=tim: e.tensor_tensor(W_(0), W_(3), tim, ALU.mult), d5_)
            p1 = pool(lambda e, tim=tim: e.tensor_tensor(W_(5), W_(1), tim, ALU.mult), d2, pe.last())
            p2 = pool(lambda e, tre=tre: e.tensor_tensor(W_(7), W_(3), tre, ALU.mult), p1)
            d7 = dve(lambda e: e.tensor_tensor(W_(4), W_(4), W_(0), ALU.subtract), d6)
            p3 = pool(lambda e: e.tensor_tensor(W_(5), W_(5), W_(7), ALU.add), p2)
            tcr.give(ck, d6, p2)
            if i == 0:
                yk, yb, yfree = Yr.take()
                pe.wait(yfree)
            pe.quiet(lambda e, yb=yb, i=i, s=s: e.matmul(ps[32 * i:32 * i + 32, yb, :], cl[:, 0, s, :], W_(4), start=True, stop=False, tile_position=(0, 32 * i)), d7)
            t = pe(lambda e, yb=yb, i=i, s=s: e.matmul(ps[32 * i:32 * i + 32, yb, :], cl[:, 1, s, :], W_(5), start=False, stop=True, tile_position=(0, 32 * i)), p3)
            dve.wait(p3)
            if i == 3:
                y = ysv[:, j, :]
                t = dve(lambda e, y=y, j=j, yb=yb: e.scalar_tensor_tensor(out=y, in0=uT[:, j, :], scalar=V("s5d", j), in1=bank(yb), op0=ALU.mult, op1=ALU.add), t)
                Yr.give(yk, t)
                i_, q, sfree = sqr.take()
                q = q[:, 0:L]
                ta = act(lambda e, q=q, y=y: e.activation(q, y, ACT.Square), t, sfree)
                t = dve(lambda e, q=q: e.tensor_scalar(q, q, 0.044715, 1.0, ALU.mult, ALU.add), ta)
                t = dve(lambda e, q=q, y=y: e.tensor_tensor(q, q, y, ALU.mult), t)
                ta = act(lambda e, q=q: e.activation(q, q, ACT.Tanh, scale=0.7978845608028654), t)
                t = dve(lambda e, q=q, y=y: e.scalar_tensor_tensor(out=y, in0=q, scalar=1.0, in1=y, op0=ALU.add, op1=ALU.mult), ta)
                sqr.give(i_, t)
        t_y5 = dve.last()
        sg5 = Wk
        hb = dve(lambda e: e.tensor_scalar(V("bglu", 0, 6), V("bglu", 0, 6), 0.5, None, ALU.mult))
        tg = []
        for m in range(6):
            (gk, pp, tok), = gemm(A["w_glu"], m, 6, lambda k: ysv[:, k, :], [(0, L)], t_y5)
            ta = act(lambda e, pp=pp, m=m: e.activation(sg5[:, m, :], pp, ACT.Tanh, scale=0.25, bias=V("bglu", m)), tok, hb, t_y5)
            G.give(gk, ta)
            (gk, pp, tok), = gemm(A["w_gs"], m, 8, lambda k: H[:, k, :], [(0, L)])
            i_, q, sfree = sqr.take()
            q = q[:, 0:L]
            ta = act(lambda e, q=q, pp=pp: e.activation(q, pp, ACT.Tanh, scale=0.5), tok, sfree)
            t = dve(lambda e, q=q, pp=pp: e.scalar_tensor_tensor(out=q, in0=q, scalar=1.0, in1=pp, op0=ALU.add, op1=ALU.mult), ta)
            G.give(gk, t)
            t = dve(lambda e, q=q, m=m: e.scalar_tensor_tensor(out=sg5[:, m, :], in0=sg5[:, m, :], scalar=1.0, in1=q, op0=ALU.add, op1=ALU.mult), t, ta)
            sqr.give(i_, t)
            tg.append(t)
        t5 = [dve(lambda e, m=m: e.tensor_tensor(ysv[:, m, :], ysv[:, m, :], sg5[:, m, :], ALU.mult), tg, pe.last()) for m in range(6)]
        fence()
        s5.close()

        fin = ExitStack()
        mrg = sb("mrg2", [P, 8, L], c=fin)
        gt = sb("gt2", [P, 6, L], c=fin)
        gr = Ring(list(range(6)))
        hb = dve(lambda e: e.tensor_scalar(V("bmerge", 0, 24), V("bmerge", 0, 24), 0.5, None, ALU.mult))
        t_m = []
        for m in range(8):
            tt = []
            for q, (wd, KT, src) in enumerate((("w_pf", 6, yf), ("w_ps", 6, ysv), ("w_pm", 4, ym))):
                (gk, pp, tok), = gemm(A["w_gl"], q * 8 + m, 8, lambda k: H[:, k, :], [(0, L)])
                ik, i_, free = gr.take()
                ta = act(lambda e, i_=i_, pp=pp, q=q, m=m: e.activation(gt[:, i_, :], pp, ACT.Tanh, scale=0.5, bias=V("bmerge", q * 8 + m)), tok, free, hb)
                G.give(gk, ta)
                (gk, pp, tok), = gemm(A[wd], m, KT, lambda k, src=src: src[:, k, :], [(0, L)], t5)
                t = dve(lambda e, i_=i_, pp=pp: e.scalar_tensor_tensor(out=gt[:, i_, :], in0=gt[:, i_, :], scalar=1.0, in1=pp, op0=ALU.add, op1=ALU.mult), tok, ta)
                G.give(gk, t)
                tt.append((ik, i_, t))
            t = pool(lambda e, a=tt[0][1], b_=tt[2][1]: e.tensor_tensor(gt[:, a, :], gt[:, a, :], gt[:, b_, :], ALU.add), tt[0][2], tt[2][2])
            t = dve(lambda e, a=tt[0][1], b_=tt[1][1], m=m: e.scalar_tensor_tensor(out=mrg[:, m, :], in0=gt[:, b_, :], scalar=0.25, in1=gt[:, a, :], op0=ALU.mult, op1=ALU.add), t)
            for ik, _, _ in tt:
                gr.give(ik, t)
            t_m.append(t)
        tx_ = []
        for m in range(8):
            (gk, pp, tok), = gemm(A["w_out2"], m, 8, lambda k: mrg[:, k, :], [(0, L)], t_m)
            t = dve(lambda e, m=m, pp=pp: e.scalar_tensor_tensor(out=X[:, m, :], in0=pp, scalar=0.25, in1=X[:, m, :], op0=ALU.mult, op1=ALU.add), tok)
            G.give(gk, t)
            tx_.append(t)
        t_r = norm_T(lambda k: X[:, k, :], 8, [(0, L)], None, tx_)
        dout = Dma("s_out")
        for k in range(8):
            t = dve(lambda e, k=k: e.scalar_tensor_tensor(out=X[:, k, :], in0=X[:, k, :], scalar=V("gf", k), in1=rstd[:, 0:L], op0=ALU.mult, op1=ALU.mult), t_r)
            t_out = dout.start(sp, out[:, k, :], X[:, k, :], t)
        sp.wait(t_out)
        fin.close()



def kernel(**inputs):
    import numpy as _np
    import concourse.bacc as _bacc
    from concourse import mybir as _mybir
    from concourse.bass_utils import run_bass_kernel_spmd as _run

    I = {k: _np.asarray(v) for k, v in inputs.items()}
    arr = {}

    def blocks(w):
        k, n = w.shape
        return _np.ascontiguousarray(w.reshape(k // 128, 128, n // 128, 128).transpose(2, 1, 0, 3).reshape(n // 128, 128, k))

    def wide(w):
        k, n = w.shape
        return _np.ascontiguousarray(w.reshape(2, 4, 128, n // 256, 256).transpose(3, 0, 2, 1, 4).reshape(n // 256, 2, 128, 1024))

    def feat(x):
        t, n = x.shape
        return _np.ascontiguousarray(x.T.reshape(n // 128, 128, t).transpose(1, 0, 2))

    def cols(v):
        return v.reshape(-1, 128).T

    arr["xT"] = feat(I["x"][0])
    arr["ctxT"] = feat(I["ctx"][0])
    arr["memT"] = feat(I["mem_2"][0])
    arr["w_mod"] = blocks(I["w_mod"][0])
    w = I["w_in"][0]
    arr["w_z"] = blocks(w[:, 0:2048])
    arr["w_xbc"] = blocks(w[:, 2048:5120])
    arr["w_dt"] = _np.ascontiguousarray(w[:, 5120:5184].reshape(8, 128, 64).transpose(1, 0, 2).reshape(128, 512))
    arr["w_qk"] = blocks(w[:, 5184:6464])
    arr["w_v"] = wide(w[:, 6464:6720])
    arr["w_g"] = blocks(w[:, 6720:8768])
    arr["w_os"] = blocks(I["w_o_ssd"][0])
    arr["w_oa"] = blocks(I["w_o_att"][0])
    arr["w_out"] = blocks(I["w_out"][0])
    arr["w_up"] = blocks(I["w_up"][0])
    arr["w_down"] = blocks(I["w_down"][0])
    w = I["w_in_2"][0]
    arr["w_fqk"] = blocks(w[:, 0:1536])
    arr["w_fv"] = wide(w[:, 1536:2304])
    arr["w_fl"] = _np.ascontiguousarray(w[:, 2304:2316].reshape(8, 128, 12).transpose(1, 0, 2).reshape(128, 96))
    arr["w_gf"] = blocks(w[:, 2316:3084])
    arr["w_u"] = blocks(w[:, 3084:3852])
    arr["w_gs"] = blocks(w[:, 3852:4620])
    arr["w_qm"] = blocks(w[:, 4620:5132])
    arr["w_gm"] = blocks(w[:, 5132:5644])
    arr["w_gl"] = blocks(w[:, 5644:8716])
    w = I["w_mem_kv_2"][0]
    arr["w_mk"] = blocks(w[:, 0:512])
    arr["w_mv"] = wide(w[:, 512:1024])
    arr["w_glu"] = blocks(I["w_glu_2"][0])
    arr["w_pf"] = blocks(I["w_proj_fox_2"][0])
    arr["w_ps"] = blocks(I["w_proj_s5_2"][0])
    arr["w_pm"] = blocks(I["w_proj_mem_2"][0])
    arr["w_out2"] = blocks(I["w_out_2"][0])
    cw, fw = I["ssd_conv_w"][0], I["ffn_conv_w"][0]
    cc = _np.stack([I["c"][0], I["c_ctx"]], axis=-1)
    vec = {
        "bmod": cols(I["b_mod"][0]), "g1": cols(I["norm1_g"][0]), "g2": cols(I["norm2_g"][0]),
        "cw0": cols(cw[0]), "cw1": cols(cw[1]), "cw2": cols(cw[2]), "cb": cols(I["ssd_conv_b"][0]),
        "sg": cols(I["ssd_norm_g"][0]), "fw0": cols(fw[0]), "fw1": cols(fw[1]), "fw2": cols(fw[2]),
        "fb": cols(I["ffn_conv_b"][0]), "fg": cols(I["final_g"]), "gn": cols(I["g_norm_2"][0]),
        "gm": cols(I["g_mem_norm_2"][0]), "gf": cols(I["g_final_2"]), "bmerge": cols(I["b_merge_2"][0]),
        "bglu": cols(I["b_glu_2"][0]), "s5d": cols(I["s5_d_2"][0]), "lre": cols(I["lam_re_2"][0]),
        "lim": cols(I["lam_im_2"][0]), "lstep": cols(_np.repeat(I["log_step_2"][0], 64)),
        "dsk": cols(_np.repeat(I["ssd_d"][0], 64)),
        "c": cc.reshape(8, 128, 2).transpose(1, 0, 2).reshape(128, 16),
    }
    arr["vecs"] = _np.ascontiguousarray(_np.concatenate([vec[n] for n, _ in VECS], axis=1))
    r = _np.concatenate([I["ssd_dt_bias"][0].reshape(-1), I["ssd_a_log"][0].reshape(-1), I["att_sink"][0], I["b_forget_2"][0]])
    arr["rows"] = _np.ascontiguousarray(_np.broadcast_to(r, (128, r.size)))
    sb_ = _np.zeros((2, 2, 64, 24, 2, 16), _np.float32)
    sc_ = _np.zeros((2, 2, 64, 24, 2, 16), _np.float32)
    for q, (bn, cn) in enumerate((("s5_b_re_2", "s5_c_re_2"), ("s5_b_im_2", "s5_c_im_2"))):
        b4 = I[bn][0].reshape(24, 2, 64, 16)
        c4 = I[cn][0].reshape(24, 2, 16, 64)
        for par in (0, 1):
            sb_[q, par, :, :, par, :] = b4[:, par].transpose(1, 0, 2)
            sc_[q, par, :, :, par, :] = c4[:, par].transpose(2, 0, 1)
    arr["s5b"] = sb_.reshape(2, 128, 768)
    arr["s5c"] = sc_.reshape(2, 128, 768)
    i = _np.arange(128)
    a, b = i[:, None], i[None, :]
    f = _np.float32
    inv = (f(10000.0) ** (-_np.arange(0, 32, 2, dtype=f) / f(32))).astype(f)
    t = _np.arange(512)
    dd = i % 64
    pos = _np.where((dd // 32 == 0)[:, None], (t // 64)[None], (t % 64)[None]).astype(f)
    ang = (pos * inv[dd % 16][:, None]).astype(f).astype(_np.float64)
    sgn = _np.where(dd % 32 < 16, -1.0, 1.0)[:, None]
    arr["consts"] = _np.concatenate([
        a == b, a <= b, a >= b, a == (b ^ 16), _np.where(b >= a, 0.0, -1e30), _np.where(b <= a, 0.0, -1e30),
        _np.ones((128, 128)), _np.cos(ang), sgn * _np.sin(ang)], axis=1).astype(f)

    nc = _bacc.Bacc("TRN2", target_bir_lowering=False, num_devices=1)
    A = {}
    for name, x in arr.items():
        A[name] = nc.dram_tensor(f"in_{name}", x.shape, _mybir.dt.float32, kind="ExternalInput").ap()
    A["csd"] = nc.dram_tensor("csd", (2, 32, 512), _mybir.dt.float32, kind="Internal").ap()
    A["xsc"] = nc.dram_tensor("xsc", (128, 8, 512), _mybir.dt.float32, kind="Internal").ap()
    out = nc.dram_tensor("out_0", (128, 8, 512), _mybir.dt.float32, kind="ExternalOutput").ap()
    fused_blocks(nc, A, out)
    r = _run(nc, [{f"in_{k}": v for k, v in arr.items()}], core_ids=[0])
    y = r.results[0]["out_0"]
    return _np.ascontiguousarray(y.transpose(2, 1, 0).reshape(1, 512, 1024))
```

```python
from contextlib import ExitStack

import numpy as np

import concourse.bass as bass
from concourse import mybir

ALU = mybir.AluOpType
ACT = mybir.ActivationFunctionType
F32 = mybir.dt.float32
F32R = mybir.dt.float32r
BF16 = mybir.dt.bfloat16
AXX = mybir.AxisListType.X

P = 128
EPS = 1e-6
L = 512
LC = 256
LT = L + LC
LOOK = 2

VECS = [("bmod", 48), ("g1", 8), ("g2", 8), ("cw0", 24), ("cw1", 24), ("cw2", 24), ("cb", 24),
        ("sg", 16), ("fw0", 44), ("fw1", 44), ("fw2", 44), ("fb", 44), ("fg", 8), ("gn", 8),
        ("gm", 8), ("gf", 8), ("bmerge", 24), ("bglu", 6), ("s5d", 6), ("lre", 24), ("lim", 24),
        ("lstep", 24), ("dsk", 16), ("c", 16)]
VOFF = {}
_o = 0
for _n, _k in VECS:
    VOFF[_n] = (_o, _k)
    _o += _k
NVEC = _o
ROWS = [("dtb", 64), ("alog", 64), ("sink", 16), ("bfor", 12)]
CONSTS = [("ident", 128), ("trif", 128), ("trib", 128), ("perm", 128), ("ml", 128), ("mr", 128),
          ("ones", 128), ("cos", 512), ("sin", 512)]


class Engine:

    def __init__(self, eng, sem):
        self.eng, self.sem, self.n, self.seen = eng, sem, 0, {}

    def wait(self, *toks):
        for t in toks:
            if t is None:
                continue
            if isinstance(t, (list, tuple)) and not (len(t) == 2 and isinstance(t[1], int)):
                self.wait(*t)
                continue
            s, v = t
            if self.seen.get(id(s), 0) < v:
                self.seen[id(s)] = v
                self.eng.wait_ge(s, v)

    def __call__(self, fn, *toks):
        self.wait(*toks)
        self.n += 1
        fn(self.eng).then_inc(self.sem, 1)
        return (self.sem, self.n)

    def quiet(self, fn, *toks):
        self.wait(*toks)
        fn(self.eng)

    def last(self):
        return (self.sem, self.n)


class Ring:

    def __init__(self, slots):
        self.slots, self.free, self.i = slots, [[] for _ in slots], 0

    def take(self):
        k = self.i % len(self.slots)
        self.i += 1
        return k, self.slots[k], self.free[k]

    def give(self, k, *toks):
        self.free[k] = list(toks)


class Weights:

    def __init__(self, order, src, sp, act, raw, dmas, hi, lo):
        self.order, self.src, self.sp, self.act = order, src, sp, act
        self.raw, self.dmas, self.hi, self.lo = raw, dmas, hi, lo
        self.asked, self.made, self.at = [], {}, 0
        self.sub = None

    def emit(self, q):
        key, n, split = self.order[q]
        k, ap, free = self.raw.take()
        t = self.dmas[k].start(self.sp, ap[:, 0:n], self.src(key), free)
        if not split:
            self.made[q] = (self.raw, k, ap[:, 0:n], None, t)
            return
        j, (h, l), hfree = self.hi.take()
        w = ap[:, 0:n]
        th = self.act(lambda e: e.copy(h[:, 0:n], w), t, hfree)
        tl = self.sub(lambda e: e.tensor_tensor(l[:, 0:n], w, h[:, 0:n].bitcast(F32), ALU.subtract), t, th, hfree)
        self.raw.give(k, th, tl)
        self.made[q] = (self.hi, j, h[:, 0:n], l[:, 0:n], (th, tl))

    def next(self, key, n, split, held=0):
        self.asked.append((key, n, split))
        q = self.at
        self.at += 1
        if q >= len(self.order):
            self.order.append((key, n, split))
        assert self.order[q] == (key, n, split)
        look = LOOK - held if split else 1
        for p in range(q, min(q + look, len(self.order) - 1) + 1):
            if p not in self.made:
                self.emit(p)
        return self.made[q]


def weave(*tasks):
    live = [[0.0, i, t] for i, t in enumerate(tasks)]
    while live:
        live.sort(key=lambda x: (x[0], x[1]))
        x = live[0]
        try:
            x[0] += next(x[2])
        except StopIteration:
            live.remove(x)


def chain_of(*gens):
    for g in gens:
        yield from g


def run(gen):
    for _ in gen:
        pass


def fused_blocks(nc, A, out, order):
    ctx = ExitStack()
    with ctx:
        def at(name, shape, kb, dt=F32):
            return nc.alloc_sbuf_tensor_at(name, shape, dt, offset=384 + int(kb * 1024))

        cursor = [40 * 1024]

        def small_at(name, shape, dt=F32):
            n = int(np.prod(shape[1:])) * (2 if dt == BF16 else 4)
            o = cursor[0]
            cursor[0] += (n + 31) // 32 * 32
            assert cursor[0] <= 50 * 1024
            return nc.alloc_sbuf_tensor_at(name, shape, dt, offset=384 + o)

        def sem(name):
            return ctx.enter_context(nc.semaphore(name))

        ps = ctx.enter_context(nc.psum_tensor("ps", [P, 8, 512], F32))

        def bank(b):
            return ps[:, b, :]

        pe = Engine(nc.tensor, sem("s_pe"))
        dve = Engine(nc.vector, sem("s_dve"))
        act = Engine(nc.scalar, sem("s_act"))
        pool = Engine(nc.gpsimd, sem("s_pool"))
        sp = Engine(nc.sync, sem("s_sp"))

        class Dma:

            def __init__(self, name):
                self.sem, self.n = sem(name), 0

            def start(self, eng, dst, src, *toks):
                eng.wait(*toks)
                self.n += 16
                eng.eng.dma_start(dst, src).then_inc(self.sem, 16)
                return (self.sem, self.n)

        def marks():
            return [e.last() for e in (pe, dve, act, pool)]

        def fence():
            m = marks()
            for e in (pe, dve, act, pool):
                e.wait(m)
            return m

        def banks(*b):
            r = Ring(list(b))
            m = marks()
            for i in range(len(b)):
                r.give(i, m)
            return r

        raww = at("raww", [P, 4, 1024], 0)
        whi = at("whi", [P, 3, 1024], 16, F32R)
        wlo = at("wlo", [P, 3, 1024], 28, F32R)

        def wsrc(key):
            name, m, a, b = key
            return A[name][m, :, a:b] if len(A[name].shape) == 3 else A[name][:, a:b] if len(A[name].shape) == 2 else A[name][m[0], m[1], :, a:b]

        W = Weights(order, wsrc, sp, act, Ring([raww[:, i, :] for i in range(4)]), [Dma(f"s_w{i}") for i in range(4)],
                    Ring([(whi[:, i, :], wlo[:, i, :]) for i in range(3)]), None)
        W.sub = pool

        G = banks(0, 1, 2)

        class Pair:

            def __init__(self, hi, lo):
                self.hi, self.lo = hi, lo

            def put(self, k, v, t0, t1, *toks, hi=None, lo=None):
                h = (hi or act)(lambda e: (e.copy if e is nc.scalar else e.tensor_copy)(self.hi(k)[:, t0:t1], v), *toks)
                l = (lo or pool)(lambda e: e.tensor_tensor(self.lo(k)[:, t0:t1], v, self.hi(k)[:, t0:t1].bitcast(F32), ALU.subtract), h, *toks)
                return [h, l]

        def pair(name, n, T, kb, kb2=None):
            h = at(name + "_h", [P, n, T], kb, F32R)
            l = at(name + "_l", [P, n, T], kb + n * T / 256 if kb2 is None else kb2, F32R)
            return Pair(lambda k: h[:, k, :], lambda k: l[:, k, :]), h, l

        def gemm(wd, m, KT, rhs, ranges, *waits):
            res = []
            pe.wait(*waits)
            for (t0, t1) in ranges:
                gk, b, free = G.take()
                pe.wait(free)
                res.append((gk, ps[:, b, 0:t1 - t0]))
            for k0 in range(0, KT, 8):
                kk = min(8, KT - k0)
                ring, slot, wh, wl, tw = W.next((wd, m, k0 * 128, (k0 + kk) * 128), kk * 128, True)
                pe.wait(tw)
                for (t0, t1), (gk, o) in zip(ranges, res):
                    for k in range(k0, k0 + kk):
                        c = slice((k - k0) * 128, (k - k0 + 1) * 128)
                        xh, xl = rhs.hi(k)[:, t0:t1], rhs.lo(k)[:, t0:t1]
                        pe.quiet(lambda e: e.matmul(o, wh[:, c], xh, start=(k == 0), stop=False))
                        pe.quiet(lambda e: e.matmul(o, wh[:, c], xl, start=False, stop=False))
                        f = lambda e: e.matmul(o, wl[:, c], xh, start=False, stop=(k == KT - 1))
                        if k == k0 + kk - 1:
                            tok = pe(f)
                        else:
                            pe.quiet(f)
                ring.give(slot, tok)
            return [(gk, o, tok) for gk, o in res]

        vc = small_at("vc", [P, NVEC])
        rows = small_at("rows", [P, 156])
        cst = small_at("cst", [P, 896])
        maskb = small_at("maskb", [P, 3, 128], BF16)
        cs_ = small_at("cs_", [P, 16])
        tmp16 = small_at("tmp16", [P, 16])
        modS = small_at("modS", [P, 48, 2])
        A1 = small_at("A1", [P, 8, 2])
        A2 = small_at("A2", [P, 8])
        pk_ = small_at("pk_", [P, 17, 24])
        dc = Dma("s_c")
        dx = Dma("s_x")
        t_vc = dc.start(sp, vc[:, :], A["vecs"])

        def V(name, i=0, n=None):
            o, k = VOFF[name]
            return vc[:, o + i:o + i + (n or 1)]

        def C(name):
            return cst[:, ["ident", "trif", "trib", "perm", "ml", "mr", "ones"].index(name) * 128:][:, 0:128]

        ident, ones = C("ident"), C("ones")

        acc = at("acc", [P, L], 50)
        rstd = at("rstd", [P, L], 52)
        sq = at("sq", [P, 2, L], 54)
        sqr = Ring([sq[:, 0, :], sq[:, 1, :]])

        def norm_sum(X, KT, T, acc, sqr, *in_toks):
            tacc = None
            for k in range(KT):
                i, s, free = sqr.take()
                ta = act(lambda e: e.activation(s[:, 0:T], X(k)[:, 0:T], ACT.Square), free, in_toks)
                if k == 0:
                    tacc = dve(lambda e: e.tensor_copy(acc[:, 0:T], s[:, 0:T]), ta)
                else:
                    tacc = dve(lambda e: e.tensor_tensor(acc[:, 0:T], acc[:, 0:T], s[:, 0:T], ALU.add), ta, tacc)
                sqr.give(i, tacc)
            return tacc

        def norm_rstd(ranges, tacc, inv, acc, rstd, tmps):
            tr = []
            for (t0, t1) in ranges:
                gk, b, free = G.take()
                tm = pe(lambda e: e.matmul(ps[:, b, 0:t1 - t0], ones, acc[:, t0:t1], start=True, stop=True), free, tacc)
                t = dve(lambda e: e.tensor_scalar(rstd[:, t0:t1], ps[:, b, 0:t1 - t0], inv, EPS, ALU.mult, ALU.add), tm)
                G.give(gk, t)
                v, r, w = rstd[:, t0:t1], tmps[0][:, t0:t1], tmps[1][:, t0:t1]
                ta = act(lambda e: e.activation(r, v, ACT.Sqrt), t)
                t = dve(lambda e: e.reciprocal(r, r), ta)
                t = dve(lambda e: e.tensor_tensor(w, r, r, ALU.mult), t)
                t = dve(lambda e: e.tensor_tensor(w, w, v, ALU.mult), t)
                t = dve(lambda e: e.tensor_scalar(w, w, -0.5, 1.5, ALU.mult, ALU.add), t)
                t = dve(lambda e: e.tensor_tensor(v, r, w, ALU.mult), t)
                tr.append(t)
            return tr

        def norm_T(X, KT, T, *in_toks):
            t = norm_sum(X, KT, T, acc, sqr, *in_toks)
            tr = norm_rstd([(0, T)], t, 1.0 / (KT * 128), acc, rstd, (sq[:, 0, :], sq[:, 1, :]))
            sqr.give(0, tr)
            sqr.give(1, tr)
            return tr

        HP, hh, hl = pair("hT", 8, LT, 58)
        xin = at("xin", [P, 8, LT], 106)
        acc1 = at("acc1", [P, LT], 136)
        rstd1 = at("rstd1", [P, LT], 139)
        sq1 = at("sq1", [P, 2, LT], 142)
        hv = at("hv", [P, 2, LT], 148)
        dx.start(sp, xin[:, :, 0:L], A["xT"])
        t_hx = dx.start(sp, xin[:, :, L:LT], A["ctxT"])
        dc.start(sp, rows[:, :], A["rows"])
        t_cst = dc.start(sp, cst[:, :], A["consts"][:, 0:896])
        for e in (pe, dve, act, pool):
            e.wait(t_cst)
        dve(lambda e: e.tensor_copy(maskb[:, 0, :], ident))
        t_mb = dve(lambda e: e.tensor_copy(maskb[:, 1:3, :].rearrange("p a b -> p (a b)"), cst[:, 512:768]))
        pe.wait(t_mb)
        ta = act(lambda e: e.activation(tmp16[:, :], V("c", 0, 16), ACT.Tanh, scale=0.5))
        t = dve(lambda e: e.scalar_tensor_tensor(out=cs_[:, :], in0=tmp16[:, :], scalar=1.0, in1=V("c", 0, 16), op0=ALU.add, op1=ALU.mult), ta)
        t_c = dve(lambda e: e.tensor_scalar(cs_[:, :], cs_[:, :], 0.5, None, ALU.mult), t)
        for nm in ("cw0", "cw1", "cw2", "cb"):
            dve(lambda e: e.tensor_scalar(V(nm, 0, 24), V(nm, 0, 24), 0.5, None, ALU.mult))
        for nm in ("fw0", "fw1", "fw2", "fb"):
            dve(lambda e: e.tensor_scalar(V(nm, 0, 22), V(nm, 0, 22), 0.5, None, ALU.mult))
        t_vh = dve(lambda e: e.tensor_scalar(V("bmerge", 0, 24), V("bmerge", 0, 24), 0.5, None, ALU.mult))
        t_vh = dve(lambda e: e.tensor_scalar(V("bglu", 0, 6), V("bglu", 0, 6), 0.5, None, ALU.mult))
        act.wait(t_vh)

        def mod_blocks(m0, m1, per=8):
            for ma in range(m0, m1, per):
                gk, b, free = G.take()
                pe.wait(free, t_c)
                for m in range(ma, ma + per):
                    ring, slot, w, _, tw = W.next(("w_mod", m, 0, 1024), 1024, False)
                    pe.wait(tw)
                    for k in range(8):
                        f = lambda e: e.matmul(ps[:, b, 2 * (m - ma):2 * (m - ma) + 2], w[:, k * 128:(k + 1) * 128],
                                               cs_[:, 2 * k:2 * k + 2], start=(k == 0), stop=(k == 7))
                        t = pe(f) if k == 7 else pe.quiet(f)
                    ring.give(slot, t)
                    if m < ma + per - 1:
                        yield 1.0
                o = VOFF["bmod"][0]
                t = dve(lambda e: e.tensor_tensor(modS[:, ma:ma + per, :], ps[:, b, 0:2 * per].rearrange("p (m s) -> p m s", s=2),
                                                  vc[:, o + ma:o + ma + per].unsqueeze(2).to_broadcast([P, per, 2]), ALU.add), t)
                G.give(gk, t)
                t_mod[0] = t
                yield 1.0

        t_mod = [None]
        t = norm_sum(lambda k: xin[:, k, :], 8, LT, acc1, Ring([sq1[:, 0, :], sq1[:, 1, :]]), t_hx)
        t_r = norm_rstd([(0, L), (L, LT)], t, 1.0 / 1024, acc1, rstd1, (sq1[:, 0, :], sq1[:, 1, :]))
        run(mod_blocks(0, 16))
        t = dve(lambda e: e.tensor_scalar(A1[:, :, :], modS[:, 8:16, :], 1.0, None, ALU.add), t_mod[0])
        t_A1 = dve(lambda e: e.tensor_tensor(A1[:, :, :], A1[:, :, :], V("g1", 0, 8).unsqueeze(2).to_broadcast([P, 8, 2]), ALU.mult), t)
        hvr = Ring([hv[:, 0, :], hv[:, 1, :]])
        t_h = []
        for k in range(8):
            i, v, free = hvr.take()
            t = dve(lambda e: e.tensor_tensor(v, xin[:, k, :], rstd1[:, :], ALU.mult), t_r, free)
            dve(lambda e: e.tensor_scalar(v[:, 0:L], v[:, 0:L], A1[:, k, 0:1], modS[:, k, 0:1], ALU.mult, ALU.add), t, t_A1)
            t = dve(lambda e: e.tensor_scalar(v[:, L:LT], v[:, L:LT], A1[:, k, 1:2], modS[:, k, 1:2], ALU.mult, ALU.add))
            tt = HP.put(k, v, 0, LT, t, lo=dve)
            hvr.give(i, tt)
            t_h.append(tt)
        pe.wait(t_h)

        def softplus(x, u, w, n):
            t = dve(lambda e: e.scalar_tensor_tensor(out=u, in0=x, scalar=-1.0, in1=x, op0=ALU.mult, op1=ALU.max), dve.last())
            t = act(lambda e: e.activation(u, u, ACT.Exp, scale=-1.0), t)
            t1 = dve(lambda e: e.tensor_scalar(w, u, 1.0, None, ALU.add), t)
            ta = act(lambda e: e.activation(n, w, ACT.Ln), t1)
            t = dve(lambda e: e.scalar_tensor_tensor(out=u, in0=w, scalar=-1.0, in1=u, op0=ALU.add, op1=ALU.subtract), t1)
            t = dve(lambda e: e.reciprocal(w, w), t, ta)
            t = dve(lambda e: e.scalar_tensor_tensor(out=u, in0=u, scalar=-1.0, in1=w, op0=ALU.mult, op1=ALU.mult), t)
            t = dve(lambda e: e.tensor_tensor(u, u, n, ALU.add), t, ta)
            return dve(lambda e: e.scalar_tensor_tensor(out=x, in0=x, scalar=0.0, in1=u, op0=ALU.max, op1=ALU.add), t)

        xsl = at("xsl", [P, 2, 4, L], 106)
        xsc_ = at("xsc_", [P, 4, LC], 122)
        BTs = at("BTs", [P, 2, LT], 126)
        CTs = at("CTs", [P, 2, L], 132)
        xtok = at("xtok", [P, 6, 512], 136)
        Btok = at("Btok", [P, 6, 128], 148)
        st = at("st", [P, 2, 4, 512], 151)
        st0 = at("st0", [P, 512], 167)
        stt_ = at("stt_", [P, 512], 169)
        csbc = at("csbc", [P, 3, 8, 128], 171)
        cbm = at("cbm", [P, 2, 128], 183)
        Ew = at("Ew", [P, 2, 8, 128], 184)
        Cs = at("Cs", [P, 2, 8, 128], 192)
        xw = at("xw", [P, 2, 512], 200)
        yg = at("yg", [P, 4, L], 204)
        dt_ = at("dt_", [P, 6, 64], 212)
        la = at("la", [P, 6, 64], 213.5)
        csm = at("csm", [P, 6, 64], 215)
        wdec = at("wdec", [P, 6, 64], 216.5)
        etot = at("etot", [P, 6, 64], 218)
        ysp = at("ysp", [P, 2, L], 219.5, F32R)
        csT = at("csT", [64, L], 167)
        csd = A["csd"]

        flat = lambda x: x[:, :, :].rearrange("p a b -> p (a b)")
        ring, slot, wdt, _, wt = W.next(("w_dt", 0, 0, 512), 512, False)
        gk, b, free = G.take()
        pe.wait(free, wt)
        hx = xin
        for c in range(6):
            for k in range(8):
                for part in (hh, hl):
                    f = lambda e: e.matmul(ps[:, b, c * 64:c * 64 + 64], part[:, k, c * 128:c * 128 + 128].bitcast(F32), wdt[:, k * 64:k * 64 + 64],
                                           start=(k == 0 and part is hh), stop=(k == 7 and part is hl))
                    if c == 5 and k == 7 and part is hl:
                        t = pe(f)
                    else:
                        pe.quiet(f)
        ring.give(slot, t)
        t = dve(lambda e: e.tensor_tensor(dt_[:, :, :], ps[:, b, 0:384].rearrange("p (c h) -> p c h", h=64),
                                          rows[:, 0:64].unsqueeze(1).to_broadcast([P, 6, 64]), ALU.add), t)
        G.give(gk, t)
        ta = act(lambda e: e.activation(rows[:, 64:128], rows[:, 64:128], ACT.Exp))
        t_dt = softplus(flat(dt_), flat(csm), flat(wdec), flat(etot))
        t = dve(lambda e: e.scalar_tensor_tensor(out=la[:, :, :], in0=dt_[:, :, :], scalar=-1.0,
                                                 in1=rows[:, 64:128].unsqueeze(1).to_broadcast([P, 6, 64]), op0=ALU.mult, op1=ALU.mult), t_dt, ta)
        pv = lambda b: ps[:, b, 0:384].rearrange("p (c h) -> p c h", h=64)
        pe.quiet(lambda e: e.matmul(pv(5)[:, :, 0:32], C("trif"), la[:, :, 0:32], start=True, stop=True), t)
        t1 = pe(lambda e: e.matmul(pv(6)[:, :, 32:64], C("trib"), la[:, :, 32:64], start=True, stop=True))
        t2 = pe(lambda e: e.matmul(pv(7), ones, la[:, :, :], start=True, stop=True))
        dve(lambda e: e.tensor_copy(csm[:, :, 0:32], pv(5)[:, :, 0:32]), t1)
        t = dve(lambda e: e.tensor_copy(csm[:, :, 32:64], pv(6)[:, :, 32:64]))
        t = dve(lambda e: e.tensor_tensor(wdec[:, :, :], pv(7), csm[:, :, :], ALU.subtract), t2, t)
        te = act(lambda e: e.activation(etot[:, :, :], pv(7), ACT.Exp), t2, t)
        t = dve(lambda e: e.tensor_scalar(flat(wdec), flat(wdec), 0.0, None, ALU.min), t)
        ta = act(lambda e: e.activation(wdec[:, :, :], wdec[:, :, :], ACT.Exp), t)
        t_wd = dve(lambda e: e.tensor_tensor(wdec[:, :, :], wdec[:, :, :], dt_[:, :, :], ALU.mult), ta)
        for c in range(4):
            t = pe(lambda e: e.transpose(ps[0:64, 3, c * 128:c * 128 + 128], csm[:, c, :], ident), t_wd)
        t_ct = dve(lambda e: e.tensor_copy(csT[:, :], ps[0:64, 3, :]), t)
        t_csd = Dma("s_csd").start(act, csd.rearrange("d h t -> (d h) t"), csT[:, :], t_ct)
        pool.wait(t_wd, te)
        pe.wait(t_wd)
        dve.wait(te)
        dbc = [Dma(f"s_bc{i}") for i in range(3)]

        def conv(psum, T, m, names, dst, *toks):
            w0, w1, w2, bb = (V(n, m) for n in names)
            t = act(lambda e: e.activation(dst, psum, ACT.Identity, bias=bb, scale=w1), toks)
            t = dve(lambda e: e.scalar_tensor_tensor(out=dst[:, 1:T], in0=psum[:, 0:T - 1], scalar=w0, in1=dst[:, 1:T],
                                                     op0=ALU.mult, op1=ALU.add), t)
            return dve(lambda e: e.scalar_tensor_tensor(out=dst[:, 0:T - 1], in0=psum[:, 1:T], scalar=w2, in1=dst[:, 0:T - 1],
                                                        op0=ALU.mult, op1=ALU.add), t)

        CW = ("cw0", "cw1", "cw2", "cb")
        Tb, Yb, Sb, Qb = banks(3, 4), banks(5), banks(6), banks(7)
        xwr = Ring([xw[:, 0, :], xw[:, 1, :]])
        bcr = Ring([0, 1, 2])
        ypr = Ring([0])
        tx = {}
        busy = {"x": {0: [], 1: []}, "xc": [], "xtok": [], "Btok": [], "st": [t_csd], "y": [], "E": []}
        dy = Dma("s_y")
        acc_tok = [None]
        t_yz = {}

        def xbc(g):
            q = g % 2
            for i in range(6):
                m = [g * 4 + 0, g * 4 + 1, g * 4 + 2, g * 4 + 3, 16 + g, 20 + g][i]
                rng = [(0, L), (L, LT)] if i < 5 else [(0, L)]
                outs = gemm("w_xbc", m, 8, HP, rng)
                tt = []
                for (t0, t1), (gk, pp, tok) in zip(rng, outs):
                    if i < 4:
                        dst = xsl[:, q, i, :] if t0 == 0 else xsc_[:, i, :]
                    elif i == 4:
                        dst = BTs[:, q, t0:t1]
                    else:
                        dst = CTs[:, q, :]
                    t = conv(pp, t1 - t0, m, CW, dst, tok, busy["x"][q], busy["xc"] if (i < 4 and t0) else None)
                    G.give(gk, t)
                    i_, s, free = sqr.take()
                    s = s[:, 0:t1 - t0]
                    ta = act(lambda e: e.activation(s, dst, ACT.Tanh), t, free)
                    t = dve(lambda e: e.scalar_tensor_tensor(out=dst, in0=s, scalar=1.0, in1=dst, op0=ALU.add, op1=ALU.mult), ta)
                    sqr.give(i_, t)
                    tt.append(t)
                tx[(g, i)] = tt
                yield 8.5 if i < 5 else 5.5

        def zgate(g):
            for j in range(4):
                m = 4 * g + j
                (gk, pp, tok), = gemm("w_z", m, 8, HP, [(0, L)])
                i_, s, free = sqr.take()
                ta = act(lambda e: e.activation(s, pp, ACT.Tanh, scale=0.5), tok, free)
                t1 = dve(lambda e: e.scalar_tensor_tensor(out=s, in0=s, scalar=1.0, in1=pp, op0=ALU.add, op1=ALU.mult), ta)
                G.give(gk, t1)
                t1 = dve(lambda e: e.tensor_tensor(yg[:, j, :], yg[:, j, :], s, ALU.mult), t1, t_yz[g])
                ta = act(lambda e: e.activation(s, yg[:, j, :], ACT.Square), t1)
                if m == 0:
                    acc_tok[0] = dve(lambda e: e.tensor_copy(acc[:, 0:L], s), ta)
                else:
                    acc_tok[0] = dve(lambda e: e.tensor_tensor(acc[:, 0:L], acc[:, 0:L], s, ALU.add), ta, acc_tok[0])
                sqr.give(i_, acc_tok[0])
                t = act(lambda e: e.activation(yg[:, j, :], yg[:, j, :], ACT.Copy, scale=V("sg", m)), ta)
                yk, _, free = ypr.take()
                th = act(lambda e: e.copy(ysp[:, 0, :], yg[:, j, :]), t, free)
                tl = pool(lambda e: e.tensor_tensor(ysp[:, 1, :], yg[:, j, :], ysp[:, 0, :].bitcast(F32), ALU.subtract), th)
                sp_or = act
                t = dy.start(act, A["ysc"][:, :, m, :].rearrange("s p t -> p s t"), ysp[:, :, :].bitcast(F32), th, tl)
                ypr.give(yk, t)
                busy["y"] = [tl, t]
                yield 5.5

        def ssd_group(g):
            q = g % 2
            xs, BT, CT = xsl[:, q], BTs[:, q], CTs[:, q]
            xcols = lambda j, c: xs[:, j, c * 128:(c + 1) * 128] if c < 4 else xsc_[:, j, (c - 4) * 128:(c - 3) * 128]
            loads = {}

            def load_cs(c, d):
                bk, bb, bfree = bcr.take()
                t_b = dbc[bk].start(act, csbc[:, bb, :, :],
                                    csd[d, g * 8:g * 8 + 8, c * 128:(c + 1) * 128].unsqueeze(0).to_broadcast([P, 8, 128]), bfree, t_csd)
                loads[(c, d)] = (bk, bb, t_b)

            load_cs(0, 0)
            load_cs(0, 1)
            t_xt = {}
            for c in (4, 5, 0, 1, 2, 3):
                ik, b, free = Tb.take()
                for j in range(4):
                    t = pe(lambda e: e.transpose(ps[:, b, j * 128:(j + 1) * 128], xcols(j, c), ident), free, tx[(g, j)])
                if c % 2:
                    t = dve(lambda e: e.tensor_copy(xtok[:, c, :], bank(b)), t, busy["xtok"])
                else:
                    t = act(lambda e: e.copy(xtok[:, c, :], bank(b)), t, busy["xtok"])
                Tb.give(ik, t)
                t_xt[c] = t
                if c == 5:
                    busy["xc"] = [t_xt[4], t_xt[5]]
                    yield 1.5
            yield 3.0
            for c0, c1 in ((0, 4), (4, 6)):
                ik, b, free = Tb.take()
                for c in range(c0, c1):
                    t = pe(lambda e: e.transpose(ps[:, b, (c - c0) * 128:(c - c0 + 1) * 128], BT[:, c * 128:(c + 1) * 128], ident), free, tx[(g, 4)])
                t = act(lambda e: e.copy(Btok[:, c0:c1, :].rearrange("p a b -> p (a b)"), ps[:, b, 0:(c1 - c0) * 128]), t, busy["Btok"])
                Tb.give(ik, t)
            t_bt = t
            yield 1.0
            t_st = {}
            for d in (0, 1):
                prev, tp = None, busy["st"]
                seq = [4, 5, 0, 1, 2] if d == 0 else [5, 4, 3, 2, 1]
                for n, c in enumerate(seq):
                    h0 = d * 32 + g * 8
                    ik, x_, free = xwr.take()
                    t = pool(lambda e: e.tensor_tensor(x_.rearrange("p (r q) -> p r q", q=64), xtok[:, c, :].rearrange("p (r q) -> p r q", q=64),
                                                       wdec[:, c, h0:h0 + 8].unsqueeze(2).to_broadcast([P, 8, 64]), ALU.mult), free, t_xt[c])
                    sk, b, sfree = Sb.take()
                    t = pe(lambda e: e.matmul(bank(b), Btok[:, c, :], x_, start=True, stop=True), t, t_bt, sfree)
                    xwr.give(ik, t)
                    if n == 0:
                        dst = st0[:, :]
                        tp = dve(lambda e: e.tensor_copy(dst, bank(b)), t, tp)
                    else:
                        use = n - 1 if d == 0 else 4 - n
                        dst = st[:, d, use, :]
                        t2 = dve(lambda e: e.tensor_tensor(stt_[:, :].rearrange("p (r q) -> p r q", q=64), prev.rearrange("p (r q) -> p r q", q=64),
                                                           etot[:, c, h0:h0 + 8].unsqueeze(2).to_broadcast([P, 8, 64]), ALU.mult), tp)
                        tp = dve(lambda e: e.tensor_tensor(dst, stt_[:, :], bank(b), ALU.add), t, t2, busy["st"])
                        t_st[(d, use)] = tp
                    prev = dst
                    Sb.give(sk, tp)
                    yield 2.2
            for c in range(4):
                qk, b, free = Qb.take()
                t = pe(lambda e: e.matmul(ps[:, b, 0:128], BT[:, c * 128:(c + 1) * 128], CT[:, c * 128:(c + 1) * 128], start=True, stop=True),
                       free, tx[(g, 4)], tx[(g, 5)])
                dve(lambda e: e.tensor_tensor(cbm[:, 0, :], ps[:, b, 0:128], C("trif"), ALU.mult), t, busy["E"])
                t_cb = dve(lambda e: e.tensor_tensor(cbm[:, 1, :], ps[:, b, 0:128], C("trib"), ALU.mult))
                Qb.give(qk, t_cb)
                tcs = []
                tE = {}
                for d in (0, 1):
                    bk, bb, t_b = loads[(c, d)]
                    te_ = act(lambda e: e.activation(Cs[:, d, :, :], csbc[:, bb, :, :], ACT.Exp), t_b, busy["E"])
                    tcs.append(pool(lambda e: e.tensor_tensor(Cs[:, d, :, :], Cs[:, d, :, :],
                                                              CT[:, c * 128:(c + 1) * 128].unsqueeze(1).to_broadcast([P, 8, 128]), ALU.mult), te_, tx[(g, 5)]))
                    for r in range(8):
                        h = d * 32 + g * 8 + r
                        t = dve(lambda e: e.tensor_scalar(Ew[:, d, r, :], csbc[:, bb, r, :], csm[:, c, h:h + 1], 0.0, ALU.subtract, ALU.min), t_b, busy["E"])
                    bcr.give(bk, te_, t)
                    tE[d] = act(lambda e: e.activation(Ew[:, d, :, :], Ew[:, d, :, :], ACT.Exp), t)
                    if c < 3:
                        load_cs(c + 1, d)
                    yield 1.6
                for d in (0, 1):
                    for r in range(8):
                        h = d * 32 + g * 8 + r
                        t = dve(lambda e: e.scalar_tensor_tensor(out=Ew[:, d, r, :], in0=Ew[:, d, r, :], scalar=dt_[:, c, h:h + 1],
                                                                 in1=cbm[:, d, :], op0=ALU.mult, op1=ALU.mult), tE[d], t_cb)
                    yield 1.8
                t_w = dve(lambda e: e.tensor_tensor(Ew[:, 0, :, :], Ew[:, 0, :, :], Ew[:, 1, :, :], ALU.add), t)
                yield 1.5
                yk, b, free = Yb.take()
                pe.wait(free, t_w, tcs, t_st[(0, c)], t_st[(1, c)])
                for r in range(8):
                    o = ps[(r % 2) * 64:(r % 2) * 64 + 64, b, (r // 2) * 128:(r // 2 + 1) * 128]
                    pe.quiet(lambda e: e.matmul(o, xtok[:, c, r * 64:r * 64 + 64], Ew[:, 0, r, :], start=True, stop=False))
                    pe.quiet(lambda e: e.matmul(o, st[:, 0, c, r * 64:r * 64 + 64], Cs[:, 0, r, :], start=False, stop=False))
                    f = lambda e: e.matmul(o, st[:, 1, c, r * 64:r * 64 + 64], Cs[:, 1, r, :], start=False, stop=True)
                    t_y = pe(f) if r == 7 else pe.quiet(f)
                busy["E"] = [t_y]
                yield 6.5
                for j in range(4):
                    t = dve(lambda e: e.scalar_tensor_tensor(out=yg[:, j, c * 128:(c + 1) * 128], in0=xs[:, j, c * 128:(c + 1) * 128],
                                                             scalar=V("dsk", 4 * g + j), in1=ps[:, b, j * 128:(j + 1) * 128], op0=ALU.mult, op1=ALU.add), t_y, busy["y"])
                Yb.give(yk, t)
            busy["x"][q] = [t, t_y, tcs]
            busy["xtok"] = busy["Btok"] = busy["st"] = [t_y]
            t_yz[g] = t

        run(xbc(0))
        weave(ssd_group(0), xbc(1))
        weave(ssd_group(1), chain_of(zgate(0), xbc(2)))
        weave(ssd_group(2), chain_of(zgate(1), xbc(3)))
        weave(ssd_group(3), chain_of(zgate(2), mod_blocks(16, 48)))
        t = dve(lambda e: e.tensor_scalar(A2[:, :], modS[:, 32:40, 0], 1.0, None, ALU.add), t_mod[0])
        t_A2 = dve(lambda e: e.tensor_tensor(A2[:, :], A2[:, :], V("g2", 0, 8), ALU.mult), t)
        run(zgate(3))
        t = norm_rstd([(0, L)], acc_tok[0], 0.25 / 2048, acc, rstd, (sq[:, 0, :], sq[:, 1, :]))
        t_rs = dve(lambda e: e.tensor_scalar(rstd[:, 0:L], rstd[:, 0:L], 0.25, None, ALU.mult), t)
        sqr.give(0, t_rs)
        sqr.give(1, t_rs)
        fm = fence()
        act.wait((dy.sem, dy.n))

        kT = at("kT", [P, 2, LT], 106)
        kTs = at("kTs", [P, 2, LT], 112)
        rope = at("rope", [P, 2, L], 118)
        gt = at("gt", [P, 16, L], 122)
        qT = at("qT", [P, 8, L], 154)
        vt = at("vt", [P, 6, 256], 170)
        raw = at("raw", [P, 2, L], 176)
        rt = at("rt", [P, 2, L], 180)
        Pm = at("Pm", [P, 4, 640], 184)
        PT = at("PT", [P, 5, 4, 128], 194)
        small = at("small", [P, 4, 4], 204)
        t_rope = Dma("s_rope").start(act, rope[:, :, :].rearrange("p a b -> p (a b)"), A["consts"][:, 896:1920], fm)
        rawr = Ring([0, 1])
        Pb = banks(3, 4)
        t_q = {}

        def qk_gemms(ms):
            for m in ms:
                isq = m < 8
                rng = [(0, L)] if isq else [(0, L), (L, LT)]
                outs = gemm("w_qk", m, 8, HP, rng)
                gk, pp, tok = outs[0]
                ik, i_, free = rawr.take()
                ta = act(lambda e: e.mul(raw[:, i_, :], pp, 0.125 if isq else 1.0), tok, free)
                G.give(gk, ta)
                bk, b, bfree = Pb.take()
                tp = pe(lambda e: e.matmul(bank(b), C("perm"), raw[:, i_, :], start=True, stop=True), ta, bfree)
                tg = dve(lambda e: e.tensor_tensor(rt[:, i_, :], raw[:, i_, :], rope[:, 0, :], ALU.mult), ta, t_rope, free)
                dst = qT[:, m, :] if isq else kT[:, m - 8, 0:L]
                t = dve(lambda e: e.tensor_tensor(dst, bank(b), rope[:, 1, :], ALU.mult), tp, t_rope)
                Pb.give(bk, t)
                t = dve(lambda e: e.tensor_tensor(dst, dst, rt[:, i_, :], ALU.add), t, tg)
                rawr.give(ik, tp, tg, t)
                t_q[m] = [t]
                if not isq:
                    gk, pp, tok = outs[1]
                    ta = act(lambda e: e.copy(kT[:, m - 8, L:LT], pp), tok)
                    G.give(gk, ta)
                    t_q[m].append(ta)

        def tokmajor(wd, nb, src, NT, dst, tl):
            for q in range(nb):
                s = [W.next((wd, (q, i), 0, 1024), 1024, True, held=i) for i in (0, 1)]
                for c in range(NT):
                    gk, b, free = G.take()
                    pe.wait(free, s[0][4], s[1][4])
                    o = ps[:, b, 0:256]
                    for k in range(8):
                        wh, wl = (x[:, (k % 4) * 256:(k % 4 + 1) * 256] for x in s[k // 4][2:4])
                        xh, xl = (f(k)[:, c * 128:(c + 1) * 128] for f in (src.hi, src.lo))
                        pe.quiet(lambda e: e.matmul(o, xh, wh, start=(k == 0), stop=False))
                        pe.quiet(lambda e: e.matmul(o, xh, wl, start=False, stop=False))
                        f = lambda e: e.matmul(o, xl, wh, start=False, stop=(k == 7))
                        t = pe(f) if k == 7 else pe.quiet(f)
                    ta = act(lambda e: e.copy(dst(c)[:, q * 256:(q + 1) * 256], o), t)
                    G.give(gk, ta)
                    tl.append(ta)
                    yield 3.0
                s[0][0].give(s[0][1], t)
                s[1][0].give(s[1][1], t)

        def softmax(S, dstP, sm, scale, sink, ready, free):
            t = dve(lambda e: e.tensor_reduce(sm[:, 0:1], S, AXX, ALU.max), ready, free)
            if sink is not None:
                t = dve(lambda e: e.tensor_scalar(sm[:, 1:2], sm[:, 0:1], sink, -1.0, ALU.max, ALU.mult), t)
            else:
                t = dve(lambda e: e.tensor_scalar(sm[:, 1:2], sm[:, 0:1], -scale, None, ALU.mult), t)
            ts = act(lambda e: e.activation(dstP, S, ACT.Exp, bias=sm[:, 1:2], scale=scale, accum_out=sm[:, 2:3]), t, free)
            ta = ts
            if sink is not None:
                ta = act(lambda e: e.activation(sm[:, 3:4], sink, ACT.Exp, bias=sm[:, 1:2]), t)
            return ta

        def normalise(dstP, sm, sink, ta):
            t = ta
            if sink:
                t = dve(lambda e: e.tensor_tensor(sm[:, 2:3], sm[:, 2:3], sm[:, 3:4], ALU.add), t)
            t = dve(lambda e: e.reciprocal(sm[:, 1:2], sm[:, 2:3]), t)
            return dve(lambda e: e.tensor_scalar(dstP, dstP, sm[:, 1:2], None, ALU.mult), t)

        qk_gemms([8, 9])
        dks = Dma("s_ks")
        dks.start(act, kTs[0:64, :, :], kT[64:128, :, :], t_q[8], t_q[9])
        t_ks = dks.start(act, kTs[64:128, :, :], kT[0:64, :, :])
        t_v = []
        run(tokmajor("w_v", 1, HP, 6, lambda c: vt[:, c, :], t_v))
        qk_gemms(range(8))
        pe.wait([t_q[m] for m in range(10)], t_v, t_ks)
        G = banks(0, 1)

        def window_attention():
            Sr, Tr, Or = banks(3, 5), banks(7), banks(2)
            pr = Ring([0, 1, 2, 3])
            pt_busy = []
            for n in range(4):
                lo, hi = max(n - 1, 0), min(n + 1, 3)
                nw = hi - lo + 1
                w0 = 512 - nw * 128
                Wd = nw * 128 + 256
                nk = nw + 2
                for kv in range(4):
                    half, kt = (kv % 2) * 64, kv // 2
                    pend = []
                    for j in range(4):
                        h = 4 * kv + j
                        qrow = (h % 2) * 64
                        sk, b, free = Sr.take()
                        q = qT[qrow:qrow + 64, h // 2, n * 128:(n + 1) * 128]
                        kk = (kT if qrow == half else kTs)[qrow:qrow + 64, kt, :]
                        pe.wait(free)
                        pe.quiet(lambda e: e.matmul(ps[:, b, w0:512], q, kk[:, lo * 128:(hi + 1) * 128], start=True, stop=False))
                        if n > 0:
                            pe.quiet(lambda e: e.matmul(ps[:, b, w0:w0 + 128], maskb[:, 0, :], maskb[:, 1, :], start=False, stop=(n == 3)))
                        if n < 3:
                            pe.quiet(lambda e: e.matmul(ps[:, b, 384:512], maskb[:, 0, :], maskb[:, 2, :], start=False, stop=True))
                        t = pe(lambda e: e.matmul(ps[:, b + 1, 0:256], q, kk[:, L:LT], start=True, stop=True))
                        S = ps[:, b:b + 2, :].rearrange("p a b -> p (a b)")[:, w0:w0 + Wd]
                        pk, pi, pfree = pr.take()
                        ta = softmax(S, Pm[:, pi, 0:Wd], small[:, pi, :], 1.0, rows[:, 128 + h:129 + h], t, pfree)
                        Sr.give(sk, ta)
                        pend.append((pk, pi, ta))
                        if j:
                            _, pi1, ta1 = pend[j - 1]
                            pend[j - 1] += (normalise(Pm[:, pi1, 0:Wd], small[:, pi1, :], True, ta1),)
                        yield 1.7
                    _, pi1, ta1 = pend[3]
                    pend[3] += (normalise(Pm[:, pi1, 0:Wd], small[:, pi1, :], True, ta1),)
                    t_pt = []
                    for kb in range(nk):
                        tk, b, free = Tr.take()
                        for j, (pk, pi, ta, tn) in enumerate(pend):
                            t = pe(lambda e: e.transpose(ps[:, b, j * 128:(j + 1) * 128], Pm[:, pi, kb * 128:(kb + 1) * 128], ident), free, tn)
                        if kb % 2:
                            t2 = dve(lambda e: e.tensor_copy(PT[:, kb, :, :].rearrange("p a b -> p (a b)"), bank(b)), t, pt_busy)
                        else:
                            t2 = act(lambda e: e.copy(PT[:, kb, :, :].rearrange("p a b -> p (a b)"), bank(b)), t, pt_busy)
                        Tr.give(tk, t2)
                        t_pt.append(t2)
                        yield 1.0
                    for pk, pi, ta, tn in pend:
                        pr.give(pk, t, tn)
                    ok, b, free = Or.take()
                    pe.wait(free, t_pt)
                    for par in (0, 1):
                        for kb in range(nk):
                            c = lo + kb if kb < nw else 4 + kb - nw
                            t = pe(lambda e: e.matmul(ps[par * 64:par * 64 + 64, b, 0:256].rearrange("p (a b) -> p a b", b=128), vt[:, c, kv * 64:(kv + 1) * 64],
                                                      PT[:, kb, par:4:2, :], start=(kb == 0), stop=(kb == nk - 1)))
                    pt_busy = [t]
                    t_o = dve(lambda e: e.tensor_copy(qT[:, 2 * kv:2 * kv + 2, n * 128:(n + 1) * 128],
                                                      ps[:, b, 0:256].rearrange("p (a b) -> p a b", b=128)), t)
                    Or.give(ok, t_o)
                    yield 4.0

        t_gate = {}

        def gates1():
            for i in range(16):
                (gk, pp, tok), = gemm("w_g", i, 8, HP, [(0, L)])
                ta = act(lambda e: e.activation(gt[:, i, :], pp, ACT.Tanh, scale=0.5), tok)
                G.give(gk, ta)
                t_gate[i] = ta
                yield GATE1

        GATE1 = 14.0
        weave(window_attention(), gates1())
        fm = fence()

        QP, _, _ = pair("qp", 8, L, 170)
        YP, yh, yl = pair("yp", 16, L, 58)
        MP_ = at("mp", [P, 16, L], 122, F32R)
        MP = Pair(lambda k: MP_[:, k, :], lambda k: MP_[:, 8 + k, :])
        X = at("X", [P, 8, L], 202)
        t_x = Dma("s_xr").start(sp, X[:, :, :], A["xT"], fm)
        dyl = [Dma(f"s_yl{i}") for i in range(4)]
        t_yl = []
        for i in range(4):
            dyl[i].start(act, yh[:, 4 * i:4 * i + 4, :].bitcast(F32), A["ysc"][0, :, 4 * i:4 * i + 4, :], fm)
            t_yl.append(dyl[i].start(act, yl[:, 4 * i:4 * i + 4, :].bitcast(F32), A["ysc"][1, :, 4 * i:4 * i + 4, :]))
        t_qp = [QP.put(k, qT[:, k, :], 0, L, lo=(dve if k % 2 else pool)) for k in range(8)]
        G = banks(0, 1, 2, 3, 4, 5, 6, 7)
        t_oa = []
        for m in range(8):
            (gk, pp, tok), = gemm("w_oa", m, 8, QP, [(0, L)], t_qp)
            t = dve(lambda e: e.scalar_tensor_tensor(out=gt[:, 8 + m, :], in0=gt[:, 8 + m, :], scalar=1.0, in1=pp, op0=ALU.add, op1=ALU.mult), tok)
            G.give(gk, t)
            t_oa.append(t)
        t_m = []
        for m in range(8):
            (gk, pp, tok), = gemm("w_os", m, 16, YP, [(0, L)], t_yl)
            t = dve(lambda e: e.scalar_tensor_tensor(out=gt[:, m, :], in0=gt[:, m, :], scalar=1.0, in1=pp, op0=ALU.add, op1=ALU.mult), tok)
            G.give(gk, t)
            t = dve(lambda e: e.tensor_tensor(gt[:, m, :], gt[:, m, :], rstd[:, 0:L], ALU.mult), t)
            i_, s, free = sqr.take()
            t = dve(lambda e: e.scalar_tensor_tensor(out=s, in0=gt[:, 8 + m, :], scalar=0.5, in1=gt[:, m, :], op0=ALU.mult, op1=ALU.add), t, t_oa[m], free)
            tt = MP.put(m, s, 0, L, t)
            sqr.give(i_, tt)
            t_m.append(tt)
        t_x1 = []
        for m in range(8):
            (gk, pp, tok), = gemm("w_out", m, 8, MP, [(0, L)], t_m)
            t = dve(lambda e: e.scalar_tensor_tensor(out=X[:, m, :], in0=pp, scalar=modS[:, 16 + m, 0:1], in1=X[:, m, :], op0=ALU.mult, op1=ALU.add), tok, t_x)
            G.give(gk, t)
            t_x1.append(t)

        H2, _, _ = pair("h2", 8, L, 58)
        PR, _, _ = pair("pr", 22, L, 90)
        ua = at("ua", [P, 4, L], 178)
        ub = at("ub", [P, 2, L], 186)
        vt2 = at("vt2", [P, 2, L], 190)
        fence()
        v2r = Ring([vt2[:, 0, :], vt2[:, 1, :]])
        t_r = norm_T(lambda k: X[:, k, :], 8, L, t_x1)
        t_h = []
        for k in range(8):
            i_, v, free = v2r.take()
            t = dve(lambda e: e.tensor_tensor(v, X[:, k, :], rstd[:, 0:L], ALU.mult), t_r, free)
            t = dve(lambda e: e.tensor_scalar(v, v, A2[:, k:k + 1], modS[:, 24 + k, 0:1], ALU.mult, ALU.add), t, t_A2)
            tt = H2.put(k, v, 0, L, t, lo=dve)
            v2r.give(i_, tt)
            t_h.append(tt)
        uar, ubr = Ring([0, 1, 2, 3]), Ring([0, 1])
        FW = ("fw0", "fw1", "fw2", "fb")
        t_p = []
        for m in range(22):
            tt = []
            for which in (0, 1):
                mm = m + 22 * which
                (gk, pp, tok), = gemm("w_up", mm, 8, H2, [(0, L)], t_h)
                ik, i_, free = uar.take()
                t = conv(pp, L, mm, FW, ua[:, i_, :], tok, free)
                G.give(gk, t)
                tt.append((ik, i_, t))
            (ka, ia, ta_), (kb_, ib, tb_) = tt
            k2, i2, free = ubr.take()
            ta = act(lambda e: e.activation(ub[:, i2, :], ua[:, ia, :], ACT.Tanh), ta_, free)
            t = dve(lambda e: e.scalar_tensor_tensor(out=ub[:, i2, :], in0=ub[:, i2, :], scalar=1.0, in1=ua[:, ia, :], op0=ALU.add, op1=ALU.mult), ta)
            t = dve(lambda e: e.tensor_tensor(ub[:, i2, :], ub[:, i2, :], ua[:, ib, :], ALU.mult), t, tb_)
            tt = PR.put(m, ub[:, i2, :], 0, L, t, lo=dve)
            uar.give(ka, t)
            uar.give(kb_, t)
            ubr.give(k2, tt)
            t_p.append(tt)
        t_x2 = []
        for m in range(8):
            (gk, pp, tok), = gemm("w_down", m, 22, PR, [(0, L)], t_p)
            t = dve(lambda e: e.scalar_tensor_tensor(out=X[:, m, :], in0=pp, scalar=modS[:, 40 + m, 0:1], in1=X[:, m, :], op0=ALU.mult, op1=ALU.add), tok)
            G.give(gk, t)
            t_x2.append(t)
        t_r = norm_T(lambda k: X[:, k, :], 8, L, t_x2)
        tl = []
        for k in range(8):
            tl.append(dve(lambda e: e.scalar_tensor_tensor(out=X[:, k, :], in0=X[:, k, :], scalar=V("fg", k), in1=rstd[:, 0:L], op0=ALU.mult, op1=ALU.mult), t_r))
        t_spill = Dma("s_spill").start(sp, A["xsc"], X[:, :, :], tl)
        fence()
        H, _, _ = pair("H", 8, L, 58)
        vt3 = at("vt3", [P, 2, L], 90)
        v3r = Ring([vt3[:, 0, :], vt3[:, 1, :]])
        t_r = norm_T(lambda k: X[:, k, :], 8, L, tl)
        t_H = []
        for k in range(8):
            i_, v, free = v3r.take()
            t = dve(lambda e: e.scalar_tensor_tensor(out=v, in0=X[:, k, :], scalar=V("gn", k), in1=rstd[:, 0:L], op0=ALU.mult, op1=ALU.mult), t_r, free)
            tt = H.put(k, v, 0, L, t, lo=dve)
            v3r.give(i_, tt)
            t_H.append(tt)
        for e in (pe, dve, act, pool):
            e.wait(t_spill, t_H)
        fence()

        yf = at("yf", [P, 6, L], 90)
        ysv = at("ysv", [P, 6, L], 102)
        ym = at("ym", [P, 4, L], 114)
        kf = at("kf", [P, 6, L], 122)
        vf = at("vf", [P, 4, 768], 134)
        Pf = at("Pf", [P, 4, L], 146)
        PTf = at("PTf", [P, 4, L], 154)
        FT = at("FT", [12, L], 162)
        lf = at("lf", [P, 4, 12], 164)
        l2 = at("l2", [P, 3, 48], 164.25)
        smf = at("smf", [P, 4, 4], 164.875)
        uT = at("uT", [P, 6, L], 165)
        z32 = at("z32", [P, 2, 24, 32], 177)
        q16 = at("q16", [P, 2, 24, 16], 183)
        bl = at("bl", [P, 2, 6, 128], 186)
        cl = at("cl", [P, 2, 24, 32], 192)
        Tc = at("Tc", [P, 2, 2, L], 198)
        Wk = at("Wk", [P, 8, L], 206)
        wkf = Wk[:, :, :].rearrange("p a b -> p (a b)")
        bre = wkf[:, 0:768].rearrange("p (a b) -> p a b", b=32)
        bim = wkf[:, 768:1536].rearrange("p (a b) -> p a b", b=32)
        bb = wkf[:, 1536:3840].rearrange("p (q a b) -> p q a b", q=3, b=32)
        G = banks(0, 1)

        t_u = []
        t_fq = {}
        t_fv = []

        def silu_gate(pp, tok, gk, src, dst, *toks):
            i_, s, sfree = sqr.take()
            ta = act(lambda e: e.activation(s, pp, ACT.Tanh, scale=0.5), tok, sfree)
            t1 = dve(lambda e: e.scalar_tensor_tensor(out=s, in0=s, scalar=1.0, in1=pp, op0=ALU.add, op1=ALU.mult), ta)
            G.give(gk, t1)
            t1 = dve(lambda e: e.tensor_tensor(dst, s, src, ALU.mult), t1, toks)
            sqr.give(i_, t1)
            return t1

        def u_gemms():
            for m in range(6):
                (gk, pp, tok), = gemm("w_u", m, 8, H, [(0, L)])
                ta = act(lambda e: e.copy(uT[:, m, :], pp), tok)
                G.give(gk, ta)
                t_u.append(ta)
                yield 5.5

        def fq_gemms():
            for m in range(12):
                (gk, pp, tok), = gemm("w_fqk", m, 8, H, [(0, L)])
                dst = yf[:, m, :] if m < 6 else kf[:, m - 6, :]
                ta = act(lambda e: e.mul(dst, pp, 0.125 if m < 6 else 1.0), tok)
                G.give(gk, ta)
                t_fq[m] = ta
                yield 5.5

        t_FT = [None]

        def forget():
            ring, slot, wfl, _, wt = W.next(("w_fl", 0, 0, 96), 96, False)
            gk, b, free = G.take()
            pe.wait(free, wt)
            for c in range(4):
                for k in range(8):
                    for q, part in enumerate((H.hi, H.lo)):
                        f = lambda e: e.matmul(ps[:, b, c * 12:c * 12 + 12], part(k)[:, c * 128:c * 128 + 128].bitcast(F32), wfl[:, k * 12:k * 12 + 12],
                                               start=(k == 0 and q == 0), stop=(k == 7 and q == 1))
                        t = pe(f) if (c == 3 and k == 7 and q == 1) else pe.quiet(f)
            ring.give(slot, t)
            t = dve(lambda e: e.scalar_tensor_tensor(out=lf[:, :, :], in0=ps[:, b, 0:48].rearrange("p (c h) -> p c h", h=12), scalar=-1.0,
                                                     in1=rows[:, 144:156].unsqueeze(1).to_broadcast([P, 4, 12]), op0=ALU.mult, op1=ALU.subtract), t)
            t_lf = softplus(flat(lf), l2[:, 0, :], l2[:, 1, :], l2[:, 2, :])
            pe.wait(t_lf)
            for c in range(4):
                for cc in range(c + 1):
                    t = pe(lambda e: e.matmul(ps[0:12, b, c * 128:(c + 1) * 128], lf[:, cc, :], C("trif") if cc == c else ones,
                                              start=(cc == 0), stop=(cc == c)))
            t = dve(lambda e: e.tensor_copy(FT[:, :], ps[0:12, b, :]), t)
            G.give(gk, t)
            t_FT[0] = t
            yield 8.0

        def gate_gemms(wd, ms, dst, ready):
            for m in ms:
                (gk, pp, tok), = gemm(wd, m, 8, H, [(0, L)])
                ready[m] = silu_gate(pp, tok, gk, dst(m), dst(m), ready[m])
                yield 6.0

        t_d5 = [None]
        K = lambda i: pk_[:, i, :]
        lr, li, ls = V("lre", 0, 24), V("lim", 0, 24), V("lstep", 0, 24)
        PI2 = 2 * np.pi
        C1, C2 = 6.28125, 0.0019350051879882812
        C3 = PI2 - C1 - C2
        MAGIC = 12582912.0
        TT = lambda o, a, b_, op: (dve, lambda e: e.tensor_tensor(o, a, b_, op))
        TS = lambda o, a, s1, s2, o1, o2=None: (dve, lambda e: e.tensor_scalar(o, a, s1, s2, o1, *([o2] if o2 is not None else [])))
        ST = lambda o, a, s, b_, o1, o2: (dve, lambda e: e.scalar_tensor_tensor(out=o, in0=a, scalar=s, in1=b_, op0=o1, op1=o2))
        CP = lambda o, a: (dve, lambda e: e.tensor_copy(o, a))
        AC = lambda o, a, f, sc=1.0: (act, lambda e: e.activation(o, a, f, scale=sc))

        def steps(fns):
            prev = [dve.last(), act.last()]
            for eng, f in fns:
                prev = [eng(f, prev)]

        def cmul(o, a, z, n, tmp):
            zr = z[0].unsqueeze(2).to_broadcast([P, 24, n])
            zi = z[1].unsqueeze(2).to_broadcast([P, 24, n])
            return [TT(tmp, a[1], zi, ALU.mult), TT(o[0], a[0], zr, ALU.mult), TT(o[0], o[0], tmp, ALU.subtract),
                    TT(tmp, a[0], zi, ALU.mult), TT(o[1], a[1], zr, ALU.mult), TT(o[1], o[1], tmp, ALU.add)]

        def csq(o, a):
            return [TT(K(14), a[1], a[1], ALU.mult), TT(K(15), a[0], a[0], ALU.mult), TT(K(15), K(15), K(14), ALU.subtract),
                    ST(K(16), a[0], 2.0, a[1], ALU.mult, ALU.mult), CP(o[0], K(15)), CP(o[1], K(16))]

        def powers(tab, z, n):
            seq = [(dve, lambda e: e.memset(tab[:, 0, :, 0], 1.0)), (dve, lambda e: e.memset(tab[:, 1, :, 0], 0.0)), CP(K(12), z[0]), CP(K(13), z[1])]
            k = 1
            while k < n:
                seq += cmul((tab[:, 0, :, k:2 * k], tab[:, 1, :, k:2 * k]), (tab[:, 0, :, 0:k], tab[:, 1, :, 0:k]), (K(12), K(13)), k, bb[:, 2, :, 0:k])
                seq += csq((K(12), K(13)), (K(12), K(13)))
                k *= 2
            return seq

        def s5_numbers():
            steps([
                AC(K(0), ls, ACT.Exp),
                TT(K(1), lr, K(0), ALU.mult),
                AC(K(2), K(1), ACT.Exp),
                TT(K(3), li, K(0), ALU.mult),
                TS(K(4), K(3), 1.0 / PI2, MAGIC, ALU.mult, ALU.add),
                TS(K(4), K(4), MAGIC, None, ALU.subtract),
                ST(K(3), K(4), -C1, K(3), ALU.mult, ALU.add),
                ST(K(3), K(4), -C2, K(3), ALU.mult, ALU.add),
                ST(K(3), K(4), -C3, K(3), ALU.mult, ALU.add),
                TS(K(3), K(3), 3.1415925, -3.1415925, ALU.min, ALU.max),
                AC(K(5), K(3), ACT.Sin),
                AC(K(6), K(3), ACT.Sin, 0.5),
                TT(K(6), K(6), K(6), ALU.mult),
                TS(K(6), K(6), -2.0, 1.0, ALU.mult, ALU.add),
                TT(K(7), K(2), K(6), ALU.mult),
                TS(K(7), K(7), 1.0, None, ALU.subtract),
                TT(K(8), K(2), K(5), ALU.mult),
                TT(K(9), lr, lr, ALU.mult),
                TT(K(10), li, li, ALU.mult),
                TT(K(9), K(9), K(10), ALU.add),
                (dve, lambda e: e.reciprocal(K(9), K(9))),
                TT(K(10), K(7), lr, ALU.mult),
                TT(K(11), K(8), li, ALU.mult),
                TT(K(10), K(10), K(11), ALU.add),
                TT(K(10), K(10), K(9), ALU.mult),
                TT(K(11), K(8), lr, ALU.mult),
                TT(K(12), K(7), li, ALU.mult),
                TT(K(11), K(11), K(12), ALU.subtract),
                TT(K(11), K(11), K(9), ALU.mult),
            ])

        def s5_tables(Tr5):
            fre = K(10).unsqueeze(2).to_broadcast([P, 24, 32])
            fim = K(11).unsqueeze(2).to_broadcast([P, 24, 32])
            dve.wait(t_d5[0])
            steps([
                TT(bb[:, 0], bre, fre, ALU.mult), TT(bb[:, 2], bim, fim, ALU.mult),
                TT(bb[:, 0], bb[:, 0], bb[:, 2], ALU.subtract),
                TT(bb[:, 1], bim, fre, ALU.mult), TT(bb[:, 2], bre, fim, ALU.mult),
                TT(bb[:, 1], bb[:, 1], bb[:, 2], ALU.add),
                TS(cl[:, 1].rearrange("p a b -> p (a b)"), cl[:, 1].rearrange("p a b -> p (a b)"), -1.0, None, ALU.mult),
            ])
            yield 6.0
            td = dve.last()
            for ri in (0, 1):
                for j in range(6):
                    tk, b, free = Tr5.take()
                    t = pe(lambda e: e.transpose(ps[:, b, 0:128], bb[:, ri, 4 * j:4 * j + 4, :].rearrange("p a b -> p (a b)"), ident), free, td)
                    t = act(lambda e: e.copy(bl[:, ri, j, :], ps[:, b, 0:128]), t)
                    Tr5.give(tk, t)
                yield 3.0
            fns = powers(z32, (K(6), K(5)), 32) + powers(q16, (K(12), K(13)), 16)
            for i in range(0, len(fns), 6):
                steps(fns[i:i + 6])
                yield 1.5
            pool.wait(dve.last())
            pe.wait(t)

        def s5_scan():
            Xr, Yr = banks(2), banks(4)
            yield from s5_tables(banks(2, 3, 4))
            W_ = lambda i: Wk[:, i, :]
            tcr = Ring([0, 1])
            v3 = lambda x: x.rearrange("p (a b) -> p a b", b=32)
            tabs, xs5 = {}, {}
            wfree = {i: [dve.last()] for i in range(8)}

            def table(s):
                ck, cb_, cfree = tcr.take()
                tre, tim = Tc[:, cb_, 0, :], Tc[:, cb_, 1, :]
                Pr, Pi = (z32[:, q, s, :].unsqueeze(1).to_broadcast([P, 16, 32]) for q in (0, 1))
                Qr, Qi = (q16[:, q, s, :].unsqueeze(2).to_broadcast([P, 16, 32]) for q in (0, 1))
                pool(lambda e: e.tensor_tensor(v3(tre), Pr, Qr, ALU.mult), cfree, wfree[6])
                a2 = pool(lambda e: e.tensor_tensor(v3(W_(6)), Pi, Qi, ALU.mult), pool.last())
                a3 = pool(lambda e: e.tensor_tensor(tre, tre, W_(6), ALU.subtract), a2)
                pool(lambda e: e.tensor_tensor(v3(tim), Pi, Qr, ALU.mult))
                a2 = pool(lambda e: e.tensor_tensor(v3(W_(6)), Pr, Qi, ALU.mult), a3)
                tabs[s] = (ck, tre, tim, pool(lambda e: e.tensor_tensor(tim, tim, W_(6), ALU.add), a2))

            def drive(s):
                j, i = s // 4, s % 4
                xk, b, free = Xr.take()
                for ri in (0, 1):
                    t = pe(lambda e: e.matmul(bank(b + ri), bl[32 * i:32 * i + 32, ri, j, :], uT[32 * i:32 * i + 32, j, :],
                                              start=True, stop=True), free, t_u[j])
                xs5[s] = (xk, b, t)

            table(0)
            drive(0)
            for s in range(24):
                j, i = s // 4, s % 4
                ck, tre, tim, t_tab = tabs.pop(s)
                xk, b, t = xs5.pop(s)
                xr, xi = bank(b), bank(b + 1)
                dve(lambda e: e.tensor_tensor(W_(0), xr, tre, ALU.mult), t, t_tab, wfree[0])
                d2 = dve(lambda e: e.tensor_tensor(W_(1), xi, tim, ALU.mult), wfree[1])
                dve(lambda e: e.tensor_tensor(W_(2), xi, tre, ALU.mult), wfree[2])
                d4 = dve(lambda e: e.tensor_tensor(W_(3), xr, tim, ALU.mult), wfree[3])
                Xr.give(xk, d4)
                if s < 23:
                    table(s + 1)
                    drive(s + 1)
                yield 4.0 * S5F
                dve(lambda e: e.tensor_tensor(W_(0), W_(0), W_(1), ALU.add), d2)
                d4 = dve(lambda e: e.tensor_tensor(W_(2), W_(2), W_(3), ALU.subtract), d4)
                mag = K(2)[:, s:s + 1].to_broadcast([P, L])
                d1 = dve(lambda e: e.tensor_tensor_scan(W_(1), mag, W_(0), 0.0, ALU.mult, ALU.add), d4)
                yield 2.5 * S5F
                d2 = dve(lambda e: e.tensor_tensor_scan(W_(3), mag, W_(2), 0.0, ALU.mult, ALU.add), d4)
                d5_ = dve(lambda e: e.tensor_tensor(W_(4), W_(1), tre, ALU.mult), d1, wfree[4])
                d6 = dve(lambda e: e.tensor_tensor(W_(0), W_(3), tim, ALU.mult), d2)
                p1 = pool(lambda e: e.tensor_tensor(W_(5), W_(1), tim, ALU.mult), d2, wfree[5])
                p2 = pool(lambda e: e.tensor_tensor(W_(7), W_(3), tre, ALU.mult), d2)
                yield 2.5 * S5F
                d7 = dve(lambda e: e.tensor_tensor(W_(4), W_(4), W_(0), ALU.subtract), d6)
                p3 = pool(lambda e: e.tensor_tensor(W_(5), W_(5), W_(7), ALU.add), p2)
                tcr.give(ck, d6, p2)
                if i == 0:
                    yk, yb, yfree = Yr.take()
                    pe.wait(yfree)
                pe.quiet(lambda e: e.matmul(ps[32 * i:32 * i + 32, yb, :], cl[:, 0, s, :], W_(4), start=True, stop=False, tile_position=(0, 32 * i)), d7)
                t = pe(lambda e: e.matmul(ps[32 * i:32 * i + 32, yb, :], cl[:, 1, s, :], W_(5), start=False, stop=True, tile_position=(0, 32 * i)), p3)
                wfree[0], wfree[2] = [d7], [d2]
                wfree[1], wfree[3] = [p1, p2, d6], [p2, d6]
                wfree[4], wfree[5] = [t], [t]
                yield 1.5 * S5F
                if i == 3:
                    y = ysv[:, j, :]
                    t = dve(lambda e: e.scalar_tensor_tensor(out=y, in0=uT[:, j, :], scalar=V("s5d", j), in1=bank(yb), op0=ALU.mult, op1=ALU.add), t)
                    Yr.give(yk, t)
                    i_, q, sfree = sqr.take()
                    ta = act(lambda e: e.activation(q, y, ACT.Square), t, sfree)
                    t = dve(lambda e: e.tensor_scalar(q, q, 0.044715, 1.0, ALU.mult, ALU.add), ta)
                    t = dve(lambda e: e.tensor_tensor(q, q, y, ALU.mult), t)
                    ta = act(lambda e: e.activation(q, q, ACT.Tanh, scale=0.7978845608028654), t)
                    t = dve(lambda e: e.scalar_tensor_tensor(out=y, in0=q, scalar=1.0, in1=y, op0=ALU.add, op1=ALU.mult), ta)
                    sqr.give(i_, t)
                    t_y5[j] = t
                    yield 2.0 * S5F

        S5F = 1.6
        t_y5 = {}

        t_yf = {}

        def fox():
            Sr, Tr, Or = banks(5), banks(6), banks(7)
            pr = Ring([0, 1, 2, 3])
            pt_busy = []
            pe.wait([t_fq[m] for m in range(12)], t_fv, t_FT[0])
            for h in range(12):
                hp = (h % 2) * 64
                pend = []
                for n in range(4):
                    Wd = (n + 1) * 128
                    sk, b, free = Sr.take()
                    pe.wait(free)
                    pe.quiet(lambda e: e.matmul(ps[:, b, 0:Wd], yf[hp:hp + 64, h // 2, n * 128:(n + 1) * 128], kf[hp:hp + 64, h // 2, 0:Wd],
                                                start=True, stop=False))
                    pe.quiet(lambda e: e.matmul(ps[:, b, 0:Wd], ident[0:12, h:h + 1].to_broadcast([12, 128]), FT[:, 0:Wd], start=False, stop=False))
                    t = pe(lambda e: e.matmul(ps[:, b, n * 128:Wd], maskb[:, 0, :], maskb[:, 2, :], start=False, stop=True))
                    pk, pi, pfree = pr.take()
                    ta = softmax(ps[:, b, 0:Wd], Pf[:, pi, 0:Wd], smf[:, pi, :], 1.0, None, t, pfree)
                    Sr.give(sk, ta)
                    pend.append((pk, pi, ta, Wd))
                    yield 2.5
                    if n:
                        _, p1, ta1, W1 = pend[n - 1]
                        pend[n - 1] += (normalise(Pf[:, p1, 0:W1], smf[:, p1, :], False, ta1),)
                _, p1, ta1, W1 = pend[3]
                pend[3] += (normalise(Pf[:, p1, 0:W1], smf[:, p1, :], False, ta1),)
                yield 1.0
                t_pt = []
                for kb in range(4):
                    tk, b, free = Tr.take()
                    for n in range(kb, 4):
                        t = pe(lambda e: e.transpose(ps[:, b, n * 128:(n + 1) * 128], Pf[:, pend[n][1], kb * 128:(kb + 1) * 128], ident), free, pend[n][4])
                    if kb % 2:
                        t2 = dve(lambda e: e.tensor_copy(PTf[:, kb, kb * 128:L], ps[:, b, kb * 128:L]), t, pt_busy)
                    else:
                        t2 = act(lambda e: e.copy(PTf[:, kb, kb * 128:L], ps[:, b, kb * 128:L]), t, pt_busy)
                    Tr.give(tk, t2)
                    t_pt.append(t2)
                    yield 1.0
                for pk, pi, ta, Wd, tn in pend:
                    pr.give(pk, t)
                if h % 2 == 0:
                    ok, ob, free = Or.take()
                    pe.wait(free)
                pe.wait(t_pt)
                for kb in range(4):
                    t = pe(lambda e: e.matmul(ps[hp:hp + 64, ob, kb * 128:L], vf[:, kb, h * 64:(h + 1) * 64], PTf[:, kb, kb * 128:L],
                                              start=(kb == 0), stop=(kb == 3)))
                pt_busy = [t]
                yield 4.0
                if h % 2:
                    t1 = act(lambda e: e.copy(yf[:, h // 2, :], bank(ob)), t)
                    Or.give(ok, t1)
                    t_yf[h // 2] = t1

        hm = at("hm", [P, 8, LC], 122)
        HM, _, _ = pair("hm", 8, LC, 130)
        mk = at("mk", [P, 4, LC], 146)
        mv = at("mv", [P, 2, 512], 150)
        Pq = at("Pq", [P, 4, LC], 154)
        PTm = at("PTm", [P, 2, L], 158)
        smm = at("smm", [P, 4, 4], 162)
        mtmp = at("mtmp", [P, LC], 163)
        dm = Dma("s_mem")
        MS = float(128) ** -0.5
        t_ym = {}

        def memory():
            t_x = dm.start(act, hm[:, :, :], A["memT"], marks())
            m_ = marks()
            for e in (act, dve, pool):
                e.wait(m_)
            t_r = norm_T(lambda k: hm[:, k, :], 8, LC, t_x)
            yield 12.0
            tl = []
            for k in range(8):
                t = dve(lambda e: e.scalar_tensor_tensor(out=hm[:, k, :], in0=hm[:, k, :], scalar=V("gm", k), in1=rstd[:, 0:LC], op0=ALU.mult, op1=ALU.mult), t_r)
                tl.append(HM.put(k, hm[:, k, :], 0, LC, t))
            yield 5.0
            tq = []
            for m in range(4):
                (gk, pp, tok), = gemm("w_mk", m, 8, HM, [(0, LC)], tl)
                ta = act(lambda e: e.copy(mk[:, m, :], pp), tok)
                G.give(gk, ta)
                yield 3.0
                (gk, pp, tok2), = gemm("w_qm", m, 8, H, [(0, L)])
                ta2 = act(lambda e: e.copy(ym[:, m, :], pp), tok2)
                G.give(gk, ta2)
                tq += [ta, ta2]
                yield 5.5
            yield from tokmajor("w_mv", 2, HM, 2, lambda c: mv[:, c, :], tq)
            pe.wait(tq)
            Sr, Tr, Or = banks(5), banks(6), banks(7)
            pr = Ring([0, 1, 2, 3])
            ptb = []
            for h in range(4):
                pend = []
                for n in range(4):
                    sk, b, free = Sr.take()
                    t = pe(lambda e: e.matmul(ps[:, b, 0:LC], ym[:, h, n * 128:(n + 1) * 128], mk[:, h, :], start=True, stop=True), free)
                    pk, pi, pfree = pr.take()
                    ta = softmax(ps[:, b, 0:LC], Pq[:, pi, :], smm[:, pi, :], MS, None, t, pfree)
                    Sr.give(sk, ta)
                    pend.append((pk, pi, ta))
                    yield 1.5
                tn = [normalise(Pq[:, pi, :], smm[:, pi, :], False, ta) for pk, pi, ta in pend]
                t_pt = []
                for kb in range(2):
                    tk, b, free = Tr.take()
                    for n in range(4):
                        t = pe(lambda e: e.transpose(ps[:, b, n * 128:(n + 1) * 128], Pq[:, pend[n][1], kb * 128:(kb + 1) * 128], ident), free, tn[n])
                    t2 = act(lambda e: e.copy(PTm[:, kb, :], bank(b)), t, ptb)
                    Tr.give(tk, t2)
                    t_pt.append(t2)
                for pk, pi, ta in pend:
                    pr.give(pk, t)
                (gk, pp, tok), = gemm("w_gm", h, 8, H, [(0, L)])
                ok, ob, free = Or.take()
                pe.wait(free, t_pt)
                for kb in range(2):
                    t = pe(lambda e: e.matmul(bank(ob), mv[:, kb, h * 128:(h + 1) * 128], PTm[:, kb, :], start=(kb == 0), stop=(kb == 1)))
                ptb = [t]
                t1 = silu_gate(pp, tok, gk, bank(ob), ym[:, h, :], t)
                Or.give(ok, t1)
                t_ym[h] = t1
                yield 8.0

        t_gs = {}

        def glu():
            sg5 = Wk
            for m in range(6):
                (gk, pp, tok), = gemm("w_gs", m, 8, H, [(0, L)])
                i_, q, sfree = sqr.take()
                ta = act(lambda e: e.activation(q, pp, ACT.Tanh, scale=0.5), tok, sfree)
                t = dve(lambda e: e.scalar_tensor_tensor(out=uT[:, m, :], in0=q, scalar=1.0, in1=pp, op0=ALU.add, op1=ALU.mult), ta)
                G.give(gk, t)
                sqr.give(i_, t)
                t_gs[m] = t
                yield 5.5

        d5 = Dma("s_s5")
        m_ = marks()
        d5.start(sp, wkf[:, 0:768], A["s5b"][0], m_, t_spill)
        d5.start(sp, wkf[:, 768:1536], A["s5b"][1])
        d5.start(sp, cl[:, 0, :, :].rearrange("p a b -> p (a b)"), A["s5c"][0])
        t_d5[0] = d5.start(sp, cl[:, 1, :, :].rearrange("p a b -> p (a b)"), A["s5c"][1])
        s5_numbers()
        run(u_gemms())
        weave(s5_scan(), chain_of(fq_gemms(), tokmajor("w_fv", 3, H, 4, lambda c: vf[:, c, :], t_fv), forget(), fox(),
                                  gate_gemms("w_gf", range(6), lambda m: yf[:, m, :], t_yf), memory()))
        run(glu())
        fence()
        G = banks(0, 1, 2, 3, 4, 5, 6, 7)
        YS, _, _ = pair("ysp2", 6, L, 122)
        t_s = [YS.put(k, ysv[:, k, :], 0, L, lo=(dve if k % 2 else pool)) for k in range(6)]
        t5 = []
        Z5 = at("Z5", [P, 2, L], 218)
        z5r = Ring([0, 1])
        t_gl = []
        for m in range(6):
            (gk, pp, tok), = gemm("w_glu", m, 6, YS, [(0, L)], t_s)
            zk, zi, zfree = z5r.take()
            ta = act(lambda e: e.activation(Z5[:, zi, :], pp, ACT.Tanh, scale=0.25, bias=V("bglu", m)), tok, zfree)
            G.give(gk, ta)
            t = dve(lambda e: e.scalar_tensor_tensor(out=uT[:, m, :], in0=Z5[:, zi, :], scalar=1.0, in1=uT[:, m, :], op0=ALU.add, op1=ALU.mult), ta)
            z5r.give(zk, t)
            t = dve(lambda e: e.tensor_tensor(ysv[:, m, :], ysv[:, m, :], uT[:, m, :], ALU.mult), t)
            t_gl.append(t)
        last_glu = tok

        YF, _, _ = pair("yf2", 6, L, 146)
        YM, _, _ = pair("ym2", 4, L, 170)
        gt2 = at("gt2", [P, 6, L], 186)
        X2 = at("X2", [P, 8, L], 198)
        MP2, _, _ = pair("mp2", 8, L, 90)
        gr = Ring(list(range(6)))
        t_f = [YF.put(k, yf[:, k, :], 0, L, lo=(dve if k % 2 else pool)) for k in range(6)]
        fm = [t_gl, last_glu]
        t_s = [YS.put(k, ysv[:, k, :], 0, L, t_gl, last_glu, lo=(dve if k % 2 else pool)) for k in range(6)]
        t_mm = [YM.put(k, ym[:, k, :], 0, L, t_gl, lo=(dve if k % 2 else pool)) for k in range(4)]
        ready = {0: t_f, 1: t_s, 2: t_mm}
        t_x = Dma("s_x2").start(sp, X2[:, :, :], A["xsc"], t_gl)
        for i in range(6):
            gr.give(i, t_gl)
        t_m = []
        for m in range(8):
            tt = []
            for q, (wd, KT, src) in enumerate((("w_pf", 6, YF), ("w_ps", 6, YS), ("w_pm", 4, YM))):
                (gk, pp, tok), = gemm("w_gl", q * 8 + m, 8, H, [(0, L)])
                ik, i_, free = gr.take()
                ta = act(lambda e: e.activation(gt2[:, i_, :], pp, ACT.Tanh, scale=0.5, bias=V("bmerge", q * 8 + m)), tok, free)
                G.give(gk, ta)
                (gk, pp, tok), = gemm(wd, m, KT, src, [(0, L)], ready[q])
                t = dve(lambda e: e.scalar_tensor_tensor(out=gt2[:, i_, :], in0=gt2[:, i_, :], scalar=1.0, in1=pp, op0=ALU.add, op1=ALU.mult), tok, ta)
                G.give(gk, t)
                tt.append((ik, i_, t))
            a, b_, c_ = (x[1] for x in tt)
            t = dve(lambda e: e.tensor_tensor(gt2[:, a, :], gt2[:, a, :], gt2[:, c_, :], ALU.add), tt[0][2], tt[2][2])
            i_, s, free = sqr.take()
            t = dve(lambda e: e.scalar_tensor_tensor(out=s, in0=gt2[:, b_, :], scalar=0.25, in1=gt2[:, a, :], op0=ALU.mult, op1=ALU.add), t, tt[1][2], free)
            for ik, _, _ in tt:
                gr.give(ik, t)
            tt = MP2.put(m, s, 0, L, t, ready[0], ready[1], ready[2])
            sqr.give(i_, tt)
            t_m.append(tt)
        tx_ = []
        for m in range(8):
            (gk, pp, tok), = gemm("w_out2", m, 8, MP2, [(0, L)], t_m)
            t = dve(lambda e: e.scalar_tensor_tensor(out=X2[:, m, :], in0=pp, scalar=0.25, in1=X2[:, m, :], op0=ALU.mult, op1=ALU.add), tok, t_x)
            G.give(gk, t)
            tx_.append(t)
        t_r = norm_T(lambda k: X2[:, k, :], 8, L, tx_)
        dout = Dma("s_out")
        for k in range(8):
            t = dve(lambda e: e.scalar_tensor_tensor(out=X2[:, k, :], in0=X2[:, k, :], scalar=V("gf", k), in1=rstd[:, 0:L], op0=ALU.mult, op1=ALU.mult), t_r)
            t_out = dout.start(sp, out[:, k, :], X2[:, k, :], t)
        sp.wait(t_out)
        return W.asked


def kernel(**inputs):
    import numpy as _np
    import concourse.bacc as _bacc
    from concourse import mybir as _mybir
    from concourse.bass_utils import run_bass_kernel_spmd as _run

    I = {k: _np.asarray(v) for k, v in inputs.items()}
    arr = {}

    def blocks(w):
        k, n = w.shape
        return _np.ascontiguousarray(w.reshape(k // 128, 128, n // 128, 128).transpose(2, 1, 0, 3).reshape(n // 128, 128, k))

    def wide(w):
        k, n = w.shape
        return _np.ascontiguousarray(w.reshape(2, 4, 128, n // 256, 256).transpose(3, 0, 2, 1, 4).reshape(n // 256, 2, 128, 1024))

    def feat(x):
        t, n = x.shape
        return _np.ascontiguousarray(x.T.reshape(n // 128, 128, t).transpose(1, 0, 2))

    def cols(v):
        return v.reshape(-1, 128).T

    arr["xT"] = feat(I["x"][0])
    arr["ctxT"] = feat(I["ctx"][0])
    arr["memT"] = feat(I["mem_2"][0])
    arr["w_mod"] = blocks(I["w_mod"][0])
    w = I["w_in"][0]
    arr["w_z"] = blocks(w[:, 0:2048])
    arr["w_xbc"] = blocks(w[:, 2048:5120])
    arr["w_dt"] = _np.ascontiguousarray(w[:, 5120:5184].reshape(8, 128, 64).transpose(1, 0, 2).reshape(128, 512))
    arr["w_qk"] = blocks(w[:, 5184:6464])
    arr["w_v"] = wide(w[:, 6464:6720])
    arr["w_g"] = blocks(w[:, 6720:8768])
    arr["w_os"] = blocks(I["w_o_ssd"][0])
    arr["w_oa"] = blocks(I["w_o_att"][0])
    arr["w_out"] = blocks(I["w_out"][0])
    arr["w_up"] = blocks(I["w_up"][0])
    arr["w_down"] = blocks(I["w_down"][0])
    w = I["w_in_2"][0]
    arr["w_fqk"] = blocks(w[:, 0:1536])
    arr["w_fv"] = wide(w[:, 1536:2304])
    arr["w_fl"] = _np.ascontiguousarray(w[:, 2304:2316].reshape(8, 128, 12).transpose(1, 0, 2).reshape(128, 96))
    arr["w_gf"] = blocks(w[:, 2316:3084])
    arr["w_u"] = blocks(w[:, 3084:3852])
    arr["w_gs"] = blocks(w[:, 3852:4620])
    arr["w_qm"] = blocks(w[:, 4620:5132])
    arr["w_gm"] = blocks(w[:, 5132:5644])
    arr["w_gl"] = blocks(w[:, 5644:8716])
    w = I["w_mem_kv_2"][0]
    arr["w_mk"] = blocks(w[:, 0:512])
    arr["w_mv"] = wide(w[:, 512:1024])
    arr["w_glu"] = blocks(I["w_glu_2"][0])
    arr["w_pf"] = blocks(I["w_proj_fox_2"][0])
    arr["w_ps"] = blocks(I["w_proj_s5_2"][0])
    arr["w_pm"] = blocks(I["w_proj_mem_2"][0])
    arr["w_out2"] = blocks(I["w_out_2"][0])
    cw, fw = I["ssd_conv_w"][0], I["ffn_conv_w"][0]
    cc = _np.stack([I["c"][0], I["c_ctx"]], axis=-1)
    vec = {
        "bmod": cols(I["b_mod"][0]), "g1": cols(I["norm1_g"][0]), "g2": cols(I["norm2_g"][0]),
        "cw0": cols(cw[0]), "cw1": cols(cw[1]), "cw2": cols(cw[2]), "cb": cols(I["ssd_conv_b"][0]),
        "sg": cols(I["ssd_norm_g"][0]), "fw0": cols(fw[0]), "fw1": cols(fw[1]), "fw2": cols(fw[2]),
        "fb": cols(I["ffn_conv_b"][0]), "fg": cols(I["final_g"]), "gn": cols(I["g_norm_2"][0]),
        "gm": cols(I["g_mem_norm_2"][0]), "gf": cols(I["g_final_2"]), "bmerge": cols(I["b_merge_2"][0]),
        "bglu": cols(I["b_glu_2"][0]), "s5d": cols(I["s5_d_2"][0]), "lre": cols(I["lam_re_2"][0]),
        "lim": cols(I["lam_im_2"][0]), "lstep": cols(_np.repeat(I["log_step_2"][0], 64)),
        "dsk": cols(_np.repeat(I["ssd_d"][0], 64)),
        "c": cc.reshape(8, 128, 2).transpose(1, 0, 2).reshape(128, 16),
    }
    arr["vecs"] = _np.ascontiguousarray(_np.concatenate([vec[n] for n, _ in VECS], axis=1))
    r = _np.concatenate([I["ssd_dt_bias"][0].reshape(-1), I["ssd_a_log"][0].reshape(-1), I["att_sink"][0], I["b_forget_2"][0]])
    arr["rows"] = _np.ascontiguousarray(_np.broadcast_to(r, (128, r.size)))
    sb_ = _np.zeros((2, 2, 64, 24, 2, 16), _np.float32)
    sc_ = _np.zeros((2, 2, 64, 24, 2, 16), _np.float32)
    for q, (bn, cn) in enumerate((("s5_b_re_2", "s5_c_re_2"), ("s5_b_im_2", "s5_c_im_2"))):
        b4 = I[bn][0].reshape(24, 2, 64, 16)
        c4 = I[cn][0].reshape(24, 2, 16, 64)
        for par in (0, 1):
            sb_[q, par, :, :, par, :] = b4[:, par].transpose(1, 0, 2)
            sc_[q, par, :, :, par, :] = c4[:, par].transpose(2, 0, 1)
    arr["s5b"] = sb_.reshape(2, 128, 768)
    arr["s5c"] = sc_.reshape(2, 128, 768)
    i = _np.arange(128)
    a, b = i[:, None], i[None, :]
    f = _np.float32
    inv = (f(10000.0) ** (-_np.arange(0, 32, 2, dtype=f) / f(32))).astype(f)
    t = _np.arange(512)
    dd = i % 64
    pos = _np.where((dd // 32 == 0)[:, None], (t // 64)[None], (t % 64)[None]).astype(f)
    ang = (pos * inv[dd % 16][:, None]).astype(f).astype(_np.float64)
    sgn = _np.where(dd % 32 < 16, -1.0, 1.0)[:, None]
    arr["consts"] = _np.concatenate([
        a == b, a <= b, a >= b, a == (b ^ 16), _np.where(b >= a, 0.0, -1e30), _np.where(b <= a, 0.0, -1e30),
        _np.ones((128, 128)), _np.cos(ang), sgn * _np.sin(ang)], axis=1).astype(f)

    def build(order):
        nc = _bacc.Bacc("TRN2", target_bir_lowering=False, num_devices=1, dynamic_dma_scratch_size=256)
        A = {}
        for name, x in arr.items():
            A[name] = nc.dram_tensor(f"in_{name}", x.shape, _mybir.dt.float32, kind="ExternalInput").ap()
        for name, shape in (("csd", (2, 32, 512)), ("xsc", (128, 8, 512)), ("ysc", (2, 128, 16, 512))):
            A[name] = nc.dram_tensor(name, shape, _mybir.dt.float32, kind="Internal").ap()
        out = nc.dram_tensor("out_0", (128, 8, 512), _mybir.dt.float32, kind="ExternalOutput").ap()
        return nc, fused_blocks(nc, A, out, order)

    _, order = build([])
    nc, _ = build(order)
    r = _run(nc, [{f"in_{k}": v for k, v in arr.items()}], core_ids=[0])
    y = r.results[0]["out_0"]
    return _np.ascontiguousarray(y.transpose(2, 1, 0).reshape(1, 512, 1024))
```

```python
from contextlib import ExitStack

import numpy as np

import concourse.bass as bass
from concourse import mybir

ALU = mybir.AluOpType
ACT = mybir.ActivationFunctionType
F32 = mybir.dt.float32
F32R = mybir.dt.float32r
BF16 = mybir.dt.bfloat16
AXX = mybir.AxisListType.X

P = 128
EPS = 1e-6
L = 512
LC = 256
LT = L + LC
LOOK = 2

VECS = [("bmod", 48), ("g1", 8), ("g2", 8), ("cw0", 24), ("cw1", 24), ("cw2", 24), ("cb", 24),
        ("sg", 16), ("fw0", 44), ("fw1", 44), ("fw2", 44), ("fb", 44), ("fg", 8), ("gn", 8),
        ("gm", 8), ("gf", 8), ("bmerge", 24), ("bglu", 6), ("s5d", 6), ("lre", 24), ("lim", 24),
        ("lstep", 24), ("dsk", 16), ("c", 16), ("bfc", 1)]
VOFF = {}
_o = 0
for _n, _k in VECS:
    VOFF[_n] = (_o, _k)
    _o += _k
NVEC = _o
ROWS = [("dtb", 64), ("alog", 64), ("sink", 16), ("bfor", 12)]
CONSTS = [("ident", 128), ("trif", 128), ("trib", 128), ("perm", 128), ("ml", 128), ("mr", 128),
          ("ones", 128), ("cos", 512), ("sin", 512)]


class Engine:

    def __init__(self, eng, sem):
        self.eng, self.sem, self.n, self.seen = eng, sem, 0, {}

    def wait(self, *toks):
        for t in toks:
            if t is None:
                continue
            if isinstance(t, (list, tuple)) and not (len(t) == 2 and isinstance(t[1], int)):
                self.wait(*t)
                continue
            s, v = t
            if self.seen.get(id(s), 0) < v:
                self.seen[id(s)] = v
                self.eng.wait_ge(s, v)

    def __call__(self, fn, *toks):
        self.wait(*toks)
        self.n += 1
        fn(self.eng).then_inc(self.sem, 1)
        return (self.sem, self.n)

    def quiet(self, fn, *toks):
        self.wait(*toks)
        fn(self.eng)

    def last(self):
        return (self.sem, self.n)


class Ring:

    def __init__(self, slots):
        self.slots, self.free, self.i = slots, [[] for _ in slots], 0

    def take(self):
        k = self.i % len(self.slots)
        self.i += 1
        return k, self.slots[k], self.free[k]

    def give(self, k, *toks):
        self.free[k] = list(toks)


class Weights:

    def __init__(self, order, src, sp, act, raw, dmas, hi, lo):
        self.order, self.src, self.sp, self.act = order, src, sp, act
        self.raw, self.dmas, self.hi, self.lo = raw, dmas, hi, lo
        self.asked, self.loaded, self.made, self.at = [], {}, {}, 0
        self.sub = None

    def load(self, p):
        key, n, split = self.order[p]
        k, ap, free = self.raw.take()
        self.loaded[p] = (k, ap[:, 0:n], self.dmas[k].start(self.sp, ap[:, 0:n], self.src(key), free))
        if not split:
            self.made[p] = (self.raw, k, ap[:, 0:n], None, self.loaded[p][2])

    def split(self, p):
        k, w, t = self.loaded[p]
        n = self.order[p][1]
        j, (h, l), hfree = self.hi.take()
        th = self.act(lambda e: e.copy(h[:, 0:n], w), t, hfree)
        tl = self.sub(lambda e: e.tensor_tensor(l[:, 0:n], w, h[:, 0:n].bitcast(F32), ALU.subtract), t, th, hfree)
        self.raw.give(k, th, tl)
        self.made[p] = (self.hi, j, h[:, 0:n], l[:, 0:n], (th, tl))

    def next(self, key, n, split, held=0):
        self.asked.append((key, n, split))
        q = self.at
        self.at += 1
        if q >= len(self.order):
            self.order.append((key, n, split))
        assert self.order[q] == (key, n, split)
        end = len(self.order)
        for p in range(q, min(q + LOOK + 6 - held, end)):
            if p not in self.loaded:
                old = p - len(self.raw.slots)
                if old >= 0 and not (old < q and (old in self.made)) and not (self.order[old][2] and old in self.made):
                    break
                self.load(p)
            if self.order[p][2] and p not in self.made and p <= q + LOOK - held:
                self.split(p)
        return self.made[q]


def weave(totals, key, *tasks):
    sums = [0.0] * len(tasks)
    whole = totals.get(key, [1.0] * len(tasks))
    live = [[0.0, i, t] for i, t in enumerate(tasks)]
    while live:
        live.sort(key=lambda x: (x[0], x[1]))
        x = live[0]
        try:
            c = next(x[2])
            sums[x[1]] += c
            x[0] += c / whole[x[1]]
        except StopIteration:
            live.remove(x)
    totals[key] = sums


def chain_of(*gens):
    for g in gens:
        yield from g


def alternate(*gens):
    live = list(gens)
    while live:
        for g in list(live):
            try:
                yield next(g)
            except StopIteration:
                live.remove(g)


def run(gen):
    for _ in gen:
        pass


def fused_blocks(nc, A, out, order, totals):
    ctx = ExitStack()
    with ctx:
        def at(name, shape, kb, dt=F32):
            return nc.alloc_sbuf_tensor_at(name, shape, dt, offset=384 + int(kb * 1024))

        cursor = [40 * 1024]

        def small_at(name, shape, dt=F32):
            n = int(np.prod(shape[1:])) * (2 if dt == BF16 else 4)
            o = cursor[0]
            cursor[0] += (n + 31) // 32 * 32
            assert cursor[0] <= 50 * 1024
            return nc.alloc_sbuf_tensor_at(name, shape, dt, offset=384 + o)

        def sem(name):
            return ctx.enter_context(nc.semaphore(name))

        ps = ctx.enter_context(nc.psum_tensor("ps", [P, 8, 512], F32))

        def bank(b):
            return ps[:, b, :]

        pe = Engine(nc.tensor, sem("s_pe"))
        dve = Engine(nc.vector, sem("s_dve"))
        act = Engine(nc.scalar, sem("s_act"))
        pool = Engine(nc.gpsimd, sem("s_pool"))
        sp = Engine(nc.sync, sem("s_sp"))

        class Dma:

            def __init__(self, name):
                self.sem, self.n = sem(name), 0

            def start(self, eng, dst, src, *toks):
                eng.wait(*toks)
                self.n += 16
                eng.eng.dma_start(dst, src).then_inc(self.sem, 16)
                return (self.sem, self.n)

        def marks():
            return [e.last() for e in (pe, dve, act, pool)]

        def fence():
            m = marks()
            for e in (pe, dve, act, pool):
                e.wait(m)
            return m

        def banks(*b):
            r = Ring(list(b))
            m = marks()
            for i in range(len(b)):
                r.give(i, m)
            return r

        raww = at("raww", [P, 4, 1024], 0)
        whi = at("whi", [P, 3, 1024], 16, F32R)
        wlo = at("wlo", [P, 3, 1024], 28, F32R)

        def wsrc(key):
            name, m, a, b = key
            return A[name][m, :, a:b] if len(A[name].shape) == 3 else A[name][:, a:b] if len(A[name].shape) == 2 else A[name][m[0], m[1], :, a:b]

        W = Weights(order, wsrc, sp, act, Ring([raww[:, i, :] for i in range(4)]), [Dma(f"s_w{i}") for i in range(4)],
                    Ring([(whi[:, i, :], wlo[:, i, :]) for i in range(3)]), None)
        W.sub = pool

        G = banks(0, 1, 2)

        class Pair:

            def __init__(self, hi, lo):
                self.hi, self.lo = hi, lo

            def put(self, k, v, t0, t1, *toks, hi=None, lo=None):
                h = (hi or act)(lambda e: (e.copy if e is nc.scalar else e.tensor_copy)(self.hi(k)[:, t0:t1], v), *toks)
                l = (lo or pool)(lambda e: e.tensor_tensor(self.lo(k)[:, t0:t1], v, self.hi(k)[:, t0:t1].bitcast(F32), ALU.subtract), h, *toks)
                return [h, l]

        def pair(name, n, T, kb, kb2=None):
            h = at(name + "_h", [P, n, T], kb, F32R)
            l = at(name + "_l", [P, n, T], kb + n * T / 256 if kb2 is None else kb2, F32R)
            return Pair(lambda k: h[:, k, :], lambda k: l[:, k, :]), h, l

        def gemm(wd, m, KT, rhs, ranges, *waits, tiles=None):
            res, toks = [], {}
            pe.wait(*waits)
            for (t0, t1) in ranges:
                gk, b, free = G.take()
                res.append((gk, ps[:, b, 0:t1 - t0], free))
            for k0 in range(0, KT, 8):
                kk = min(8, KT - k0)
                ring, slot, wh, wl, tw = W.next((wd, m, k0 * 128, (k0 + kk) * 128), kk * 128, True)
                pe.wait(tw)
                for (t0, t1), (gk, o, free) in zip(ranges, res):
                    pe.wait(free)
                    for k in range(k0, k0 + kk):
                        c = slice((k - k0) * 128, (k - k0 + 1) * 128)
                        xh, xl = rhs.hi(k)[:, t0:t1], rhs.lo(k)[:, t0:t1]
                        if tiles:
                            pe.wait(tiles[k])
                        pe.quiet(lambda e: e.matmul(o, wh[:, c], xh, start=(k == 0), stop=False))
                        pe.quiet(lambda e: e.matmul(o, wh[:, c], xl, start=False, stop=False))
                        f = lambda e: e.matmul(o, wl[:, c], xh, start=False, stop=(k == KT - 1))
                        if k == k0 + kk - 1:
                            tok = pe(f)
                        else:
                            pe.quiet(f)
                    toks[t0] = tok
                ring.give(slot, tok)
            return [(gk, o, toks[t0]) for (t0, _), (gk, o, _) in zip(ranges, res)]

        vc = small_at("vc", [P, NVEC])
        rows = small_at("rows", [P, 156])
        cst = small_at("cst", [P, 896])
        maskb = small_at("maskb", [P, 3, 128], BF16)
        cs_ = small_at("cs_", [P, 16])
        tmp16 = small_at("tmp16", [P, 16])
        modS = small_at("modS", [P, 48, 2])
        A1 = small_at("A1", [P, 8, 2])
        A2 = small_at("A2", [P, 8])
        pk_ = small_at("pk_", [P, 17, 24])
        dc = Dma("s_c")
        dx = Dma("s_x")
        t_vc = dc.start(sp, vc[:, :], A["vecs"])

        def V(name, i=0, n=None):
            o, k = VOFF[name]
            return vc[:, o + i:o + i + (n or 1)]

        def C(name):
            return cst[:, ["ident", "trif", "trib", "perm", "ml", "mr", "ones"].index(name) * 128:][:, 0:128]

        ident, ones = C("ident"), C("ones")

        acc = at("acc", [P, L], 50)
        rstd = at("rstd", [P, L], 52)
        sq = at("sq", [P, 2, L], 54)
        sqr = Ring([sq[:, 0, :], sq[:, 1, :]])

        summed = {}

        def norm_add(k, x, T, acc, sqr, *in_toks):
            i, s, free = sqr.take()
            ta = act(lambda e: e.activation(s[:, 0:T], x[:, 0:T], ACT.Square), free, in_toks)
            if k == 0:
                t = dve(lambda e: e.tensor_copy(acc[:, 0:T], s[:, 0:T]), ta)
            else:
                t = dve(lambda e: e.tensor_tensor(acc[:, 0:T], acc[:, 0:T], s[:, 0:T], ALU.add), ta, summed[id(acc)])
            summed[id(acc)] = t
            sqr.give(i, t)
            return t

        def norm_sum(X, KT, T, acc, sqr, *in_toks):
            for k in range(KT):
                t = norm_add(k, X(k), T, acc, sqr, *in_toks)
            return t

        def norm_rstd(ranges, tacc, inv, acc, rstd, tmps):
            tr = []
            for (t0, t1) in ranges:
                gk, b, free = G.take()
                tm = pe(lambda e: e.matmul(ps[:, b, 0:t1 - t0], ones, acc[:, t0:t1], start=True, stop=True), free, tacc)
                t = dve(lambda e: e.tensor_scalar(rstd[:, t0:t1], ps[:, b, 0:t1 - t0], inv, EPS, ALU.mult, ALU.add), tm)
                G.give(gk, t)
                v, r, w = rstd[:, t0:t1], tmps[0][:, t0:t1], tmps[1][:, t0:t1]
                ta = act(lambda e: e.activation(r, v, ACT.Sqrt), t)
                t = dve(lambda e: e.reciprocal(r, r), ta)
                t = dve(lambda e: e.tensor_tensor(w, r, r, ALU.mult), t)
                t = dve(lambda e: e.tensor_tensor(w, w, v, ALU.mult), t)
                t = dve(lambda e: e.tensor_scalar(w, w, -0.5, 1.5, ALU.mult, ALU.add), t)
                t = dve(lambda e: e.tensor_tensor(v, r, w, ALU.mult), t)
                tr.append(t)
            return tr

        def rstd_of(KT, T, t):
            tr = norm_rstd([(0, T)], t, 1.0 / (KT * 128), acc, rstd, (sq[:, 0, :], sq[:, 1, :]))
            sqr.give(0, tr)
            sqr.give(1, tr)
            return tr

        HP, hh, hl = pair("hT", 8, LT, 58)
        xin = at("xin", [P, 8, LT], 106)
        acc1 = at("acc1", [P, LT], 136)
        rstd1 = at("rstd1", [P, LT], 139)
        sq1 = at("sq1", [P, 2, LT], 142)
        hv = at("hv", [P, 2, LT], 148)
        dx.start(sp, xin[:, :, 0:L], A["xT"])
        t_hx = dx.start(sp, xin[:, :, L:LT], A["ctxT"])
        dc.start(sp, rows[:, :], A["rows"])
        t_cst = dc.start(sp, cst[:, :], A["consts"][:, 0:896])
        for e in (pe, dve, act, pool):
            e.wait(t_cst)
        dve(lambda e: e.tensor_copy(maskb[:, 0, :], ident))
        t_mb = dve(lambda e: e.tensor_copy(maskb[:, 1:3, :].rearrange("p a b -> p (a b)"), cst[:, 512:768]))
        pe.wait(t_mb)
        ta = act(lambda e: e.activation(tmp16[:, :], V("c", 0, 16), ACT.Tanh, scale=0.5))
        t = dve(lambda e: e.scalar_tensor_tensor(out=cs_[:, :], in0=tmp16[:, :], scalar=1.0, in1=V("c", 0, 16), op0=ALU.add, op1=ALU.mult), ta)
        t_c = dve(lambda e: e.tensor_scalar(cs_[:, :], cs_[:, :], 0.5, None, ALU.mult), t)
        for nm in ("cw0", "cw1", "cw2", "cb"):
            dve(lambda e: e.tensor_scalar(V(nm, 0, 24), V(nm, 0, 24), 0.5, None, ALU.mult))
        for nm in ("fw0", "fw1", "fw2", "fb"):
            dve(lambda e: e.tensor_scalar(V(nm, 0, 22), V(nm, 0, 22), 0.5, None, ALU.mult))
        t_vh = dve(lambda e: e.tensor_scalar(V("bmerge", 0, 24), V("bmerge", 0, 24), 0.5, None, ALU.mult))
        t_vh = dve(lambda e: e.tensor_scalar(V("bglu", 0, 6), V("bglu", 0, 6), 0.5, None, ALU.mult))
        act.wait(t_vh)

        def mod_blocks(ms):
            per = 1
            for ma in ms:
                gk, b, free = G.take()
                pe.wait(free, t_c)
                for m in range(ma, ma + per):
                    ring, slot, w, _, tw = W.next(("w_mod", m, 0, 1024), 1024, False)
                    pe.wait(tw)
                    for k in range(8):
                        f = lambda e: e.matmul(ps[:, b, 2 * (m - ma):2 * (m - ma) + 2], w[:, k * 128:(k + 1) * 128],
                                               cs_[:, 2 * k:2 * k + 2], start=(k == 0), stop=(k == 7))
                        t = pe(f) if k == 7 else pe.quiet(f)
                    ring.give(slot, t)
                o = VOFF["bmod"][0]
                t = dve(lambda e: e.tensor_tensor(modS[:, ma:ma + per, :], ps[:, b, 0:2 * per].rearrange("p (m s) -> p m s", s=2),
                                                  vc[:, o + ma:o + ma + per].unsqueeze(2).to_broadcast([P, per, 2]), ALU.add), t)
                G.give(gk, t)
                t_mod[0] = t
                yield 0.3

        t_mod = [None]
        t = norm_sum(lambda k: xin[:, k, :], 8, LT, acc1, Ring([sq1[:, 0, :], sq1[:, 1, :]]), t_hx)
        t_r = norm_rstd([(0, L), (L, LT)], t, 1.0 / 1024, acc1, rstd1, (sq1[:, 0, :], sq1[:, 1, :]))
        hvr = Ring([hv[:, 0, :], hv[:, 1, :]])
        for k in range(8):
            t_xn = dve(lambda e: e.tensor_tensor(xin[:, k, :], xin[:, k, :], rstd1[:, :], ALU.mult), t_r)
        t_h = []
        for k in range(8):
            run(mod_blocks((k, 8 + k)))
            t = dve(lambda e: e.scalar_tensor_tensor(out=A1[:, k, :], in0=modS[:, 8 + k, :], scalar=1.0, in1=V("g1", k).to_broadcast([P, 2]),
                                                     op0=ALU.add, op1=ALU.mult), t_mod[0])
            i, v, free = hvr.take()
            dve(lambda e: e.tensor_scalar(v[:, 0:L], xin[:, k, 0:L], A1[:, k, 0:1], modS[:, k, 0:1], ALU.mult, ALU.add), t, t_xn, free)
            t = dve(lambda e: e.tensor_scalar(v[:, L:LT], xin[:, k, L:LT], A1[:, k, 1:2], modS[:, k, 1:2], ALU.mult, ALU.add))
            tt = HP.put(k, v, 0, LT, t, lo=dve)
            hvr.give(i, tt)
            t_h.append(tt)
        pe.wait(t_h)

        def softplus(x, u, w, n):
            t = dve(lambda e: e.scalar_tensor_tensor(out=u, in0=x, scalar=-1.0, in1=x, op0=ALU.mult, op1=ALU.max), dve.last())
            t = act(lambda e: e.activation(u, u, ACT.Exp, scale=-1.0), t)
            t1 = dve(lambda e: e.tensor_scalar(w, u, 1.0, None, ALU.add), t)
            ta = act(lambda e: e.activation(n, w, ACT.Ln), t1)
            t = dve(lambda e: e.scalar_tensor_tensor(out=u, in0=w, scalar=-1.0, in1=u, op0=ALU.add, op1=ALU.subtract), t1)
            t = dve(lambda e: e.reciprocal(w, w), t, ta)
            t = dve(lambda e: e.scalar_tensor_tensor(out=u, in0=u, scalar=-1.0, in1=w, op0=ALU.mult, op1=ALU.mult), t)
            t = dve(lambda e: e.tensor_tensor(u, u, n, ALU.add), t, ta)
            return dve(lambda e: e.scalar_tensor_tensor(out=x, in0=x, scalar=0.0, in1=u, op0=ALU.max, op1=ALU.add), t)

        xsl = [at(f"xsl{i}", [P, 4, L], 106 + 13 * i) for i in (0, 1)]
        BTs = [at(f"BTs{i}", [P, LT], 114 + 13 * i) for i in (0, 1)]
        CTs = [at(f"CTs{i}", [P, L], 117 + 13 * i) for i in (0, 1)]
        xsc_ = at("xsc_", [P, 4, LC], 132)
        xtok = at("xtok", [P, 6, 512], 136)
        Btok = at("Btok", [P, 6, 128], 148)
        st = at("st", [P, 2, 4, 512], 151)
        st0 = at("st0", [P, 512], 167)
        stt_ = at("stt_", [P, 512], 169)
        csbc = at("csbc", [P, 3, 8, 128], 171)
        cbm = at("cbm", [P, 2, 128], 183)
        Ew = at("Ew", [P, 3, 8, 128], 184)
        Cs = at("Cs", [P, 2, 8, 128], 196)
        xw = at("xw", [P, 2, 512], 204)
        yg = at("yg", [P, 4, L], 208)
        dt_ = at("dt_", [P, 6, 64], 216)
        la = at("la", [P, 6, 64], 217.5)
        csm = at("csm", [P, 6, 64], 219)
        wdec = at("wdec", [P, 6, 64], 220.5)
        etot = at("etot", [P, 6, 64], 222)
        csT = at("csT", [64, L], 167)
        csd = A["csd"]

        flat = lambda x: x[:, :, :].rearrange("p a b -> p (a b)")
        dtT = at("dtT", [64, LT], 151)
        pv = lambda b: ps[:, b, 0:384].rearrange("p (c h) -> p c h", h=64)
        t_csd = [None]
        dbc = [Dma(f"s_bc{i}") for i in range(3)]

        def narrow(key, n, M, rhs, ranges, out):
            ring, slot, wh, wl, wt = W.next(key, n, True)
            tt = []
            for (t0, t1) in ranges:
                gk, b, free = G.take()
                pe.wait(free, wt)
                o = ps[0:M, b, 0:t1 - t0]
                for k in range(8):
                    c = slice(k * M, (k + 1) * M)
                    pe.quiet(lambda e: e.matmul(o, wh[:, c], rhs.hi(k)[:, t0:t1], start=(k == 0), stop=False))
                    pe.quiet(lambda e: e.matmul(o, wh[:, c], rhs.lo(k)[:, t0:t1], start=False, stop=False))
                    f = lambda e: e.matmul(o, wl[:, c], rhs.hi(k)[:, t0:t1], start=False, stop=(k == 7))
                    t = pe(f) if k == 7 else pe.quiet(f)
                tt.append(out(t0, t1, o, t))
                G.give(gk, tt[-1])
            ring.give(slot, t)
            return tt

        def step_sizes():
            tt = narrow(("w_dt", 0, 0, 512), 512, 64, HP, [(0, L), (L, LT)], lambda t0, t1, o, t: act(lambda e: e.copy(dtT[:, t0:t1], o), t))
            yield 8.0
            for c in range(6):
                t = pe(lambda e: e.transpose(ps[:, 4, c * 64:c * 64 + 64], dtT[:, c * 128:c * 128 + 128], ident[0:64, 0:64]), tt)
            t = dve(lambda e: e.tensor_tensor(dt_[:, :, :], pv(4), rows[:, 0:64].unsqueeze(1).to_broadcast([P, 6, 64]), ALU.add), t)
            ta = act(lambda e: e.activation(rows[:, 64:128], rows[:, 64:128], ACT.Exp))
            t_dt = softplus(flat(dt_), flat(csm), flat(wdec), flat(etot))
            t = dve(lambda e: e.scalar_tensor_tensor(out=la[:, :, :], in0=dt_[:, :, :], scalar=-1.0,
                                                     in1=rows[:, 64:128].unsqueeze(1).to_broadcast([P, 6, 64]), op0=ALU.mult, op1=ALU.mult), t_dt, ta)
            yield 8.0
            pe.quiet(lambda e: e.matmul(pv(5)[:, :, 0:32], C("trif"), la[:, :, 0:32], start=True, stop=True), t)
            t1 = pe(lambda e: e.matmul(pv(6)[:, :, 32:64], C("trib"), la[:, :, 32:64], start=True, stop=True))
            t2 = pe(lambda e: e.matmul(pv(7), ones, la[:, :, :], start=True, stop=True))
            dve(lambda e: e.tensor_copy(csm[:, :, 0:32], pv(5)[:, :, 0:32]), t1)
            t = dve(lambda e: e.tensor_copy(csm[:, :, 32:64], pv(6)[:, :, 32:64]))
            t = dve(lambda e: e.tensor_tensor(wdec[:, :, :], pv(7), csm[:, :, :], ALU.subtract), t2, t)
            te = act(lambda e: e.activation(etot[:, :, :], pv(7), ACT.Exp), t2, t)
            t = dve(lambda e: e.tensor_scalar(flat(wdec), flat(wdec), 0.0, None, ALU.min), t)
            ta = act(lambda e: e.activation(wdec[:, :, :], wdec[:, :, :], ACT.Exp), t)
            t_wd = dve(lambda e: e.tensor_tensor(wdec[:, :, :], wdec[:, :, :], dt_[:, :, :], ALU.mult), ta)
            yield 8.0
            for c in range(4):
                t = pe(lambda e: e.transpose(ps[0:64, 3, c * 128:c * 128 + 128], csm[:, c, :], ident), t_wd)
            t_ct = dve(lambda e: e.tensor_copy(csT[:, :], ps[0:64, 3, :]), t)
            t_csd[0] = Dma("s_csd").start(act, csd.rearrange("d h t -> (d h) t"), csT[:, :], t_ct)
            pool.wait(t_wd, te)
            pe.wait(t_wd)
            dve.wait(te)
            yield 8.0

        def conv(psum, T, m, names, dst, *toks):
            w0, w1, w2, bb = (V(n, m) for n in names)
            t = act(lambda e: e.activation(dst, psum, ACT.Identity, bias=bb, scale=w1), toks)
            t = dve(lambda e: e.scalar_tensor_tensor(out=dst[:, 1:T], in0=psum[:, 0:T - 1], scalar=w0, in1=dst[:, 1:T],
                                                     op0=ALU.mult, op1=ALU.add), t)
            return dve(lambda e: e.scalar_tensor_tensor(out=dst[:, 0:T - 1], in0=psum[:, 1:T], scalar=w2, in1=dst[:, 0:T - 1],
                                                        op0=ALU.mult, op1=ALU.add), t)

        CW = ("cw0", "cw1", "cw2", "cb")
        xwr = Ring([xw[:, 0, :], xw[:, 1, :]])
        bcr = Ring([0, 1, 2])
        tx = {}
        busy = {"x": {0: [], 1: []}, "xc": [], "xtok": [], "Btok": [], "st": [], "y": [], "E": [[], []], "E2": [], "C": [], "cbm": []}
        dy = Dma("s_y")
        acc_tok = [None]
        t_yz = {}
        gated = {}

        def xbc(g):
            q = g % 2
            for i in range(6):
                m = [g * 4 + 0, g * 4 + 1, g * 4 + 2, g * 4 + 3, 16 + g, 20 + g][i]
                rng = [(0, L), (L, LT)] if i < 5 else [(0, L)]
                outs = gemm("w_xbc", m, 8, HP, rng)
                yield 8.5 if i < 5 else 5.5
                tt = []
                for (t0, t1), (gk, pp, tok) in zip(rng, outs):
                    if i < 4:
                        dst = xsl[q][:, i, :] if t0 == 0 else xsc_[:, i, :]
                    elif i == 4:
                        dst = BTs[q][:, t0:t1]
                    else:
                        dst = CTs[q][:, :]
                    t = conv(pp, t1 - t0, m, CW, dst, tok, busy["x"][q], busy["xc"] if (i < 4 and t0) else None)
                    G.give(gk, t)
                    i_, s, free = sqr.take()
                    s = s[:, 0:t1 - t0]
                    ta = act(lambda e: e.activation(s, dst, ACT.Tanh), t, free)
                    t = dve(lambda e: e.scalar_tensor_tensor(out=dst, in0=s, scalar=1.0, in1=dst, op0=ALU.add, op1=ALU.mult), ta)
                    sqr.give(i_, t)
                    tt.append(t)
                tx[(g, i)] = tt

        def zgate(g):
            for j in range(4):
                m = 4 * g + j
                (gk, pp, tok), = gemm("w_z", m, 8, HP, [(0, L)])
                yield 5.5
                i_, s, free = sqr.take()
                ta = act(lambda e: e.activation(s, pp, ACT.Tanh, scale=0.5), tok, free)
                t1 = dve(lambda e: e.scalar_tensor_tensor(out=s, in0=s, scalar=1.0, in1=pp, op0=ALU.add, op1=ALU.mult), ta)
                G.give(gk, t1)
                t1 = dve(lambda e: e.tensor_tensor(yg[:, j, :], yg[:, j, :], s, ALU.mult), t1, t_yz[g])
                ta = act(lambda e: e.activation(s, yg[:, j, :], ACT.Square), t1)
                if m == 0:
                    acc_tok[0] = dve(lambda e: e.tensor_copy(acc[:, 0:L], s), ta)
                else:
                    acc_tok[0] = dve(lambda e: e.tensor_tensor(acc[:, 0:L], acc[:, 0:L], s, ALU.add), ta, acc_tok[0])
                sqr.give(i_, acc_tok[0])
                t = act(lambda e: e.activation(yg[:, j, :], yg[:, j, :], ACT.Copy, scale=V("sg", m)), ta)
                gated[g] = j + 1
                busy["y"] = [dy.start(act, A["ysc"][:, m, :], yg[:, j, :], t)]

        def ssd_group(g):
            q = g % 2
            xs, BT, CT = xsl[q], BTs[q], CTs[q]
            xcols = lambda j, c: xs[:, j, c * 128:(c + 1) * 128] if c < 4 else xsc_[:, j, (c - 4) * 128:(c - 3) * 128]
            loads = {}

            def load_cs(c, d):
                bk, bb, bfree = bcr.take()
                t_b = dbc[bk].start(act, csbc[:, bb, :, :],
                                    csd[d, g * 8:g * 8 + 8, c * 128:(c + 1) * 128].unsqueeze(0).to_broadcast([P, 8, 128]), bfree, t_csd[0])
                loads[(c, d)] = (bk, bb, t_b)

            load_cs(0, 0)
            load_cs(0, 1)
            t_xt = {}
            for c in (4, 5, 0, 1, 2, 3):
                ik, b, free = Tb.take()
                for j in range(4):
                    t = pe(lambda e: e.transpose(ps[:, b, j * 128:(j + 1) * 128], xcols(j, c), ident), free, tx[(g, j)])
                if c % 2:
                    t = dve(lambda e: e.tensor_copy(xtok[:, c, :], bank(b)), t, busy["xtok"])
                else:
                    t = act(lambda e: e.copy(xtok[:, c, :], bank(b)), t, busy["xtok"])
                Tb.give(ik, t)
                t_xt[c] = t
                if c == 5:
                    busy["xc"] = [t_xt[4], t_xt[5]]
                    yield 1.5
            yield 3.0
            for c0, c1 in ((0, 4), (4, 6)):
                ik, b, free = Tb.take()
                for c in range(c0, c1):
                    t = pe(lambda e: e.transpose(ps[:, b, (c - c0) * 128:(c - c0 + 1) * 128], BT[:, c * 128:(c + 1) * 128], ident), free, tx[(g, 4)])
                t = act(lambda e: e.copy(Btok[:, c0:c1, :].rearrange("p a b -> p (a b)"), ps[:, b, 0:(c1 - c0) * 128]), t, busy["Btok"])
                Tb.give(ik, t)
            t_bt = t
            yield 1.0
            t_st = {}
            for d in (0, 1):
                prev, tp = None, busy["st"]
                seq = [4, 5, 0, 1, 2] if d == 0 else [5, 4, 3, 2, 1]
                for n, c in enumerate(seq):
                    h0 = d * 32 + g * 8
                    ik, x_, free = xwr.take()
                    t = pool(lambda e: e.tensor_tensor(x_.rearrange("p (r q) -> p r q", q=64), xtok[:, c, :].rearrange("p (r q) -> p r q", q=64),
                                                       wdec[:, c, h0:h0 + 8].unsqueeze(2).to_broadcast([P, 8, 64]), ALU.mult), free, t_xt[c])
                    sk, b, sfree = Sb.take()
                    t = pe(lambda e: e.matmul(bank(b), Btok[:, c, :], x_, start=True, stop=True), t, t_bt, sfree)
                    xwr.give(ik, t)
                    if n == 0:
                        dst = st0[:, :]
                        tp = dve(lambda e: e.tensor_copy(dst, bank(b)), t, tp)
                    else:
                        use = n - 1 if d == 0 else 4 - n
                        dst = st[:, d, use, :]
                        t2 = dve(lambda e: e.tensor_tensor(stt_[:, :].rearrange("p (r q) -> p r q", q=64), prev.rearrange("p (r q) -> p r q", q=64),
                                                           etot[:, c, h0:h0 + 8].unsqueeze(2).to_broadcast([P, 8, 64]), ALU.mult), tp)
                        tp = dve(lambda e: e.tensor_tensor(dst, stt_[:, :], bank(b), ALU.add), t, t2, busy["st"])
                        t_st[(d, use)] = tp
                    prev = dst
                    Sb.give(sk, tp)
                    yield 2.2
            ready = {}
            qk, qb, free = Qb.take()
            for c in range(4):
                t_q4 = pe(lambda e: e.matmul(ps[:, qb, c * 128:(c + 1) * 128], BT[:, c * 128:(c + 1) * 128], CT[:, c * 128:(c + 1) * 128],
                                             start=True, stop=True), free, tx[(g, 4)], tx[(g, 5)])

            def weights(c):
                eb = c % 2
                dve(lambda e: e.tensor_tensor(cbm[:, 0, :], ps[:, qb, c * 128:(c + 1) * 128], C("trif"), ALU.mult), t_q4, busy["cbm"])
                t_cb = dve(lambda e: e.tensor_tensor(cbm[:, 1, :], ps[:, qb, c * 128:(c + 1) * 128], C("trib"), ALU.mult))
                if c == 3:
                    Qb.give(qk, t_cb)
                tcs, tE = [], {}
                for d in (0, 1):
                    E = Ew[:, 2 if d else eb]
                    bk, bb, t_b = loads[(c, d)]
                    for r in range(8):
                        h = d * 32 + g * 8 + r
                        t = dve(lambda e: e.tensor_scalar(E[:, r, :], csbc[:, bb, r, :], csm[:, c, h:h + 1], 0.0, ALU.subtract, ALU.min), t_b, busy["E2"] if d else busy["E"][eb])
                    te_ = act(lambda e: e.activation(Cs[:, d, :, :], csbc[:, bb, :, :], ACT.Exp), t_b, busy["C"])
                    tcs.append(pool(lambda e: e.tensor_tensor(Cs[:, d, :, :], Cs[:, d, :, :],
                                                              CT[:, c * 128:(c + 1) * 128].unsqueeze(1).to_broadcast([P, 8, 128]), ALU.mult), te_, tx[(g, 5)]))
                    bcr.give(bk, te_, t)
                    tE[d] = act(lambda e: e.activation(E, E, ACT.Exp), t)
                    if c < 3:
                        load_cs(c + 1, d)
                    yield 2.0
                for d in (0, 1):
                    E = Ew[:, 2 if d else eb]
                    for r in range(8):
                        h = d * 32 + g * 8 + r
                        t = dve(lambda e: e.scalar_tensor_tensor(out=E[:, r, :], in0=E[:, r, :], scalar=dt_[:, c, h:h + 1],
                                                                 in1=cbm[:, d, :], op0=ALU.mult, op1=ALU.mult), tE[d], t_cb)
                    yield 2.0
                busy["cbm"] = [t]
                t_w = dve(lambda e: e.tensor_tensor(Ew[:, eb, :, :], Ew[:, eb, :, :], Ew[:, 2, :, :], ALU.add), t)
                busy["E2"] = [t_w]
                ready[c] = (eb, t_w, tcs)

            def outputs(c):
                eb, t_w, tcs = ready[c]
                yk, b, free = Yb.take()
                pe.wait(free, t_w, tcs, t_st[(0, c)], t_st[(1, c)])
                for r in range(8):
                    o = ps[(r % 2) * 64:(r % 2) * 64 + 64, b, (r // 2) * 128:(r // 2 + 1) * 128]
                    pe.quiet(lambda e: e.matmul(o, xtok[:, c, r * 64:r * 64 + 64], Ew[:, eb, r, :], start=True, stop=False))
                    pe.quiet(lambda e: e.matmul(o, st[:, 0, c, r * 64:r * 64 + 64], Cs[:, 0, r, :], start=False, stop=False))
                    f = lambda e: e.matmul(o, st[:, 1, c, r * 64:r * 64 + 64], Cs[:, 1, r, :], start=False, stop=True)
                    t_y = pe(f) if r == 7 else pe.quiet(f)
                busy["E"][eb] = [t_y]
                busy["C"] = [t_y]
                return yk, b, t_y

            def keep(c, yk, b, t_y):
                assert g == 0 or gated[g - 1] == 4
                for j in range(4):
                    t = dve(lambda e: e.scalar_tensor_tensor(out=yg[:, j, c * 128:(c + 1) * 128], in0=xs[:, j, c * 128:(c + 1) * 128],
                                                             scalar=V("dsk", 4 * g + j), in1=ps[:, b, j * 128:(j + 1) * 128], op0=ALU.mult, op1=ALU.add), t_y, busy["y"])
                Yb.give(yk, t)
                return t

            yield from weights(0)
            for c in range(4):
                y = outputs(c)
                yield 6.5
                if c < 3:
                    yield from weights(c + 1)
                t = keep(c, *y)
                yield 1.0
            t_y = y[2]
            tcs = ready[3][2]
            busy["x"][q] = [t, t_y, tcs]
            busy["xtok"] = busy["Btok"] = busy["st"] = [t_y]
            t_yz[g] = t

        def tokmajor(wd, nb, src, NT, dst, tl):
            for q in range(nb):
                s = [W.next((wd, (q, i), 0, 1024), 1024, True, held=i) for i in (0, 1)]
                for c in range(NT):
                    gk, b, free = G.take()
                    pe.wait(free, s[0][4], s[1][4])
                    o = ps[:, b, 0:256]
                    for k in range(8):
                        wh, wl = (x[:, (k % 4) * 256:(k % 4 + 1) * 256] for x in s[k // 4][2:4])
                        xh, xl = (f(k)[:, c * 128:(c + 1) * 128] for f in (src.hi, src.lo))
                        pe.quiet(lambda e: e.matmul(o, xh, wh, start=(k == 0), stop=False))
                        pe.quiet(lambda e: e.matmul(o, xh, wl, start=False, stop=False))
                        f = lambda e: e.matmul(o, xl, wh, start=False, stop=(k == 7))
                        t = pe(f) if k == 7 else pe.quiet(f)
                    yield 3.0
                    ta = act(lambda e: e.copy(dst(c)[:, q * 256:(q + 1) * 256], o), t)
                    G.give(gk, ta)
                    tl.append(ta)
                s[0][0].give(s[0][1], t)
                s[1][0].give(s[1][1], t)

        kT = at("kT", [P, 2, LT], 106)
        vt = at("vt", [P, 6, 256], 112)
        t_v, t_k = [], {}

        def keys_and_values():
            act.wait(busy["x"][0])
            yield from tokmajor("w_v", 1, HP, 6, lambda c: vt[:, c, :], t_v)
            for m in (8, 9):
                outs = gemm("w_qk", m, 8, HP, [(0, L), (L, LT)])
                yield 8.5
                t_k[m] = []
                for (t0, t1), (gk, pp, tok) in zip([(0, L), (L, LT)], outs):
                    ta = act(lambda e: e.copy(kT[:, m - 8, t0:t1], pp), tok)
                    G.give(gk, ta)
                    t_k[m].append(ta)

        weave(totals, "g", step_sizes(), xbc(0))
        Tb, Yb, Qb = banks(3, 4, 6), banks(5), banks(7)
        Sb = Tb
        busy["st"] = [t_csd[0]]
        weave(totals, "g0", ssd_group(0), xbc(1))
        weave(totals, "g1", ssd_group(1), alternate(chain_of(zgate(0), xbc(2)), mod_blocks(range(16, 26))))
        weave(totals, "g2", ssd_group(2), alternate(chain_of(zgate(1), xbc(3)), mod_blocks(range(26, 36))))
        weave(totals, "g3", ssd_group(3), alternate(chain_of(zgate(2), keys_and_values()), mod_blocks(range(36, 48))))
        t = dve(lambda e: e.tensor_scalar(A2[:, :], modS[:, 32:40, 0], 1.0, None, ALU.add), t_mod[0])
        t_A2 = dve(lambda e: e.tensor_tensor(A2[:, :], A2[:, :], V("g2", 0, 8), ALU.mult), t)
        run(zgate(3))
        t = norm_rstd([(0, L)], acc_tok[0], 0.25 / 2048, acc, rstd, (sq[:, 0, :], sq[:, 1, :]))
        t_rs = dve(lambda e: e.tensor_scalar(rstd[:, 0:L], rstd[:, 0:L], 0.25, None, ALU.mult), t)
        sqr.give(0, t_rs)
        sqr.give(1, t_rs)
        fm = fence()
        act.wait((dy.sem, dy.n))

        kTs = at("kTs", [P, 2, LT], 170)
        rope = at("rope", [P, 2, L], 118)
        gt = at("gt", [P, 16, L], 122)
        qT = at("qT", [P, 8, L], 154)
        raw = at("raw", [P, 2, L], 176)
        rt = at("rt", [P, 2, L], 180)
        Pm = at("Pm", [P, 8, 640], 184)
        PT = at("PT", [P, 5, 4, 128], 204)
        small = at("small", [P, 8, 4], 214)
        t_rope = Dma("s_rope").start(act, rope[:, :, :].rearrange("p a b -> p (a b)"), A["consts"][:, 896:1920], fm)
        rawr = Ring([0, 1])
        Pb = banks(3, 4)
        t_q = {}

        def qk_gemms(ms):
            for m in ms:
                isq = m < 8
                ik, i_, free = rawr.take()
                if isq:
                    (gk, pp, tok), = gemm("w_qk", m, 8, HP, [(0, L)])
                    x_ = raw[:, i_, :]
                    ta = act(lambda e: e.mul(x_, pp, 0.125), tok, free)
                    G.give(gk, ta)
                else:
                    x_ = kT[:, m - 8, 0:L]
                    ta = t_k[m]
                bk, b, bfree = Pb.take()
                tp = pe(lambda e: e.matmul(bank(b), C("perm"), x_, start=True, stop=True), ta, bfree)
                tg = dve(lambda e: e.tensor_tensor(rt[:, i_, :], x_, rope[:, 0, :], ALU.mult), ta, t_rope, free)
                dst = qT[:, m, :] if isq else kT[:, m - 8, 0:L]
                t = dve(lambda e: e.tensor_tensor(dst, bank(b), rope[:, 1, :], ALU.mult), tp, t_rope, tg)
                Pb.give(bk, t)
                t = dve(lambda e: e.tensor_tensor(dst, dst, rt[:, i_, :], ALU.add), t, tg)
                rawr.give(ik, tp, tg, t)
                t_q[m] = [t] if isq else [t, t_k[m]]

        def softmax(S, dstP, sm, scale, sink, ready, free):
            t = dve(lambda e: e.tensor_reduce(sm[:, 0:1], S, AXX, ALU.max), ready, free)
            if sink is not None:
                t = dve(lambda e: e.tensor_scalar(sm[:, 1:2], sm[:, 0:1], sink, -1.0, ALU.max, ALU.mult), t)
            else:
                t = dve(lambda e: e.tensor_scalar(sm[:, 1:2], sm[:, 0:1], -scale, None, ALU.mult), t)
            ts = act(lambda e: e.activation(dstP, S, ACT.Exp, bias=sm[:, 1:2], scale=scale, accum_out=sm[:, 2:3]), t, free)
            ta = ts
            if sink is not None:
                ta = act(lambda e: e.activation(sm[:, 3:4], sink, ACT.Exp, bias=sm[:, 1:2]), t)
            return ta

        def normalise(dstP, sm, sink, ta):
            t = ta
            if sink:
                t = dve(lambda e: e.tensor_tensor(sm[:, 2:3], sm[:, 2:3], sm[:, 3:4], ALU.add), t)
            t = dve(lambda e: e.reciprocal(sm[:, 1:2], sm[:, 2:3]), t)
            return dve(lambda e: e.tensor_scalar(dstP, dstP, sm[:, 1:2], None, ALU.mult), t)

        qk_gemms([8, 9])
        dks = Dma("s_ks")
        dks.start(act, kTs[0:64, :, :], kT[64:128, :, :], t_q[8], t_q[9])
        t_ks = dks.start(act, kTs[64:128, :, :], kT[0:64, :, :])
        qk_gemms(range(8))
        pe.wait([t_q[m] for m in range(10)], t_v, t_ks)
        G = banks(0)

        def window_attention():
            Sr, Tr, Or = banks(3, 5), banks(7, 1), banks(2)
            busy_P, busy_PT, pend = [[], []], [], {}

            def shape(n):
                lo, hi = max(n - 1, 0), min(n + 1, 3)
                nw = hi - lo + 1
                return lo, hi, nw, 512 - nw * 128, nw * 128 + 256

            def scores(i):
                n, kv = i // 4, i % 4
                lo, hi, nw, w0, Wd = shape(n)
                half, kt = (kv % 2) * 64, kv // 2
                pend[i] = []
                last = None
                for j in range(4):
                    h = 4 * kv + j
                    qrow = (h % 2) * 64
                    sk, b, free = Sr.take()
                    q = qT[qrow:qrow + 64, h // 2, n * 128:(n + 1) * 128]
                    kk = (kT if qrow == half else kTs)[qrow:qrow + 64, kt, :]
                    pe.wait(free)
                    pe.quiet(lambda e: e.matmul(ps[:, b, w0:512], q, kk[:, lo * 128:(hi + 1) * 128], start=True, stop=False))
                    if n > 0:
                        pe.quiet(lambda e: e.matmul(ps[:, b, w0:w0 + 128], maskb[:, 0, :], maskb[:, 1, :], start=False, stop=(n == 3)))
                    if n < 3:
                        pe.quiet(lambda e: e.matmul(ps[:, b, 384:512], maskb[:, 0, :], maskb[:, 2, :], start=False, stop=True))
                    t = pe(lambda e: e.matmul(ps[:, b + 1, 0:256], q, kk[:, L:LT], start=True, stop=True))
                    S = ps[:, b:b + 2, :].rearrange("p a b -> p (a b)")[:, w0:w0 + Wd]
                    pi = (i % 2) * 4 + j
                    ta = softmax(S, Pm[:, pi, 0:Wd], small[:, pi, :], 1.0, rows[:, 128 + h:129 + h], t, busy_P[i % 2])
                    Sr.give(sk, ta)
                    if last:
                        pend[i].append(normalise(*last))
                    last = (Pm[:, pi, 0:Wd], small[:, pi, :], True, ta)
                    yield 1.7
                pend[i].append(normalise(*last))

            def apply(i):
                n, kv = i // 4, i % 4
                lo, hi, nw, w0, Wd = shape(n)
                nk = nw + 2
                t_pt = []
                for kb in range(nk):
                    tk, b, free = Tr.take()
                    for j in range(4):
                        t = pe(lambda e: e.transpose(ps[:, b, j * 128:(j + 1) * 128], Pm[:, (i % 2) * 4 + j, kb * 128:(kb + 1) * 128], ident), free, pend[i][j])
                    if kb % 2:
                        t2 = dve(lambda e: e.tensor_copy(PT[:, kb, :, :].rearrange("p a b -> p (a b)"), bank(b)), t, busy_PT)
                    else:
                        t2 = act(lambda e: e.copy(PT[:, kb, :, :].rearrange("p a b -> p (a b)"), bank(b)), t, busy_PT)
                    Tr.give(tk, t2)
                    t_pt.append(t2)
                    yield 1.0
                busy_P[i % 2] = [t]
                ok, b, free = Or.take()
                pe.wait(free, t_pt)
                for par in (0, 1):
                    for kb in range(nk):
                        c = lo + kb if kb < nw else 4 + kb - nw
                        t = pe(lambda e: e.matmul(ps[par * 64:par * 64 + 64, b, 0:256].rearrange("p (a b) -> p a b", b=128), vt[:, c, kv * 64:(kv + 1) * 64],
                                                  PT[:, kb, par:4:2, :], start=(kb == 0), stop=(kb == nk - 1)))
                busy_PT[:] = [t]
                t_o = dve(lambda e: e.tensor_copy(qT[:, 2 * kv:2 * kv + 2, n * 128:(n + 1) * 128],
                                                  ps[:, b, 0:256].rearrange("p (a b) -> p a b", b=128)), t)
                Or.give(ok, t_o)
                yield 4.0

            yield from scores(0)
            for i in range(16):
                if i < 15:
                    yield from alternate(scores(i + 1), apply(i))
                else:
                    yield from apply(i)

        t_gate = {}

        def gates1():
            for i in range(16):
                (gk, pp, tok), = gemm("w_g", i, 8, HP, [(0, L)])
                ta = act(lambda e: e.activation(gt[:, i, :], pp, ACT.Tanh, scale=0.5), tok)
                G.give(gk, ta)
                t_gate[i] = ta
                yield 5.5

        weave(totals, "wa", window_attention(), gates1())
        fm = fence()

        QP, _, _ = pair("qp", 8, L, 170)
        YP, yh, yl = pair("yp", 16, L, 58)
        MP_ = at("mp", [P, 16, L], 122, F32R)
        MP = Pair(lambda k: MP_[:, k, :], lambda k: MP_[:, 8 + k, :])
        X = at("X", [P, 8, L], 202)
        t_x = Dma("s_xr").start(sp, X[:, :, :], A["xT"], fm)
        dyl = [Dma(f"s_yl{i}") for i in range(4)]
        t_yr, t_yl = [], []
        yraw = yl[:, :, :].bitcast(F32)
        for i in range(4):
            t_yr.append(dyl[i].start(act, yraw[:, 4 * i:4 * i + 4, :], A["ysc"][:, 4 * i:4 * i + 4, :], fm))
        t_qp = [QP.put(k, qT[:, k, :], 0, L, lo=(dve if k % 2 else pool)) for k in range(8)]
        G = banks(0, 1, 2, 3, 4, 5, 6, 7)
        t_oa = []
        for m in range(8):
            (gk, pp, tok), = gemm("w_oa", m, 8, QP, [(0, L)], tiles=(t_qp if m == 0 else None))
            t = dve(lambda e: e.scalar_tensor_tensor(out=gt[:, 8 + m, :], in0=gt[:, 8 + m, :], scalar=1.0, in1=pp, op0=ALU.add, op1=ALU.mult), tok)
            G.give(gk, t)
            t_oa.append(t)
            for k in (2 * m, 2 * m + 1):
                t_yl.append(YP.put(k, yraw[:, k, :], 0, L, t_yr[k // 4], lo=dve))
        t_m = []
        for m in range(8):
            (gk, pp, tok), = gemm("w_os", m, 16, YP, [(0, L)], tiles=(t_yl if m == 0 else None))
            t = dve(lambda e: e.scalar_tensor_tensor(out=gt[:, m, :], in0=gt[:, m, :], scalar=1.0, in1=pp, op0=ALU.add, op1=ALU.mult), tok)
            G.give(gk, t)
            t = dve(lambda e: e.tensor_tensor(gt[:, m, :], gt[:, m, :], rstd[:, 0:L], ALU.mult), t)
            i_, s, free = sqr.take()
            t = dve(lambda e: e.scalar_tensor_tensor(out=s, in0=gt[:, 8 + m, :], scalar=0.5, in1=gt[:, m, :], op0=ALU.mult, op1=ALU.add), t, t_oa[m], free)
            tt = MP.put(m, s, 0, L, t)
            sqr.give(i_, tt)
            t_m.append(tt)
        for m in range(8):
            (gk, pp, tok), = gemm("w_out", m, 8, MP, [(0, L)], tiles=(t_m if m == 0 else None))
            t = dve(lambda e: e.scalar_tensor_tensor(out=X[:, m, :], in0=pp, scalar=modS[:, 16 + m, 0:1], in1=X[:, m, :], op0=ALU.mult, op1=ALU.add), tok, t_x)
            G.give(gk, t)
            t_n = norm_add(m, X[:, m, :], L, acc, sqr, t)

        H2, _, _ = pair("h2", 8, L, 58)
        PR, _, _ = pair("pr", 22, L, 90)
        ua = at("ua", [P, 4, L], 178)
        ub = at("ub", [P, 2, L], 186)
        vt2 = at("vt2", [P, 2, L], 190)
        fence()
        v2r = Ring([vt2[:, 0, :], vt2[:, 1, :]])
        t_r = rstd_of(8, L, t_n)
        t_h = []
        for k in range(8):
            i_, v, free = v2r.take()
            t = dve(lambda e: e.tensor_tensor(v, X[:, k, :], rstd[:, 0:L], ALU.mult), t_r, free)
            t = dve(lambda e: e.tensor_scalar(v, v, A2[:, k:k + 1], modS[:, 24 + k, 0:1], ALU.mult, ALU.add), t, t_A2)
            tt = H2.put(k, v, 0, L, t, lo=(pool if k % 2 else dve))
            v2r.give(i_, tt)
            t_h.append(tt)
        uar, ubr = Ring([0, 1, 2, 3]), Ring([0, 1])
        FW = ("fw0", "fw1", "fw2", "fb")
        t_p = []
        for m in range(22):
            tt = []
            for which in (0, 1):
                mm = m + 22 * which
                (gk, pp, tok), = gemm("w_up", mm, 8, H2, [(0, L)], tiles=(t_h if m == 0 else None))
                ik, i_, free = uar.take()
                t = conv(pp, L, mm, FW, ua[:, i_, :], tok, free)
                G.give(gk, t)
                tt.append((ik, i_, t))
            (ka, ia, ta_), (kb_, ib, tb_) = tt
            k2, i2, free = ubr.take()
            ta = act(lambda e: e.activation(ub[:, i2, :], ua[:, ia, :], ACT.Tanh), ta_, free)
            t = dve(lambda e: e.scalar_tensor_tensor(out=ub[:, i2, :], in0=ub[:, i2, :], scalar=1.0, in1=ua[:, ia, :], op0=ALU.add, op1=ALU.mult), ta)
            t = dve(lambda e: e.tensor_tensor(ub[:, i2, :], ub[:, i2, :], ua[:, ib, :], ALU.mult), t, tb_)
            tt = PR.put(m, ub[:, i2, :], 0, L, t, lo=dve)
            uar.give(ka, t)
            uar.give(kb_, t)
            ubr.give(k2, tt)
            t_p.append(tt)

        HM, _, _ = pair("hm", 8, LC, 178)
        hm = at("hm", [P, 8, LC], 194)
        accm = at("accm", [P, LC], 58)
        rstdm = at("rstdm", [P, LC], 59)
        sqm = at("sqm", [P, 2, LC], 60)
        mk = at("mk", [P, 4, LC], 102)
        mv = at("mv", [P, 2, 512], 106)
        t_up = marks()
        for e in (act, dve, pool):
            e.wait(t_up)
        t_hm = Dma("s_mem").start(sp, hm[:, :, :], A["memT"], t_up)
        t_HM = []

        def memory_norm():
            sqmr = Ring([sqm[:, 0, :], sqm[:, 1, :]])
            t = norm_sum(lambda k: hm[:, k, :], 8, LC, accm, sqmr, t_hm)
            yield
            t_r = norm_rstd([(0, LC)], t, 1.0 / 1024, accm, rstdm, (sqm[:, 0, :], sqm[:, 1, :]))
            yield
            for k in range(8):
                t = dve(lambda e: e.scalar_tensor_tensor(out=hm[:, k, :], in0=hm[:, k, :], scalar=V("gm", k), in1=rstdm[:, :], op0=ALU.mult, op1=ALU.mult), t_r)
                t_HM.append(HM.put(k, hm[:, k, :], 0, LC, t))
                if k % 2:
                    yield

        mem = memory_norm()
        for m in range(8):
            (gk, pp, tok), = gemm("w_down", m, 22, PR, [(0, L)], tiles=(t_p if m == 0 else None))
            t = dve(lambda e: e.scalar_tensor_tensor(out=X[:, m, :], in0=pp, scalar=modS[:, 40 + m, 0:1], in1=X[:, m, :], op0=ALU.mult, op1=ALU.add), tok)
            G.give(gk, t)
            t_n = norm_add(m, X[:, m, :], L, acc, sqr, t)
            if m:
                next(mem, None)
        run(mem)
        t_r = rstd_of(8, L, t_n)
        t_mkv = []
        for m in range(4):
            (gk, pp, tok), = gemm("w_mk", m, 8, HM, [(0, LC)], t_HM)
            ta = act(lambda e: e.copy(mk[:, m, :], pp), tok)
            G.give(gk, ta)
            t_mkv.append(ta)
        tl = []
        for k in range(8):
            tl.append(dve(lambda e: e.scalar_tensor_tensor(out=X[:, k, :], in0=X[:, k, :], scalar=V("fg", k), in1=rstd[:, 0:L], op0=ALU.mult, op1=ALU.mult), t_r))
            t_n = norm_add(k, X[:, k, :], L, acc, sqr, tl[-1])
        t_spill = Dma("s_spill").start(sp, A["xsc"], X[:, :, :], tl)
        H, _, _ = pair("H", 8, L, 58)
        vt3 = at("vt3", [P, 2, L], 90)
        v3r = Ring([vt3[:, 0, :], vt3[:, 1, :]])
        t_r = rstd_of(8, L, t_n)
        run(tokmajor("w_mv", 2, HM, 2, lambda c: mv[:, c, :], t_mkv))
        t_H = []
        for k in range(8):
            i_, v, free = v3r.take()
            t = dve(lambda e: e.scalar_tensor_tensor(out=v, in0=X[:, k, :], scalar=V("gn", k), in1=rstd[:, 0:L], op0=ALU.mult, op1=ALU.mult), t_r, free)
            tt = H.put(k, v, 0, L, t, lo=(pool if k % 2 else dve))
            v3r.give(i_, tt)
            t_H.append(tt)
        for e in (dve, act, pool):
            e.wait(t_spill, t_H, t_mkv)

        yf = at("yf", [P, 6, L], 90)
        ym = at("ym", [P, 4, L], 114)
        kf = at("kf", [P, 6, L], 122)
        vf = at("vf", [P, 4, 768], 134)
        Pf = at("Pf", [P, 2, 1280], 146)
        PTf = at("PTf", [P, 1280], 156)
        FT = at("FT", [12, L], 162)
        ffs = at("ffs", [12, 4, L], 146)
        smf = at("smf", [P, 8, 4], 161)
        uT = at("uT", [P, 6, L], 165)
        ysv = uT
        z32 = at("z32", [P, 2, 24, 32], 177)
        q16 = at("q16", [P, 2, 24, 16], 183)
        bl = at("bl", [P, 2, 6, 128], 186)
        cl = at("cl", [P, 2, 24, 32], 192)
        Tc = at("Tc", [P, 2, 2, L], 198)
        Wk = at("Wk", [P, 8, L], 206)
        wkf = Wk[:, :, :].rearrange("p a b -> p (a b)")
        bre = wkf[:, 0:768].rearrange("p (a b) -> p a b", b=32)
        bim = wkf[:, 768:1536].rearrange("p (a b) -> p a b", b=32)
        bb = wkf[:, 1536:3840].rearrange("p (q a b) -> p q a b", q=3, b=32)
        G = banks(0, 1)

        t_u = []
        t_fq = {}
        t_fv = []

        def silu_gate(pp, tok, gk, src, dst, *toks):
            i_, s, sfree = sqr.take()
            ta = act(lambda e: e.activation(s, pp, ACT.Tanh, scale=0.5), tok, sfree)
            t1 = dve(lambda e: e.scalar_tensor_tensor(out=s, in0=s, scalar=1.0, in1=pp, op0=ALU.add, op1=ALU.mult), ta)
            G.give(gk, t1)
            t1 = dve(lambda e: e.tensor_tensor(dst, s, src, ALU.mult), t1, toks)
            sqr.give(i_, t1)
            return t1

        def u_gemms():
            for m in range(6):
                (gk, pp, tok), = gemm("w_u", m, 8, H, [(0, L)], tiles=(t_H if m == 0 else None))
                ta = act(lambda e: e.copy(uT[:, m, :], pp), tok)
                G.give(gk, ta)
                t_u.append(ta)
                yield 5.5

        def fq_gemms():
            for m in range(12):
                (gk, pp, tok), = gemm("w_fqk", m, 8, H, [(0, L)])
                yield 5.5
                dst = yf[:, m, :] if m < 6 else kf[:, m - 6, :]
                ta = act(lambda e: e.mul(dst, pp, 0.125 if m < 6 else 1.0), tok)
                G.give(gk, ta)
                t_fq[m] = ta

        t_FT = [None]

        def forget():
            fu, fw, fn, fl = (ffs[:, i, :] for i in range(4))
            tt = narrow(("w_fl", 0, 0, 96), 96, 12, H, [(0, L)],
                        lambda t0, t1, o, t: dve(lambda e: e.tensor_scalar(fl, o, -1.0, V("bfc")[0:12, :], ALU.mult, ALU.subtract), t))
            yield 6.0
            t = softplus(fl, fu, fw, fn)
            t = dve(lambda e: e.tensor_tensor_scan(FT[:, :], ones[0:12, 0:1].to_broadcast([12, L]), fl, 0.0, ALU.mult, ALU.add), t)
            t_FT[0] = t
            yield 8.0

        def gate_gemms(wd, ms, dst, ready):
            for m in ms:
                (gk, pp, tok), = gemm(wd, m, 8, H, [(0, L)])
                yield 5.5
                ready[m] = silu_gate(pp, tok, gk, dst(m), dst(m), ready[m])

        t_d5 = [None]
        K = lambda i: pk_[:, i, :]
        lr, li, ls = V("lre", 0, 24), V("lim", 0, 24), V("lstep", 0, 24)
        PI2 = 2 * np.pi
        C1, C2 = 6.28125, 0.0019350051879882812
        C3 = PI2 - C1 - C2
        MAGIC = 12582912.0
        TT = lambda o, a, b_, op: (dve, lambda e: e.tensor_tensor(o, a, b_, op))
        TS = lambda o, a, s1, s2, o1, o2=None: (dve, lambda e: e.tensor_scalar(o, a, s1, s2, o1, *([o2] if o2 is not None else [])))
        ST = lambda o, a, s, b_, o1, o2: (dve, lambda e: e.scalar_tensor_tensor(out=o, in0=a, scalar=s, in1=b_, op0=o1, op1=o2))
        CP = lambda o, a: (dve, lambda e: e.tensor_copy(o, a))
        AC = lambda o, a, f, sc=1.0: (act, lambda e: e.activation(o, a, f, scale=sc))

        def steps(fns):
            prev = [dve.last(), act.last()]
            for eng, f in fns:
                prev = [eng(f, prev)]

        def cmul(o, a, z, n, tmp):
            zr = z[0].unsqueeze(2).to_broadcast([P, 24, n])
            zi = z[1].unsqueeze(2).to_broadcast([P, 24, n])
            return [TT(tmp, a[1], zi, ALU.mult), TT(o[0], a[0], zr, ALU.mult), TT(o[0], o[0], tmp, ALU.subtract),
                    TT(tmp, a[0], zi, ALU.mult), TT(o[1], a[1], zr, ALU.mult), TT(o[1], o[1], tmp, ALU.add)]

        def csq(o, a):
            return [TT(K(14), a[1], a[1], ALU.mult), TT(K(15), a[0], a[0], ALU.mult), TT(K(15), K(15), K(14), ALU.subtract),
                    ST(K(16), a[0], 2.0, a[1], ALU.mult, ALU.mult), CP(o[0], K(15)), CP(o[1], K(16))]

        def powers(tab, z, n):
            seq = [(dve, lambda e: e.memset(tab[:, 0, :, 0], 1.0)), (dve, lambda e: e.memset(tab[:, 1, :, 0], 0.0)), CP(K(12), z[0]), CP(K(13), z[1])]
            k = 1
            while k < n:
                seq += cmul((tab[:, 0, :, k:2 * k], tab[:, 1, :, k:2 * k]), (tab[:, 0, :, 0:k], tab[:, 1, :, 0:k]), (K(12), K(13)), k, bb[:, 2, :, 0:k])
                seq += csq((K(12), K(13)), (K(12), K(13)))
                k *= 2
            return seq

        def s5_numbers():
            steps([
                AC(K(0), ls, ACT.Exp),
                TT(K(1), lr, K(0), ALU.mult),
                AC(K(2), K(1), ACT.Exp),
                TT(K(3), li, K(0), ALU.mult),
                TS(K(4), K(3), 1.0 / PI2, MAGIC, ALU.mult, ALU.add),
                TS(K(4), K(4), MAGIC, None, ALU.subtract),
                ST(K(3), K(4), -C1, K(3), ALU.mult, ALU.add),
                ST(K(3), K(4), -C2, K(3), ALU.mult, ALU.add),
                ST(K(3), K(4), -C3, K(3), ALU.mult, ALU.add),
                TS(K(3), K(3), 3.1415925, -3.1415925, ALU.min, ALU.max),
                AC(K(5), K(3), ACT.Sin),
                AC(K(6), K(3), ACT.Sin, 0.5),
                TT(K(6), K(6), K(6), ALU.mult),
                TS(K(6), K(6), -2.0, 1.0, ALU.mult, ALU.add),
                TT(K(7), K(2), K(6), ALU.mult),
                TS(K(7), K(7), 1.0, None, ALU.subtract),
                TT(K(8), K(2), K(5), ALU.mult),
                TT(K(9), lr, lr, ALU.mult),
                TT(K(10), li, li, ALU.mult),
                TT(K(9), K(9), K(10), ALU.add),
                (dve, lambda e: e.reciprocal(K(9), K(9))),
                TT(K(10), K(7), lr, ALU.mult),
                TT(K(11), K(8), li, ALU.mult),
                TT(K(10), K(10), K(11), ALU.add),
                TT(K(10), K(10), K(9), ALU.mult),
                TT(K(11), K(8), lr, ALU.mult),
                TT(K(12), K(7), li, ALU.mult),
                TT(K(11), K(11), K(12), ALU.subtract),
                TT(K(11), K(11), K(9), ALU.mult),
            ])

        def s5_tables(Tr5):
            fre = K(10).unsqueeze(2).to_broadcast([P, 24, 32])
            fim = K(11).unsqueeze(2).to_broadcast([P, 24, 32])
            dve.wait(t_d5[0])
            steps([
                TT(bb[:, 0], bre, fre, ALU.mult), TT(bb[:, 2], bim, fim, ALU.mult),
                TT(bb[:, 0], bb[:, 0], bb[:, 2], ALU.subtract),
                TT(bb[:, 1], bim, fre, ALU.mult), TT(bb[:, 2], bre, fim, ALU.mult),
                TT(bb[:, 1], bb[:, 1], bb[:, 2], ALU.add),
                TS(cl[:, 1].rearrange("p a b -> p (a b)"), cl[:, 1].rearrange("p a b -> p (a b)"), -1.0, None, ALU.mult),
            ])
            yield 6.0
            td = dve.last()
            for ri in (0, 1):
                for j in range(6):
                    tk, b, free = Tr5.take()
                    t = pe(lambda e: e.transpose(ps[:, b, 0:128], bb[:, ri, 4 * j:4 * j + 4, :].rearrange("p a b -> p (a b)"), ident), free, td)
                    t = act(lambda e: e.copy(bl[:, ri, j, :], ps[:, b, 0:128]), t)
                    Tr5.give(tk, t)
                yield 3.0
            fns = powers(z32, (K(6), K(5)), 32) + powers(q16, (K(12), K(13)), 16)
            for i in range(0, len(fns), 6):
                steps(fns[i:i + 6])
                yield 1.5
            pool.wait(dve.last())
            pe.wait(t)

        def s5_scan():
            Xr, Yr = banks(2), banks(4)
            yield from s5_tables(banks(2, 3, 4))
            W_ = lambda i: Wk[:, i, :]
            tcr = Ring([0, 1])
            v3 = lambda x: x.rearrange("p (a b) -> p a b", b=32)
            tabs, xs5 = {}, {}
            wfree = {i: [dve.last()] for i in range(8)}

            def table(s):
                ck, cb_, cfree = tcr.take()
                tre, tim = Tc[:, cb_, 0, :], Tc[:, cb_, 1, :]
                Pr, Pi = (z32[:, q, s, :].unsqueeze(1).to_broadcast([P, 16, 32]) for q in (0, 1))
                Qr, Qi = (q16[:, q, s, :].unsqueeze(2).to_broadcast([P, 16, 32]) for q in (0, 1))
                pool(lambda e: e.tensor_tensor(v3(tre), Pr, Qr, ALU.mult), cfree, wfree[6])
                a2 = pool(lambda e: e.tensor_tensor(v3(W_(6)), Pi, Qi, ALU.mult), pool.last())
                a3 = pool(lambda e: e.tensor_tensor(tre, tre, W_(6), ALU.subtract), a2)
                pool(lambda e: e.tensor_tensor(v3(tim), Pi, Qr, ALU.mult))
                a2 = pool(lambda e: e.tensor_tensor(v3(W_(6)), Pr, Qi, ALU.mult), a3)
                tabs[s] = (ck, tre, tim, pool(lambda e: e.tensor_tensor(tim, tim, W_(6), ALU.add), a2))

            def drive(s):
                j, i = s // 4, s % 4
                xk, b, free = Xr.take()
                for ri in (0, 1):
                    t = pe(lambda e: e.matmul(bank(b + ri), bl[32 * i:32 * i + 32, ri, j, :], uT[32 * i:32 * i + 32, j, :],
                                              start=True, stop=True), free, t_u[j])
                xs5[s] = (xk, b, t)

            late = []
            table(0)
            drive(0)
            for s in range(24):
                j, i = s // 4, s % 4
                ck, tre, tim, t_tab = tabs.pop(s)
                xk, b, t = xs5.pop(s)
                xr, xi = bank(b), bank(b + 1)
                dve(lambda e: e.tensor_tensor(W_(0), xr, tre, ALU.mult), t, t_tab, wfree[0])
                d2 = dve(lambda e: e.tensor_tensor(W_(1), xi, tim, ALU.mult), wfree[1])
                dve(lambda e: e.tensor_tensor(W_(2), xi, tre, ALU.mult), wfree[2])
                d4 = dve(lambda e: e.tensor_tensor(W_(3), xr, tim, ALU.mult), wfree[3])
                Xr.give(xk, d4)
                if s < 23:
                    table(s + 1)
                yield 4.0
                dve(lambda e: e.tensor_tensor(W_(0), W_(0), W_(1), ALU.add), d2)
                d4 = dve(lambda e: e.tensor_tensor(W_(2), W_(2), W_(3), ALU.subtract), d4)
                mag = K(2)[:, s:s + 1].to_broadcast([P, L])
                d1 = dve(lambda e: e.tensor_tensor_scan(W_(1), mag, W_(0), 0.0, ALU.mult, ALU.add), d4)
                yield 2.5
                if s < 23:
                    drive(s + 1)
                if late:
                    yield from late.pop()()
                d2 = dve(lambda e: e.tensor_tensor_scan(W_(3), mag, W_(2), 0.0, ALU.mult, ALU.add), d4)
                d5_ = dve(lambda e: e.tensor_tensor(W_(4), W_(1), tre, ALU.mult), d1, wfree[4])
                d6 = dve(lambda e: e.tensor_tensor(W_(0), W_(3), tim, ALU.mult), d2)
                p1 = pool(lambda e: e.tensor_tensor(W_(5), W_(1), tim, ALU.mult), d2, wfree[5])
                p2 = pool(lambda e: e.tensor_tensor(W_(7), W_(3), tre, ALU.mult), d2)
                yield 2.5
                d7 = dve(lambda e: e.tensor_tensor(W_(4), W_(4), W_(0), ALU.subtract), d6)
                p3 = pool(lambda e: e.tensor_tensor(W_(5), W_(5), W_(7), ALU.add), p2)
                tcr.give(ck, d6, p2)
                wfree[0], wfree[2] = [d7], [d2]
                wfree[1], wfree[3] = [p1, p2, d6], [p2, d6]

                def finish(s=s, i=i, j=j, d7=d7, p3=p3):
                    if i == 0:
                        Y5[0] = Yr.take()
                        pe.wait(Y5[0][2])
                    yk, yb, _ = Y5[0]
                    pe.quiet(lambda e: e.matmul(ps[32 * i:32 * i + 32, yb, :], cl[:, 0, s, :], W_(4), start=True, stop=False, tile_position=(0, 32 * i)), d7)
                    t = pe(lambda e: e.matmul(ps[32 * i:32 * i + 32, yb, :], cl[:, 1, s, :], W_(5), start=False, stop=True, tile_position=(0, 32 * i)), p3)
                    wfree[4], wfree[5] = [t], [t]
                    if i == 3:
                        y = ysv[:, j, :]
                        t = dve(lambda e: e.scalar_tensor_tensor(out=y, in0=uT[:, j, :], scalar=V("s5d", j), in1=bank(yb), op0=ALU.mult, op1=ALU.add), t)
                        Yr.give(yk, t)
                        i_, q, sfree = sqr.take()
                        ta = act(lambda e: e.activation(q, y, ACT.Square), t, sfree)
                        t = dve(lambda e: e.tensor_scalar(q, q, 0.044715, 1.0, ALU.mult, ALU.add), ta)
                        t = dve(lambda e: e.tensor_tensor(q, q, y, ALU.mult), t)
                        ta = act(lambda e: e.activation(q, q, ACT.Tanh, scale=0.7978845608028654), t)
                        t = dve(lambda e: e.scalar_tensor_tensor(out=y, in0=q, scalar=1.0, in1=y, op0=ALU.add, op1=ALU.mult), ta)
                        sqr.give(i_, t)
                        t_y5[j] = t
                        yield 2.0

                late.append(finish)
                yield 1.5
            yield from late.pop()()

        Y5 = [None]
        t_y5 = {}

        t_qm = []

        def qm_gemm(m):
            (gk, pp, tok), = gemm("w_qm", m, 8, H, [(0, L)])
            yield 5.5
            ta = act(lambda e: e.copy(ym[:, m, :], pp), tok)
            G.give(gk, ta)
            t_qm.append(ta)

        t_yf = {}

        def fox():
            nonlocal G
            left = Ring([0])
            left.give(0, *G.free[0])
            G = left
            Sr, Tr, Or = banks(5, 1), banks(6), banks(7)
            pe.wait([t_fq[m] for m in range(12)], t_fv, t_FT[0])
            row = lambda hb, n: Pf[:, hb, n * (n + 1) * 64:(n + 1) * (n + 2) * 64]
            col = lambda kb: PTf[:, (4 * kb - kb * (kb - 1) // 2) * 128:][:, 0:(4 - kb) * 128]
            state = {"P": [[], []], "PT": [], "pend": {}}

            def scores(h):
                hp, hb = (h % 2) * 64, h % 2
                pend = state["pend"][h] = []
                last = None
                for n in range(4):
                    Wd = (n + 1) * 128
                    sk, b, free = Sr.take()
                    pe.wait(free)
                    pe.quiet(lambda e: e.matmul(ps[:, b, 0:Wd], yf[hp:hp + 64, h // 2, n * 128:(n + 1) * 128], kf[hp:hp + 64, h // 2, 0:Wd],
                                                start=True, stop=False))
                    pe.quiet(lambda e: e.matmul(ps[:, b, 0:Wd], ident[0:12, h:h + 1].to_broadcast([12, 128]), FT[:, 0:Wd], start=False, stop=False))
                    t = pe(lambda e: e.matmul(ps[:, b, n * 128:Wd], maskb[:, 0, :], maskb[:, 2, :], start=False, stop=True))
                    sm = smf[:, 4 * hb + n, :]
                    ta = softmax(ps[:, b, 0:Wd], row(hb, n), sm, 1.0, None, t, state["P"][hb])
                    Sr.give(sk, ta)
                    if last:
                        pend.append(normalise(*last))
                    last = (row(hb, n), sm, False, ta)
                    yield 1.0 + n * 0.5
                pend.append(normalise(*last))

            def apply(h):
                hp, hb = (h % 2) * 64, h % 2
                pend = state["pend"][h]
                t_pt = []
                for kb in range(4):
                    tk, b, free = Tr.take()
                    for n in range(kb, 4):
                        t = pe(lambda e: e.transpose(ps[:, b, n * 128:(n + 1) * 128], row(hb, n)[:, kb * 128:(kb + 1) * 128], ident), free, pend[n])
                    if kb % 2:
                        t2 = dve(lambda e: e.tensor_copy(col(kb), ps[:, b, kb * 128:L]), t, state["PT"])
                    else:
                        t2 = act(lambda e: e.copy(col(kb), ps[:, b, kb * 128:L]), t, state["PT"])
                    Tr.give(tk, t2)
                    t_pt.append(t2)
                    yield 1.0
                state["P"][hb] = [t]
                if h % 2 == 0:
                    state["o"] = Or.take()
                ok, ob, free = state["o"]
                pe.wait(free, t_pt)
                for kb in range(4):
                    t = pe(lambda e: e.matmul(ps[hp:hp + 64, ob, kb * 128:L], vf[:, kb, h * 64:(h + 1) * 64], col(kb),
                                              start=(kb == 0), stop=(kb == 3)))
                state["PT"] = [t]
                yield 2.5
                if h % 2:
                    t1 = act(lambda e: e.copy(yf[:, h // 2, :], bank(ob)), t)
                    Or.give(ok, t1)
                    t_yf[h // 2] = t1

            yield from scores(0)
            for h in range(12):
                m = h // 2
                extra = iter(()) if h == 0 else gate_gemms("w_gf", [m - 1], lambda m: yf[:, m, :], t_yf) if h % 2 == 0 else qm_gemm(m) if m < 4 else iter(())
                yield from alternate(scores(h + 1) if h < 11 else iter(()), apply(h), extra)
            yield from gate_gemms("w_gf", [5], lambda m: yf[:, m, :], t_yf)

        Pq = at("Pq", [P, 8, LC], 122)
        PTm = at("PTm", [P, 2, L], 130)
        smm = at("smm", [P, 8, 4], 222)
        MS = float(128) ** -0.5
        t_ym = {}

        def memory():
            pe.wait(t_qm)
            Sr, Tr, Or = banks(5, 1), banks(6), banks(7)
            busy_P, ptb, pend = [[], []], [[]], {}

            def scores(h):
                pend[h] = []
                last = None
                for n in range(4):
                    sk, b, free = Sr.take()
                    t = pe(lambda e: e.matmul(ps[:, b, 0:LC], ym[:, h, n * 128:(n + 1) * 128], mk[:, h, :], start=True, stop=True), free)
                    pi = (h % 2) * 4 + n
                    ta = softmax(ps[:, b, 0:LC], Pq[:, pi, :], smm[:, pi, :], MS, None, t, busy_P[h % 2])
                    Sr.give(sk, ta)
                    if last:
                        pend[h].append(normalise(*last))
                    last = (Pq[:, pi, :], smm[:, pi, :], False, ta)
                    yield 1.5
                pend[h].append(normalise(*last))

            def apply(h):
                (gk, pp, tok), = gemm("w_gm", h, 8, H, [(0, L)])
                yield 5.5
                t_pt = []
                for kb in range(2):
                    tk, b, free = Tr.take()
                    for n in range(4):
                        t = pe(lambda e: e.transpose(ps[:, b, n * 128:(n + 1) * 128], Pq[:, (h % 2) * 4 + n, kb * 128:(kb + 1) * 128], ident), free, pend[h][n])
                    t2 = act(lambda e: e.copy(PTm[:, kb, :], bank(b)), t, ptb[0])
                    Tr.give(tk, t2)
                    t_pt.append(t2)
                    yield 1.0
                busy_P[h % 2] = [t]
                ok, ob, free = Or.take()
                pe.wait(free, t_pt)
                for kb in range(2):
                    t = pe(lambda e: e.matmul(bank(ob), mv[:, kb, h * 128:(h + 1) * 128], PTm[:, kb, :], start=(kb == 0), stop=(kb == 1)))
                ptb[0] = t
                t1 = silu_gate(pp, tok, gk, bank(ob), ym[:, h, :], t)
                Or.give(ok, t1)
                t_ym[h] = t1
                yield 2.0

            yield from scores(0)
            for h in range(4):
                yield from alternate(scores(h + 1) if h < 3 else iter(()), apply(h))

        t_gs = {}
        sg5 = at("sg5", [P, 6, L], 177)

        def glu():
            for m in range(6):
                (gk, pp, tok), = gemm("w_gs", m, 8, H, [(0, L)])
                i_, q, sfree = sqr.take()
                ta = act(lambda e: e.activation(q, pp, ACT.Tanh, scale=0.5), tok, sfree)
                t = dve(lambda e: e.scalar_tensor_tensor(out=sg5[:, m, :], in0=q, scalar=1.0, in1=pp, op0=ALU.add, op1=ALU.mult), ta)
                G.give(gk, t)
                sqr.give(i_, t)
                t_gs[m] = t
                yield 5.5

        d5 = Dma("s_s5")
        m_ = marks()
        d5.start(sp, wkf[:, 0:768], A["s5b"][0], m_, t_spill)
        d5.start(sp, wkf[:, 768:1536], A["s5b"][1])
        d5.start(sp, cl[:, 0, :, :].rearrange("p a b -> p (a b)"), A["s5c"][0])
        t_d5[0] = d5.start(sp, cl[:, 1, :, :].rearrange("p a b -> p (a b)"), A["s5c"][1])
        s5_numbers()
        W.sub = dve
        run(u_gemms())
        weave(totals, "s5", s5_scan(), chain_of(fq_gemms(), forget(), tokmajor("w_fv", 3, H, 4, lambda c: vf[:, c, :], t_fv), fox(),
                                  memory()))
        G = banks(0, 1, 2, 3, 4, 5, 6, 7)
        run(glu())
        fence()
        G = banks(0, 1, 2, 3, 4, 5, 6, 7)
        W.sub = pool
        YS, _, _ = pair("ysp2", 6, L, 122)
        t_s = [YS.put(k, ysv[:, k, :], 0, L, lo=(dve if k % 2 else pool)) for k in range(6)]
        t5 = []
        Z5 = at("Z5", [P, 2, L], 218)
        z5r = Ring([0, 1])
        t_gl = []
        for m in range(6):
            (gk, pp, tok), = gemm("w_glu", m, 6, YS, [(0, L)], tiles=(t_s if m == 0 else None))
            zk, zi, zfree = z5r.take()
            ta = act(lambda e: e.activation(Z5[:, zi, :], pp, ACT.Tanh, scale=0.25, bias=V("bglu", m)), tok, zfree)
            G.give(gk, ta)
            t = dve(lambda e: e.scalar_tensor_tensor(out=sg5[:, m, :], in0=Z5[:, zi, :], scalar=1.0, in1=sg5[:, m, :], op0=ALU.add, op1=ALU.mult), ta)
            z5r.give(zk, t)
            t = dve(lambda e: e.tensor_tensor(ysv[:, m, :], ysv[:, m, :], sg5[:, m, :], ALU.mult), t)
            t_gl.append(t)
        last_glu = tok

        YF, _, _ = pair("yf2", 6, L, 146, 189)
        YM, _, _ = pair("ym2", 4, L, 158)
        gt2 = at("gt2", [P, 6, L], 177)
        X2 = at("X2", [P, 8, L], 202)
        MP2, _, _ = pair("mp2", 8, L, 90)
        gr = Ring(list(range(6)))
        t_f = [YF.put(k, yf[:, k, :], 0, L, lo=(dve if k % 2 else pool)) for k in range(6)]
        fm = [t_gl, last_glu]
        t_s = [YS.put(k, ysv[:, k, :], 0, L, t_gl, last_glu, lo=(dve if k % 2 else pool)) for k in range(6)]
        t_mm = [YM.put(k, ym[:, k, :], 0, L, t_gl, t_s, lo=(dve if k % 2 else pool)) for k in range(4)]
        ready = {0: t_f, 1: t_s, 2: t_mm}
        t_x = Dma("s_x2").start(sp, X2[:, :, :], A["xsc"], t_gl)
        for i in range(6):
            gr.give(i, t_gl)
        t_m = []
        for m in range(8):
            tt = []
            for q, (wd, KT, src) in enumerate((("w_pf", 6, YF), ("w_ps", 6, YS), ("w_pm", 4, YM))):
                (gk, pp, tok), = gemm("w_gl", q * 8 + m, 8, H, [(0, L)])
                ik, i_, free = gr.take()
                ta = act(lambda e: e.activation(gt2[:, i_, :], pp, ACT.Tanh, scale=0.5, bias=V("bmerge", q * 8 + m)), tok, free)
                G.give(gk, ta)
                (gk, pp, tok), = gemm(wd, m, KT, src, [(0, L)], tiles=(ready[q] if m == 0 else None))
                t = dve(lambda e: e.scalar_tensor_tensor(out=gt2[:, i_, :], in0=gt2[:, i_, :], scalar=1.0, in1=pp, op0=ALU.add, op1=ALU.mult), tok, ta)
                G.give(gk, t)
                tt.append((ik, i_, t))
            a, b_, c_ = (x[1] for x in tt)
            t = dve(lambda e: e.tensor_tensor(gt2[:, a, :], gt2[:, a, :], gt2[:, c_, :], ALU.add), tt[0][2], tt[2][2])
            i_, s, free = sqr.take()
            t = dve(lambda e: e.scalar_tensor_tensor(out=s, in0=gt2[:, b_, :], scalar=0.25, in1=gt2[:, a, :], op0=ALU.mult, op1=ALU.add), t, tt[1][2], free)
            for ik, _, _ in tt:
                gr.give(ik, t)
            tt = MP2.put(m, s, 0, L, t, ready[0], ready[1], ready[2])
            sqr.give(i_, tt)
            t_m.append(tt)
        for m in range(8):
            (gk, pp, tok), = gemm("w_out2", m, 8, MP2, [(0, L)], tiles=(t_m if m == 0 else None))
            t = dve(lambda e: e.scalar_tensor_tensor(out=X2[:, m, :], in0=pp, scalar=0.25, in1=X2[:, m, :], op0=ALU.mult, op1=ALU.add), tok, t_x)
            G.give(gk, t)
            t_n = norm_add(m, X2[:, m, :], L, acc, sqr, t)
        t_r = rstd_of(8, L, t_n)
        dout = Dma("s_out")
        for k in range(8):
            t = dve(lambda e: e.scalar_tensor_tensor(out=X2[:, k, :], in0=X2[:, k, :], scalar=V("gf", k), in1=rstd[:, 0:L], op0=ALU.mult, op1=ALU.mult), t_r)
            t_out = dout.start(sp, out[:, k, :], X2[:, k, :], t)
        sp.wait(t_out)
        return W.asked


def kernel(**inputs):
    import numpy as _np
    import concourse.bacc as _bacc
    from concourse import mybir as _mybir
    from concourse.bass_utils import run_bass_kernel_spmd as _run

    I = {k: _np.asarray(v) for k, v in inputs.items()}
    arr = {}

    def blocks(w):
        k, n = w.shape
        return _np.ascontiguousarray(w.reshape(k // 128, 128, n // 128, 128).transpose(2, 1, 0, 3).reshape(n // 128, 128, k))

    def wide(w):
        k, n = w.shape
        return _np.ascontiguousarray(w.reshape(2, 4, 128, n // 256, 256).transpose(3, 0, 2, 1, 4).reshape(n // 256, 2, 128, 1024))

    def feat(x):
        t, n = x.shape
        return _np.ascontiguousarray(x.T.reshape(n // 128, 128, t).transpose(1, 0, 2))

    def cols(v):
        return v.reshape(-1, 128).T

    arr["xT"] = feat(I["x"][0])
    arr["ctxT"] = feat(I["ctx"][0])
    arr["memT"] = feat(I["mem_2"][0])
    arr["w_mod"] = blocks(I["w_mod"][0])
    w = I["w_in"][0]
    arr["w_z"] = blocks(w[:, 0:2048])
    arr["w_xbc"] = blocks(w[:, 2048:5120])
    arr["w_dt"] = _np.ascontiguousarray(w[:, 5120:5184].reshape(8, 128, 64).transpose(1, 0, 2).reshape(128, 512))
    arr["w_qk"] = blocks(w[:, 5184:6464])
    arr["w_v"] = wide(w[:, 6464:6720])
    arr["w_g"] = blocks(w[:, 6720:8768])
    arr["w_os"] = blocks(I["w_o_ssd"][0])
    arr["w_oa"] = blocks(I["w_o_att"][0])
    arr["w_out"] = blocks(I["w_out"][0])
    arr["w_up"] = blocks(I["w_up"][0])
    arr["w_down"] = blocks(I["w_down"][0])
    w = I["w_in_2"][0]
    arr["w_fqk"] = blocks(w[:, 0:1536])
    arr["w_fv"] = wide(w[:, 1536:2304])
    arr["w_fl"] = _np.ascontiguousarray(w[:, 2304:2316].reshape(8, 128, 12).transpose(1, 0, 2).reshape(128, 96))
    arr["w_gf"] = blocks(w[:, 2316:3084])
    arr["w_u"] = blocks(w[:, 3084:3852])
    arr["w_gs"] = blocks(w[:, 3852:4620])
    arr["w_qm"] = blocks(w[:, 4620:5132])
    arr["w_gm"] = blocks(w[:, 5132:5644])
    arr["w_gl"] = blocks(w[:, 5644:8716])
    w = I["w_mem_kv_2"][0]
    arr["w_mk"] = blocks(w[:, 0:512])
    arr["w_mv"] = wide(w[:, 512:1024])
    arr["w_glu"] = blocks(I["w_glu_2"][0])
    arr["w_pf"] = blocks(I["w_proj_fox_2"][0])
    arr["w_ps"] = blocks(I["w_proj_s5_2"][0])
    arr["w_pm"] = blocks(I["w_proj_mem_2"][0])
    arr["w_out2"] = blocks(I["w_out_2"][0])
    cw, fw = I["ssd_conv_w"][0], I["ffn_conv_w"][0]
    cc = _np.stack([I["c"][0], I["c_ctx"]], axis=-1)
    vec = {
        "bmod": cols(I["b_mod"][0]), "g1": cols(I["norm1_g"][0]), "g2": cols(I["norm2_g"][0]),
        "cw0": cols(cw[0]), "cw1": cols(cw[1]), "cw2": cols(cw[2]), "cb": cols(I["ssd_conv_b"][0]),
        "sg": cols(I["ssd_norm_g"][0]), "fw0": cols(fw[0]), "fw1": cols(fw[1]), "fw2": cols(fw[2]),
        "fb": cols(I["ffn_conv_b"][0]), "fg": cols(I["final_g"]), "gn": cols(I["g_norm_2"][0]),
        "gm": cols(I["g_mem_norm_2"][0]), "gf": cols(I["g_final_2"]), "bmerge": cols(I["b_merge_2"][0]),
        "bglu": cols(I["b_glu_2"][0]), "s5d": cols(I["s5_d_2"][0]), "lre": cols(I["lam_re_2"][0]),
        "lim": cols(I["lam_im_2"][0]), "lstep": cols(_np.repeat(I["log_step_2"][0], 64)),
        "dsk": cols(_np.repeat(I["ssd_d"][0], 64)),
        "bfc": cols(_np.pad(I["b_forget_2"][0], (0, 116))),
        "c": cc.reshape(8, 128, 2).transpose(1, 0, 2).reshape(128, 16),
    }
    arr["vecs"] = _np.ascontiguousarray(_np.concatenate([vec[n] for n, _ in VECS], axis=1))
    r = _np.concatenate([I["ssd_dt_bias"][0].reshape(-1), I["ssd_a_log"][0].reshape(-1), I["att_sink"][0], I["b_forget_2"][0]])
    arr["rows"] = _np.ascontiguousarray(_np.broadcast_to(r, (128, r.size)))
    sb_ = _np.zeros((2, 2, 64, 24, 2, 16), _np.float32)
    sc_ = _np.zeros((2, 2, 64, 24, 2, 16), _np.float32)
    for q, (bn, cn) in enumerate((("s5_b_re_2", "s5_c_re_2"), ("s5_b_im_2", "s5_c_im_2"))):
        b4 = I[bn][0].reshape(24, 2, 64, 16)
        c4 = I[cn][0].reshape(24, 2, 16, 64)
        for par in (0, 1):
            sb_[q, par, :, :, par, :] = b4[:, par].transpose(1, 0, 2)
            sc_[q, par, :, :, par, :] = c4[:, par].transpose(2, 0, 1)
    arr["s5b"] = sb_.reshape(2, 128, 768)
    arr["s5c"] = sc_.reshape(2, 128, 768)
    i = _np.arange(128)
    a, b = i[:, None], i[None, :]
    f = _np.float32
    inv = (f(10000.0) ** (-_np.arange(0, 32, 2, dtype=f) / f(32))).astype(f)
    t = _np.arange(512)
    dd = i % 64
    pos = _np.where((dd // 32 == 0)[:, None], (t // 64)[None], (t % 64)[None]).astype(f)
    ang = (pos * inv[dd % 16][:, None]).astype(f).astype(_np.float64)
    sgn = _np.where(dd % 32 < 16, -1.0, 1.0)[:, None]
    arr["consts"] = _np.concatenate([
        a == b, a <= b, a >= b, a == (b ^ 16), _np.where(b >= a, 0.0, -1e30), _np.where(b <= a, 0.0, -1e30),
        _np.ones((128, 128)), _np.cos(ang), sgn * _np.sin(ang)], axis=1).astype(f)

    def build(order, totals):
        nc = _bacc.Bacc("TRN2", target_bir_lowering=False, num_devices=1, dynamic_dma_scratch_size=256)
        A = {}
        for name, x in arr.items():
            A[name] = nc.dram_tensor(f"in_{name}", x.shape, _mybir.dt.float32, kind="ExternalInput").ap()
        for name, shape in (("csd", (2, 32, 512)), ("xsc", (128, 8, 512)), ("ysc", (128, 16, 512))):
            A[name] = nc.dram_tensor(name, shape, _mybir.dt.float32, kind="Internal").ap()
        out = nc.dram_tensor("out_0", (128, 8, 512), _mybir.dt.float32, kind="ExternalOutput").ap()
        return nc, fused_blocks(nc, A, out, order, totals)

    totals = {}
    build([], totals)
    _, order = build([], totals)
    nc, _ = build(order, totals)
    r = _run(nc, [{f"in_{k}": v for k, v in arr.items()}], core_ids=[0])
    y = r.results[0]["out_0"]
    return _np.ascontiguousarray(y.transpose(2, 1, 0).reshape(1, 512, 1024))
```
